# Optimizing a Trainium2 kernel written in Bass

```python
import jax, jax.numpy as jnp
from jax import lax
import numpy as np
import math
import jax
import jax.numpy as jnp

D_MODEL = 1024
BATCH = 1
SEQ = 256
DEPTH = 2

GRID_W = 64
CTX_LEN = 256
N_MIXERS = 2
N_HEADS = 16
N_KV_HEADS = 4
HEAD_DIM = 64
GROUP = N_HEADS // N_KV_HEADS
Q_WIDTH = N_HEADS * HEAD_DIM
KV_WIDTH = N_KV_HEADS * HEAD_DIM
WINDOW = 128
BLOCK = 128
SPAN = BLOCK + 2 * WINDOW
ROPE_BASE = 10000.0
AXIS_DIM = HEAD_DIM // 2
FOURIER_GROUPS = 4
FOURIER_GROUP_CH = D_MODEL // FOURIER_GROUPS
D_FF = 2816
N_MOD = 9
LN_EPS = 1e-5
ALPHA = (2.0 * DEPTH) ** 0.25
BETA = (8.0 * DEPTH) ** -0.25
NEG_INF = -1e30
N_ATTN_LAYERS = (DEPTH + N_MIXERS - 1) // N_MIXERS
N_FOURIER_LAYERS = (DEPTH + N_MIXERS - 2) // N_MIXERS


def layer_norm(x, g, b):
    xf = x.astype(jnp.float32)
    mu = xf.mean(-1, keepdims=True)
    var = jnp.square(xf - mu).mean(-1, keepdims=True)
    return ((xf - mu) * lax.rsqrt(var + LN_EPS) * g + b).astype(x.dtype)

def modulate(x, mod, j):
    shift, scale = mod[:, 3 * j], mod[:, 3 * j + 1]
    return x * (1 + scale[:, None, :]) + shift[:, None, :]

def post_norm_update(x, y, mod, j, g, b):
    gate = mod[:, 3 * j + 2][:, None, :]
    return layer_norm(ALPHA * x + gate * y, g, b)

def swiglu(h, wi, wo):
    a, g = jnp.split(h @ wi, 2, axis=-1)
    return (a * jax.nn.silu(g)) @ wo

def half_ffn_sublayer(x, mod, j, wi, wo, g, b):
    y = 0.5 * swiglu(modulate(x, mod, j), wi, wo)
    return post_norm_update(x, y, mod, j, g, b)

def axial_rope_tables(n_tokens):
    rows = n_tokens // GRID_W
    row = jnp.repeat(jnp.arange(rows), GRID_W).astype(jnp.float32)
    col = jnp.tile(jnp.arange(GRID_W), rows).astype(jnp.float32)
    inv = ROPE_BASE ** (-jnp.arange(0, AXIS_DIM, 2, dtype=jnp.float32) / AXIS_DIM)
    ang = jnp.concatenate([row[:, None] * inv, col[:, None] * inv], axis=-1)
    return jnp.cos(ang), jnp.sin(ang)

def apply_axial_rope(x, cos, sin):
    B_, L_, H_, Dh = x.shape
    half = AXIS_DIM // 2
    xr = x.astype(jnp.float32).reshape(B_, L_, H_, 2, 2, half)
    x1, x2 = xr[..., 0, :], xr[..., 1, :]
    c = cos.reshape(L_, 1, 2, half)
    s = sin.reshape(L_, 1, 2, half)
    out = jnp.stack([x1 * c - x2 * s, x1 * s + x2 * c], axis=-2)
    return out.reshape(B_, L_, H_, Dh).astype(x.dtype)

def window_sink_attention(h, hc, w_qkv, b_qkv, w_o, sink, cos, sin, ctx_queries):
    B_, S_, _ = h.shape
    C_ = hc.shape[1]
    n_blocks = S_ // BLOCK
    scale = HEAD_DIM ** -0.5
    q, k, v = jnp.split(h @ w_qkv + b_qkv, [Q_WIDTH, Q_WIDTH + KV_WIDTH], axis=-1)
    q = apply_axial_rope(q.reshape(B_, S_, N_HEADS, HEAD_DIM) * scale, cos, sin)
    q = q.reshape(B_, S_, N_KV_HEADS, GROUP, HEAD_DIM)
    k = apply_axial_rope(k.reshape(B_, S_, N_KV_HEADS, HEAD_DIM), cos, sin)
    v = v.reshape(B_, S_, N_KV_HEADS, HEAD_DIM)
    kvc = hc @ w_qkv[:, Q_WIDTH:] + b_qkv[Q_WIDTH:]
    kc, vc = jnp.split(kvc, [KV_WIDTH], axis=-1)
    kc = kc.reshape(B_, C_, N_KV_HEADS, HEAD_DIM)
    vc = vc.reshape(B_, C_, N_KV_HEADS, HEAD_DIM)

    pad = ((0, 0), (WINDOW, WINDOW), (0, 0), (0, 0))
    k_pad = jnp.pad(k, pad)
    v_pad = jnp.pad(v, pad)
    sink_logit = sink.astype(jnp.float32).reshape(1, N_KV_HEADS, GROUP, 1, 1)
    rel = jnp.arange(BLOCK)[:, None] - jnp.arange(SPAN)[None, :] + WINDOW
    band = jnp.abs(rel) <= WINDOW

    def block(bi):
        start = bi * BLOCK
        q_b = lax.dynamic_slice_in_dim(q, start, BLOCK, axis=1)
        k_b = lax.dynamic_slice_in_dim(k_pad, start, SPAN, axis=1)
        v_b = lax.dynamic_slice_in_dim(v_pad, start, SPAN, axis=1)
        key_pos = start - WINDOW + jnp.arange(SPAN)
        valid = band & ((key_pos >= 0) & (key_pos < S_))[None, :]
        s_win = jnp.einsum('bqhgd,bkhd->bhgqk', q_b, k_b, preferred_element_type=jnp.float32)
        s_win = jnp.where(valid, s_win, NEG_INF)
        s_ctx = jnp.einsum('bqhgd,bkhd->bhgqk', q_b, kc, preferred_element_type=jnp.float32)
        sinks = jnp.broadcast_to(sink_logit, s_ctx.shape[:-1] + (1,))
        p = jax.nn.softmax(jnp.concatenate([s_win, s_ctx, sinks], axis=-1), axis=-1).astype(v.dtype)
        o = (jnp.einsum('bhgqk,bkhd->bqhgd', p[..., :SPAN], v_b)
             + jnp.einsum('bhgqk,bkhd->bqhgd', p[..., SPAN:SPAN + C_], vc))
        return o

    o = lax.map(block, jnp.arange(n_blocks))
    o = jnp.moveaxis(o, 0, 1).reshape(B_, S_, Q_WIDTH)
    y = o @ w_o
    if not ctx_queries:
        return y, None
    qc = (hc @ w_qkv[:, :Q_WIDTH] + b_qkv[:Q_WIDTH]) * scale
    qc = qc.reshape(B_, C_, N_KV_HEADS, GROUP, HEAD_DIM)
    sc = jnp.einsum('bqhgd,bkhd->bhgqk', qc, kc, preferred_element_type=jnp.float32)
    sinks_c = jnp.broadcast_to(sink_logit, sc.shape[:-1] + (1,))
    pc = jax.nn.softmax(jnp.concatenate([sc, sinks_c], axis=-1), axis=-1).astype(vc.dtype)
    oc = jnp.einsum('bhgqk,bkhd->bqhgd', pc[..., :C_], vc).reshape(B_, C_, Q_WIDTH)
    return y, oc @ w_o

def fourier_mix(h, w_o):
    B_, L_, D_ = h.shape
    hg = h.astype(jnp.float32).reshape(B_, L_, FOURIER_GROUPS, FOURIER_GROUP_CH)
    f = jnp.fft.fft2(hg, axes=(1, 3), norm="ortho").real
    return f.reshape(B_, L_, D_).astype(h.dtype) @ w_o

def first_inputs(seed: int = 0) -> dict:
    key = jax.random.key(seed)
    ks = jax.random.split(key, 16)

    def nrm(k, shape, s):
        return jax.random.normal(k, shape, jnp.float32) * s

    qkv_w = Q_WIDTH + 2 * KV_WIDTH
    return {
        "x": nrm(ks[0], (BATCH, SEQ, D_MODEL), 1.0),
        "c": nrm(ks[1], (BATCH, D_MODEL), 1.0),
        "ctx": nrm(ks[2], (BATCH, CTX_LEN, D_MODEL), 1.0),
        "c_ctx": nrm(ks[3], (D_MODEL,), 1.0),
        "mod_w": nrm(ks[4], (DEPTH, D_MODEL, N_MOD * D_MODEL), D_MODEL ** -0.5),
        "mod_b": nrm(ks[5], (DEPTH, N_MOD * D_MODEL), 0.02),
        "ln_g": 1.0 + nrm(ks[6], (DEPTH, 3, D_MODEL), 0.02),
        "ln_b": nrm(ks[7], (DEPTH, 3, D_MODEL), 0.02),
        "ffn_wi": nrm(ks[8], (DEPTH, 2, D_MODEL, 2 * D_FF), D_MODEL ** -0.5),
        "ffn_wo": nrm(ks[9], (DEPTH, 2, D_FF, D_MODEL), BETA * D_FF ** -0.5),
        "attn_wqkv": nrm(ks[10], (N_ATTN_LAYERS, D_MODEL, qkv_w), D_MODEL ** -0.5),
        "attn_bqkv": nrm(ks[11], (N_ATTN_LAYERS, qkv_w), 0.02),
        "attn_wo": nrm(ks[12], (N_ATTN_LAYERS, Q_WIDTH, D_MODEL), BETA * Q_WIDTH ** -0.5),
        "attn_sink": nrm(ks[13], (N_ATTN_LAYERS, N_HEADS), 1.0),
        "fourier_wo": nrm(ks[14], (N_FOURIER_LAYERS, D_MODEL, D_MODEL), BETA * D_MODEL ** -0.5),
    }

def first_block(x, c, ctx, c_ctx, mod_w, mod_b, ln_g, ln_b, ffn_wi, ffn_wo,
              attn_wqkv, attn_bqkv, attn_wo, attn_sink, fourier_wo):
    cos, sin = axial_rope_tables(x.shape[1])
    silu_c = jax.nn.silu(c)
    silu_cc = jax.nn.silu(c_ctx)
    ctx_s = ctx
    for i in range(DEPTH):
        kind = i % N_MIXERS
        ctx_out_live = any(j % N_MIXERS == 0 for j in range(i + 1, DEPTH))
        ctx_in_live = (kind == 0) or ctx_out_live
        g, b = ln_g[i], ln_b[i]
        mod_lat = (silu_c @ mod_w[i] + mod_b[i]).reshape(-1, N_MOD, D_MODEL)
        x = half_ffn_sublayer(x, mod_lat, 0, ffn_wi[i, 0], ffn_wo[i, 0], g[0], b[0])
        if ctx_in_live:
            mod_ctx = (silu_cc @ mod_w[i] + mod_b[i]).reshape(1, N_MOD, D_MODEL)
            ctx_s = half_ffn_sublayer(ctx_s, mod_ctx, 0, ffn_wi[i, 0], ffn_wo[i, 0], g[0], b[0])
        h = modulate(x, mod_lat, 1)
        if kind == 0:
            a = i // N_MIXERS
            y, yc = window_sink_attention(h, modulate(ctx_s, mod_ctx, 1), attn_wqkv[a], attn_bqkv[a],
                                          attn_wo[a], attn_sink[a], cos, sin, ctx_out_live)
        else:
            f = i // N_MIXERS
            y = fourier_mix(h, fourier_wo[f])
            yc = fourier_mix(modulate(ctx_s, mod_ctx, 1), fourier_wo[f]) if ctx_out_live else None
        x = post_norm_update(x, y, mod_lat, 1, g[1], b[1])
        x = half_ffn_sublayer(x, mod_lat, 2, ffn_wi[i, 1], ffn_wo[i, 1], g[2], b[2])
        if ctx_out_live:
            ctx_s = post_norm_update(ctx_s, yc, mod_ctx, 1, g[1], b[1])
            ctx_s = half_ffn_sublayer(ctx_s, mod_ctx, 2, ffn_wi[i, 1], ffn_wo[i, 1], g[2], b[2])
    return x


CHUNK = GRID_W
N_EVEN = (DEPTH + 1) // 2
N_ODD = DEPTH // 2
EPS = 1e-6

GDN_HEADS = 4
GDN_DK = 128
GDN_DV = 128
GDN_QK = GDN_HEADS * GDN_DK
GDN_V = GDN_HEADS * GDN_DV
SHORT_CONV = 3

GLA_HEADS = 4
GLA_DK = 64
GLA_DV = 128
GLA_QK = GLA_HEADS * GLA_DK
GLA_V = GLA_HEADS * GLA_DV
GLA_GATE_RANK = 16
GLA_GATE_TAU = 16.0

AB_SIZES = (GDN_QK, GDN_QK, GDN_V, GDN_V, 2 * GDN_HEADS, 2 * GDN_HEADS, GLA_QK, GLA_QK, GLA_V, GLA_V, 2 * GLA_GATE_RANK)
AB_SPLITS = tuple(sum(AB_SIZES[: i + 1]) for i in range(len(AB_SIZES) - 1))
AB_WIDTH = sum(AB_SIZES)
MIX_WIDTH = GDN_V + GLA_V

HY_ORDER = 2
HY_SHORT = 3
HY_EMB = 33
HY_BANDS = (HY_EMB - 1) // 2
HY_HIDDEN = 64
HY_MIN_DECAY = math.log(1e-2) / 1.5
HY_MAX_DECAY = math.log(1e-2) / 0.3
HY_SHIFT = 0.05

D_FF_2 = -(-8 * D_MODEL // (3 * 256)) * 256


def rmsnorm(x, gain):
    xf = x.astype(jnp.float32)
    y = xf * lax.rsqrt(jnp.mean(xf * xf, axis=-1, keepdims=True) + EPS)
    return (y * gain.astype(jnp.float32)).astype(x.dtype)

def modulate_2(x, gain, shift, scale):
    return rmsnorm(x, gain) * (1 + scale) + shift

def head_rmsnorm(o, gain):
    return o * lax.rsqrt(jnp.mean(o * o, axis=-1, keepdims=True) + EPS) * gain.astype(jnp.float32)

def l2norm(u):
    return u * lax.rsqrt(jnp.sum(u * u, axis=-1, keepdims=True) + EPS)

def short_conv(x, w):
    k, l = w.shape[0], x.shape[1]
    xp = jnp.pad(x, ((0, 0), (k // 2, k // 2), (0, 0)))
    return sum(xp[:, j:j + l] * w[j] for j in range(k))

def swiglu_2(u, w1, w3, w2):
    return (jax.nn.silu(u @ w1) * (u @ w3)) @ w2

def to_chunks(t):
    b, l, hh = t.shape[:3]
    rows = l // GRID_W
    t = t.reshape((b, rows, CHUNK, hh) + t.shape[3:])
    return jnp.moveaxis(t, 3, 1)

def from_chunks(t):
    b, hh, n, cl, d = t.shape
    return jnp.moveaxis(t, 1, 3).reshape(b, n * cl, hh, d)

def run_gdn(q, k, v, g, beta, s0, emit):
    q, k, v, g, beta = map(to_chunks, (q, k, v, g, beta))
    dv = v.shape[-1]
    lower = jnp.tril(jnp.ones((CHUNK, CHUNK), dtype=bool))
    strict = jnp.tril(jnp.ones((CHUNK, CHUNK), dtype=bool), -1)
    gc = jnp.cumsum(g, axis=-1)
    decay = jnp.exp(jnp.where(lower, gc[..., :, None] - gc[..., None, :], -jnp.inf))
    kb = k * beta[..., None]
    lmat = jnp.where(strict, jnp.einsum('bhncd,bhnsd->bhncs', kb, k) * decay, 0.0) + jnp.eye(CHUNK, dtype=k.dtype)
    rhs = jnp.concatenate([v * beta[..., None], kb * jnp.exp(gc)[..., None]], axis=-1)
    sol = lax.linalg.triangular_solve(lmat, rhs, left_side=True, lower=True, unit_diagonal=True)
    u0, kcd = sol[..., :dv], sol[..., dv:]
    kd = k * jnp.exp(gc[..., -1:] - gc)[..., None]
    gl = jnp.exp(gc[..., -1])
    xs = (u0, kcd, kd, gl)
    if emit:
        attn = jnp.einsum('bhncd,bhnsd->bhncs', q, k) * decay
        xs = xs + (attn, q * jnp.exp(gc)[..., None])
    xs = tuple(jnp.moveaxis(t, 2, 0) for t in xs)

    def step(s, inp):
        u0_i, kcd_i, kd_i, gl_i = inp[:4]
        u = u0_i - jnp.einsum('bhcd,bhde->bhce', kcd_i, s)
        s_new = s * gl_i[..., None, None] + jnp.einsum('bhcd,bhce->bhde', kd_i, u)
        if not emit:
            return s_new, None
        attn_i, qd_i = inp[4:]
        o = jnp.einsum('bhcd,bhde->bhce', qd_i, s) + jnp.einsum('bhcs,bhse->bhce', attn_i, u)
        return s_new, o

    s_fin, out = lax.scan(step, s0, xs)
    out = from_chunks(jnp.moveaxis(out, 0, 2)) if emit else None
    return out, s_fin

def run_gla(q, k, v, log_a, s0, emit):
    q, k, v, log_a = map(to_chunks, (q, k, v, log_a))
    bc = jnp.cumsum(log_a, axis=-2)
    kd = k * jnp.exp(bc[..., -1:, :] - bc)
    gl = jnp.exp(bc[..., -1, :])
    xs = (kd, v, gl)
    if emit:
        lower = jnp.tril(jnp.ones((CHUNK, CHUNK), dtype=bool))
        ref = bc[..., CHUNK // 2:CHUNK // 2 + 1, :]
        attn = jnp.einsum('bhncd,bhnsd->bhncs', q * jnp.exp(bc - ref), k * jnp.exp(ref - bc))
        attn = jnp.where(lower, attn, 0.0)
        intra = jnp.einsum('bhncs,bhnse->bhnce', attn, v)
        xs = xs + (q * jnp.exp(bc),)
    xs = tuple(jnp.moveaxis(t, 2, 0) for t in xs)

    def step(s, inp):
        kd_i, v_i, gl_i = inp[:3]
        s_new = s * gl_i[..., :, None] + jnp.einsum('bhcd,bhce->bhde', kd_i, v_i)
        if not emit:
            return s_new, None
        o = jnp.einsum('bhcd,bhde->bhce', inp[3], s)
        return s_new, o

    s_fin, inter = lax.scan(step, s0, xs)
    out = from_chunks(jnp.moveaxis(inter, 0, 2) + intra) if emit else None
    return out, s_fin

def orient(t, d):
    return t if d == 0 else jnp.flip(t, axis=1)

def bidirectional(run, ctx_dirs, lat_dirs, s0, ctx_out):
    lat_outs, ctx_outs = [], []
    for d in range(2):
        oc, s_ctx = run(*[orient(t, d) for t in ctx_dirs[d]], s0, ctx_out)
        ol, _ = run(*[orient(t, d) for t in lat_dirs[d]], s_ctx, True)
        lat_outs.append(orient(ol, d))
        if ctx_out:
            ctx_outs.append(orient(oc, d))
    return lat_outs[0] + lat_outs[1], (ctx_outs[0] + ctx_outs[1] if ctx_out else None)

def ab_prepare(t, w_in, conv_w, a_log, dt_bias, gla_gate_w, gla_gate_b):
    b, l, _ = t.shape
    f32 = jnp.float32
    gq, gk, gv, gz, ga, gb, lq, lk, lv, lg, llr = jnp.split(t @ w_in, AB_SPLITS, axis=-1)
    qkv = jax.nn.silu(short_conv(jnp.concatenate([gq, gk, gv], axis=-1), conv_w)).astype(f32)
    gq, gk, gv = jnp.split(qkv, (GDN_QK, 2 * GDN_QK), axis=-1)

    def heads(u, h, d):
        return u.astype(f32).reshape(b, l, h, d)

    gate = jnp.einsum('bldr,drk->bldk', heads(llr, 2, GLA_GATE_RANK), gla_gate_w.astype(f32)) + gla_gate_b.astype(f32)
    return dict(
        gdn_q=l2norm(heads(gq, GDN_HEADS, GDN_DK)) * GDN_DK ** -0.5,
        gdn_k=l2norm(heads(gk, GDN_HEADS, GDN_DK)),
        gdn_v=heads(gv, GDN_HEADS, GDN_DV),
        gdn_g=-jnp.exp(a_log.astype(f32)) * jax.nn.softplus(heads(ga, 2, GDN_HEADS) + dt_bias.astype(f32)),
        gdn_beta=jax.nn.sigmoid(heads(gb, 2, GDN_HEADS)),
        gdn_z=heads(gz, GDN_HEADS, GDN_DV),
        gla_q=heads(lq, GLA_HEADS, GLA_DK) * GLA_DK ** -0.5,
        gla_k=heads(lk, GLA_HEADS, GLA_DK),
        gla_v=heads(lv, GLA_HEADS, GLA_DV),
        gla_log_a=(jax.nn.log_sigmoid(gate) / GLA_GATE_TAU).reshape(b, l, 2, GLA_HEADS, GLA_DK),
        gla_g=heads(lg, GLA_HEADS, GLA_DV),
    )

def ab_mixer(a, ac, w_in, conv_w, a_log, dt_bias, gdn_norm_w, gla_gate_w, gla_gate_b, gla_norm_w, w_out, ctx_out):
    pl = ab_prepare(a, w_in, conv_w, a_log, dt_bias, gla_gate_w, gla_gate_b)
    pc = ab_prepare(ac, w_in, conv_w, a_log, dt_bias, gla_gate_w, gla_gate_b)
    b = a.shape[0]
    s0_gdn = jnp.zeros((b, GDN_HEADS, GDN_DK, GDN_DV), jnp.float32)
    s0_gla = jnp.zeros((b, GLA_HEADS, GLA_DK, GLA_DV), jnp.float32)

    def gdn_dir(p, d):
        return (p['gdn_q'], p['gdn_k'], p['gdn_v'], p['gdn_g'][:, :, d], p['gdn_beta'][:, :, d])

    def gla_dir(p, d):
        return (p['gla_q'], p['gla_k'], p['gla_v'], p['gla_log_a'][:, :, d])

    o_gdn, oc_gdn = bidirectional(run_gdn, [gdn_dir(pc, d) for d in range(2)], [gdn_dir(pl, d) for d in range(2)], s0_gdn, ctx_out)
    o_gla, oc_gla = bidirectional(run_gla, [gla_dir(pc, d) for d in range(2)], [gla_dir(pl, d) for d in range(2)], s0_gla, ctx_out)

    def merge(og, ol, p, dtype):
        bb, l = og.shape[:2]
        y_gdn = (head_rmsnorm(og, gdn_norm_w) * jax.nn.silu(p['gdn_z'])).reshape(bb, l, GDN_V)
        y_gla = (head_rmsnorm(ol, gla_norm_w) * jax.nn.silu(p['gla_g'])).reshape(bb, l, GLA_V)
        return jnp.concatenate([y_gdn, y_gla], axis=-1).astype(dtype) @ w_out

    m = merge(o_gdn, o_gla, pl, a.dtype)
    mc = merge(oc_gdn, oc_gla, pc, ac.dtype) if ctx_out else None
    return m, mc

def hyena_filters(l, w1, b1, w2, b2, w3, b3, freq, filt_out):
    f32 = jnp.float32
    t = jnp.linspace(0.0, 1.0, l, dtype=f32)[:, None]
    w = (2.0 * math.pi / l) * jnp.arange(l, dtype=f32)[:, None]
    f = jnp.linspace(1e-4, HY_BANDS - 1, HY_BANDS, dtype=f32)[None, :]
    z = jnp.concatenate([t, jnp.cos(f * w), -jnp.sin(f * w)], axis=-1)
    fr = freq.astype(f32)
    hdn = jnp.sin(fr * (z @ w1.astype(f32) + b1.astype(f32)))
    hdn = jnp.sin(fr * (hdn @ w2.astype(f32) + b2.astype(f32)))
    hdn = jnp.sin(fr * (hdn @ w3.astype(f32) + b3.astype(f32)))
    h = (hdn @ filt_out.astype(f32)).reshape(l, 2, HY_ORDER, D_MODEL)
    deltas = jnp.abs(jnp.linspace(HY_MIN_DECAY, HY_MAX_DECAY, D_MODEL, dtype=f32))
    window = jnp.exp(-t.reshape(l, 1, 1, 1) * deltas) + HY_SHIFT
    return h * window

def long_conv(z, h_fwd, h_bwd, skip):
    l = z.shape[1]
    k = jnp.concatenate([h_fwd, jnp.zeros_like(h_fwd[:1]), jnp.flip(h_bwd[1:], axis=0)], axis=0)
    y = jnp.fft.irfft(jnp.fft.rfft(z, n=2 * l, axis=1) * jnp.fft.rfft(k, axis=0)[None], n=2 * l, axis=1)[:, :l]
    return y + z * skip.astype(jnp.float32)

def hyena_mixer(a, w_in, conv_w, w1, b1, w2, b2, w3, b3, freq, filt_out, skip, w_out):
    l = a.shape[1]
    u = short_conv(a @ w_in, conv_w).astype(jnp.float32)
    v, x1, x2 = jnp.split(u, 3, axis=-1)
    filt = hyena_filters(l, w1, b1, w2, b2, w3, b3, freq, filt_out)
    z = v
    for n, gate in enumerate((x1, x2)):
        z = gate * long_conv(z, filt[:, 0, n], filt[:, 1, n], skip[n])
    return z.astype(a.dtype) @ w_out

def second_inputs(seed: int = 0) -> dict:
    key = jax.random.key(seed)
    ks = iter(jax.random.split(key, 40))
    f32 = jnp.float32
    D = D_MODEL

    def nrm(shape, scale):
        return jax.random.normal(next(ks), shape, f32) * scale

    dt = jnp.exp(jax.random.uniform(next(ks), (N_EVEN, 2, GDN_HEADS), f32, math.log(1e-3), math.log(1e-1)))
    return {
        'x': nrm((BATCH, SEQ, D), 1.0),
        'c': nrm((BATCH, D), 1.0),
        'ctx': nrm((BATCH, CTX_LEN, D), 1.0),
        'c_ctx': nrm((D,), 1.0),
        'mod_w': nrm((DEPTH, D, 6 * D), 0.5 * D ** -0.5),
        'mod_b': nrm((DEPTH, 6 * D), 0.02),
        'norm1_w': 1.0 + nrm((DEPTH, D), 0.02),
        'norm2_w': 1.0 + nrm((DEPTH, D), 0.02),
        'ab_w_in': nrm((N_EVEN, D, AB_WIDTH), D ** -0.5),
        'ab_conv_w': nrm((N_EVEN, SHORT_CONV, 2 * GDN_QK + GDN_V), SHORT_CONV ** -0.5),
        'gdn_a_log': jnp.log(jax.random.uniform(next(ks), (N_EVEN, 2, GDN_HEADS), f32, 1.0, 16.0)),
        'gdn_dt_bias': dt + jnp.log(-jnp.expm1(-dt)),
        'gdn_norm_w': 1.0 + nrm((N_EVEN, GDN_DV), 0.02),
        'gla_gate_w': nrm((N_EVEN, 2, GLA_GATE_RANK, GLA_QK), GLA_GATE_RANK ** -0.5),
        'gla_gate_b': nrm((N_EVEN, 2, GLA_QK), 0.1),
        'gla_norm_w': 1.0 + nrm((N_EVEN, GLA_DV), 0.02),
        'ab_w_out': nrm((N_EVEN, MIX_WIDTH, D), MIX_WIDTH ** -0.5),
        'hy_w_in': nrm((N_ODD, D, 3 * D), D ** -0.5),
        'hy_conv_w': nrm((N_ODD, HY_SHORT, 3 * D), HY_SHORT ** -0.5),
        'hy_pos_w1': nrm((N_ODD, HY_EMB, HY_HIDDEN), HY_EMB ** -0.5),
        'hy_pos_b1': nrm((N_ODD, HY_HIDDEN), 0.1),
        'hy_pos_w2': nrm((N_ODD, HY_HIDDEN, HY_HIDDEN), HY_HIDDEN ** -0.5),
        'hy_pos_b2': nrm((N_ODD, HY_HIDDEN), 0.1),
        'hy_pos_w3': nrm((N_ODD, HY_HIDDEN, HY_HIDDEN), HY_HIDDEN ** -0.5),
        'hy_pos_b3': nrm((N_ODD, HY_HIDDEN), 0.1),
        'hy_freq': 1.0 + nrm((N_ODD, HY_HIDDEN), 0.02),
        'hy_filt_out': nrm((N_ODD, HY_HIDDEN, 2 * HY_ORDER * D), 0.03 * HY_HIDDEN ** -0.5),
        'hy_skip': nrm((N_ODD, HY_ORDER, D), 0.5),
        'hy_w_out': nrm((N_ODD, D, D), D ** -0.5),
        'ffn_w1': nrm((DEPTH, D, D_FF_2), D ** -0.5),
        'ffn_w3': nrm((DEPTH, D, D_FF_2), D ** -0.5),
        'ffn_w2': nrm((DEPTH, D_FF_2, D), D_FF_2 ** -0.5),
        'final_norm_w': 1.0 + nrm((D,), 0.02),
    }

def second_block(x, c, ctx, c_ctx, mod_w, mod_b, norm1_w, norm2_w, ab_w_in, ab_conv_w, gdn_a_log, gdn_dt_bias,
              gdn_norm_w, gla_gate_w, gla_gate_b, gla_norm_w, ab_w_out, hy_w_in, hy_conv_w, hy_pos_w1, hy_pos_b1,
              hy_pos_w2, hy_pos_b2, hy_pos_w3, hy_pos_b3, hy_freq, hy_filt_out, hy_skip, hy_w_out,
              ffn_w1, ffn_w3, ffn_w2, final_norm_w):
    silu_c = jax.nn.silu(c)
    silu_cc = jax.nn.silu(c_ctx)
    h, hc = x, ctx
    for i in range(DEPTH):
        even = i % 2 == 0
        ctx_carry = any(j % 2 == 0 for j in range(i + 1, DEPTH))
        ctx_read = even or ctx_carry
        sh1, sc1, g1, sh2, sc2, g2 = jnp.split((silu_c @ mod_w[i] + mod_b[i])[:, None, :], 6, axis=-1)
        a = modulate_2(h, norm1_w[i], sh1, sc1)
        if ctx_read:
            csh1, csc1, cg1, csh2, csc2, cg2 = jnp.split(silu_cc @ mod_w[i] + mod_b[i], 6, axis=-1)
            ac = modulate_2(hc, norm1_w[i], csh1, csc1)
        if even:
            e = i // 2
            m, mc = ab_mixer(a, ac, ab_w_in[e], ab_conv_w[e], gdn_a_log[e], gdn_dt_bias[e], gdn_norm_w[e],
                             gla_gate_w[e], gla_gate_b[e], gla_norm_w[e], ab_w_out[e], ctx_carry)
        else:
            o = i // 2
            hy = (hy_w_in[o], hy_conv_w[o], hy_pos_w1[o], hy_pos_b1[o], hy_pos_w2[o], hy_pos_b2[o],
                  hy_pos_w3[o], hy_pos_b3[o], hy_freq[o], hy_filt_out[o], hy_skip[o], hy_w_out[o])
            m = hyena_mixer(a, *hy)
            mc = hyena_mixer(ac, *hy) if ctx_carry else None
        h = h + g1 * m
        h = h + g2 * swiglu_2(modulate_2(h, norm2_w[i], sh2, sc2), ffn_w1[i], ffn_w3[i], ffn_w2[i])
        if ctx_carry:
            hc = hc + cg1 * mc
            hc = hc + cg2 * swiglu_2(modulate_2(hc, norm2_w[i], csh2, csc2), ffn_w1[i], ffn_w3[i], ffn_w2[i])
    return rmsnorm(h, final_norm_w)


def setup_inputs(seed=0):
    out = dict(first_inputs(seed))
    for name, value in second_inputs(seed + 1).items():
        if name != "x":
            out[name + "_2"] = value
    return out


def reference(
    x, c, ctx, c_ctx, mod_w, mod_b, ln_g, ln_b, ffn_wi, ffn_wo, attn_wqkv, attn_bqkv, attn_wo,
    attn_sink, fourier_wo, c_2, ctx_2, c_ctx_2, mod_w_2, mod_b_2, norm1_w_2, norm2_w_2,
    ab_w_in_2, ab_conv_w_2, gdn_a_log_2, gdn_dt_bias_2, gdn_norm_w_2, gla_gate_w_2,
    gla_gate_b_2, gla_norm_w_2, ab_w_out_2, hy_w_in_2, hy_conv_w_2, hy_pos_w1_2, hy_pos_b1_2,
    hy_pos_w2_2, hy_pos_b2_2, hy_pos_w3_2, hy_pos_b3_2, hy_freq_2, hy_filt_out_2, hy_skip_2,
    hy_w_out_2, ffn_w1_2, ffn_w3_2, ffn_w2_2, final_norm_w_2,
):
    x = first_block(
        x, c, ctx, c_ctx, mod_w, mod_b, ln_g, ln_b, ffn_wi, ffn_wo, attn_wqkv, attn_bqkv,
        attn_wo, attn_sink, fourier_wo,
    )
    return second_block(
        x, c_2, ctx_2, c_ctx_2, mod_w_2, mod_b_2, norm1_w_2, norm2_w_2, ab_w_in_2, ab_conv_w_2,
        gdn_a_log_2, gdn_dt_bias_2, gdn_norm_w_2, gla_gate_w_2, gla_gate_b_2, gla_norm_w_2,
        ab_w_out_2, hy_w_in_2, hy_conv_w_2, hy_pos_w1_2, hy_pos_b1_2, hy_pos_w2_2, hy_pos_b2_2,
        hy_pos_w3_2, hy_pos_b3_2, hy_freq_2, hy_filt_out_2, hy_skip_2, hy_w_out_2, ffn_w1_2,
        ffn_w3_2, ffn_w2_2, final_norm_w_2,
    )


_drawn_inputs = setup_inputs


def setup_inputs(seed=0):
    import zlib

    import numpy as np

    out = dict(_drawn_inputs(seed))
    spreads = {}
    factors = {'mod_b': 3.771,
     'attn_bqkv': 8.0,
     'attn_sink': 8.0,
     'c_ctx_2': 3.108,
     'norm1_w_2': 7.355,
     'norm2_w_2': 7.185,
     'gdn_norm_w_2': 8.0,
     'gla_gate_b_2': 8.0,
     'gla_norm_w_2': 8.0,
     'hy_pos_b1_2': 8.0,
     'hy_pos_b2_2': 8.0,
     'hy_pos_b3_2': 7.248,
     'hy_freq_2': 8.0,
     'final_norm_w_2': 2.817}
    for name, (base, spread) in spreads.items():
        noise = np.random.default_rng([zlib.crc32(name.encode()), seed]).standard_normal(out[name].shape)
        drawn = base * np.exp(spread * noise) if base else spread * noise
        out[name] = jnp.asarray(drawn.astype(out[name].dtype))
    for name, factor in factors.items():
        out[name] = (out[name] * factor).astype(out[name].dtype)
    return out
```

```python
import math

import numpy as np

import concourse.bass as bass
from concourse import mybir
from contextlib import ExitStack, contextmanager

F32 = mybir.dt.float32
U32 = mybir.dt.uint32
ALU = mybir.AluOpType
ACT = mybir.ActivationFunctionType
AX = mybir.AxisListType

P = 128
D = 1024
DT = D // P
T = 256
TT = T // P
FF = 2816
FFT = FF // P
PAIRS = FFT // 2
CH = 2048
NSLOT = 6
NH, NKV, HD = 16, 4, 64
LN_EPS, RMS_EPS = 1e-5, 1e-6
ALPHA = 4.0 ** 0.25
NEG = -1e30
CK = 64


class Counter:

    def __init__(self, sem):
        self.sem, self.base, self.pending = sem, 0, 0

    def advance(self, n):
        self.base += n


class Steps:

    def __init__(self, eng, counter):
        self.eng, self.counter, self.n = eng, counter, 0

    def __call__(self, instruction):
        self.n += 1
        instruction.then_inc(self.counter.sem, 1)
        self.eng.wait_ge(self.counter.sem, self.counter.base + self.n)

    def end(self):
        self.counter.pending += self.n


class Core:

    def __init__(self, nc, ctx, weights):
        self.nc, self.ctx, self.weights = nc, ctx, weights
        self.counters = {}
        self.issued = 0
        self.taken = 0
        self.total = weights.shape[0]
        self.wbuf = self.sb("weight_ring", [P, NSLOT, CH])
        self.loaded = [self.counter(f"weights_loaded_{s}") for s in range(NSLOT)]
        self.used = self.counter("weights_used")
        self.ps = [ctx.enter_context(nc.psum_tensor(f"bank{b}", [P, 512], F32)) for b in range(8)]

    def sb(self, name, shape, dt=F32):
        return self.ctx.enter_context(self.nc.sbuf_tensor(name, shape, dt))

    def counter(self, name):
        if name not in self.counters:
            self.counters[name] = Counter(self.ctx.enter_context(self.nc.semaphore(name)))
        return self.counters[name]

    @contextmanager
    def block(self):
        with self.nc.Block() as block:
            yield block
        for s in self.counters.values():
            s.base, s.pending = s.base + s.pending, 0

    def acc(self, j):
        return self.ps[j // 2][:, (j % 2) * T:(j % 2) * T + T]

    def load_ahead(self, sp, n):
        end = min(self.taken + n + NSLOT, self.total)
        first = self.issued
        count = end - first
        rounds = count // NSLOT

        def load(i, s):
            if not isinstance(i, int) or i >= NSLOT:
                sp.wait_ge(self.used.sem, i - (NSLOT - 1))
            sp.dma_start(self.wbuf[:, s, :], self.weights[i, :, :]).then_inc(self.loaded[s].sem, 16)

        i = first
        while i < end and i < NSLOT:
            load(i, i % NSLOT)
            i += 1
        rounds = (end - i) // NSLOT
        if rounds >= 2:
            with sp.Fori(0, rounds) as r:
                for s in range(NSLOT):
                    load(r * NSLOT + (i + s), (i + s) % NSLOT)
            i += rounds * NSLOT
        while i < end:
            load(i, i % NSLOT)
            i += 1
        self.issued = end

    def chunk(self, pe, n, r=0):
        i = self.taken + n
        pe.wait_ge(self.loaded[i % NSLOT].sem, 16 * (i // NSLOT + 1) + r * 16)
        return self.wbuf[:, i % NSLOT, :]


def ffn(core, h, hid, sg):
    nc = core.nc
    used = core.used
    silu_ready = core.counter("ffn_silu_ready")
    hid_ready = core.counter("ffn_hidden_ready")
    up_at = lambda p, t: used.base + 3 * p + t
    down_at = lambda p: used.base + 3 * p + 5
    rounds = (PAIRS - 3) // 2

    with core.block() as block:
        @block.sync
        def _(sp):
            core.load_ahead(sp, 3 * PAIRS)

        @block.tensor
        def _(pe):
            def up(p, par, n, r=0, first=False):
                for t in range(2):
                    w = core.chunk(pe, n + t, r)
                    if not first:
                        pe.wait_ge(hid_ready.sem, p * 2 + (hid_ready.base + t - 3))
                    bank = core.ps[4 + 2 * par + t]
                    for half in range(2):
                        for k in range(DT):
                            last = nc.tensor.matmul(bank[:, half * T:half * T + T],
                                                    w[:, k * 2 * P + half * P:k * 2 * P + half * P + P],
                                                    h[:, k, :], start=(k == 0), stop=(k == DT - 1))
                    last.then_inc(used.sem, 1)

            def down(p, par, n, r=0, first=False, final=False):
                w = core.chunk(pe, n, r)
                for t in range(2):
                    pe.wait_ge(hid_ready.sem, p * 2 + (hid_ready.base + t + 1))
                    for j in range(DT):
                        last = nc.tensor.matmul(core.acc(j), w[:, t * D + j * P:t * D + j * P + P],
                                                hid[:, par, t, :], start=(first and t == 0 and j % 2 == 0),
                                                stop=(final and t == 1), skip_group_check=True)
                last.then_inc(used.sem, 1)

            up(0, 0, 0, first=True)
            up(1, 1, 2, first=True)
            down(0, 0, 4, first=True)
            with pe.Fori(0, rounds) as r:
                up(r * 2 + 2, 0, 5, r)
                down(r * 2 + 1, 1, 7, r)
                up(r * 2 + 3, 1, 8, r)
                down(r * 2 + 2, 0, 10, r)
            up(PAIRS - 1, 0, 3 * PAIRS - 4)
            down(PAIRS - 2, 1, 3 * PAIRS - 2)
            down(PAIRS - 1, 0, 3 * PAIRS - 1, final=True)

        @block.scalar
        def _(act):
            def silu(p, at, par, t, first=False):
                act.wait_ge(used.sem, at)
                if not first:
                    act.wait_ge(hid_ready.sem, p * 2 + (hid_ready.base + t - 3))
                nc.scalar.activation(sg[:, par, t, :], core.ps[4 + 2 * par + t][:, T:2 * T],
                                     ACT.Silu).then_inc(silu_ready.sem, 1)

            for t in range(2):
                silu(0, used.base + t + 1, 0, t, True)
            for t in range(2):
                silu(1, up_at(1, t), 1, t, True)
            with act.Fori(0, rounds) as r:
                for n in range(4):
                    silu(r * 2 + (2 + n // 2), r * 6 + up_at(2 + n // 2, n % 2), n // 2, n % 2)
            for t in range(2):
                silu(PAIRS - 1, up_at(PAIRS - 1, t), 0, t)

        @block.vector
        def _(dve):
            def gate(p, par, t, freed=None):
                dve.wait_ge(silu_ready.sem, p * 2 + (silu_ready.base + t + 1))
                if freed is not None:
                    dve.wait_ge(used.sem, freed)
                nc.vector.tensor_tensor(hid[:, par, t, :], core.ps[4 + 2 * par + t][:, 0:T],
                                        sg[:, par, t, :], ALU.mult).then_inc(hid_ready.sem, 1)

            for n in range(4):
                gate(n // 2, n // 2, n % 2)
            with dve.Fori(0, rounds) as r:
                for n in range(4):
                    gate(r * 2 + (2 + n // 2), n // 2, n % 2, r * 6 + down_at(n // 2))
            for t in range(2):
                gate(PAIRS - 1, 0, t, down_at(PAIRS - 3))

    used.advance(3 * PAIRS)
    silu_ready.advance(2 * PAIRS)
    hid_ready.advance(2 * PAIRS)
    core.taken += 3 * PAIRS


def linear_tiles(core, pe, w, h, outs):
    for j, out in enumerate(outs):
        for k in range(DT):
            last = core.nc.tensor.matmul(out, w[:, k * 2 * P + j * P:k * 2 * P + j * P + P], h[:, k, :],
                                         start=(k == 0), stop=(k == DT - 1))
    return last


def linear(core, h, name="linear"):
    nc, used = core.nc, core.used
    with core.block() as block:
        @block.sync
        def _(sp):
            core.load_ahead(sp, 4)

        @block.tensor
        def _(pe):
            for c in range(4):
                w = core.chunk(pe, c)
                linear_tiles(core, pe, w, h, [core.acc(2 * c), core.acc(2 * c + 1)]).then_inc(used.sem, 1)

    used.advance(4)
    core.taken += 4


def modulation(core, cpad, bias, mod, nvec, partial):
    nc, used = core.nc, core.used
    nch = nvec * DT // 2
    parts_ready, turned = core.counter("mod_partial_copied"), core.counter("mod_turned")
    finished = core.counter("mod_finished")

    with core.block() as block:
        @block.sync
        def _(sp):
            core.load_ahead(sp, nch)

        @block.tensor
        def _(pe):
            def turn(n):
                pe.wait_ge(parts_ready.sem, parts_ready.base + n + 1)
                for t in range(2):
                    m = 2 * n + t
                    last = nc.tensor.matmul(core.ps[7][:, 2 * m:2 * m + 2], partial[:, n % 2, t * P:t * P + P],
                                            core.selector[:, :], start=True, stop=True)
                last.then_inc(turned.sem, 1)

            for n in range(nch):
                w = core.chunk(pe, n)
                if n >= 2:
                    pe.wait_ge(parts_ready.sem, parts_ready.base + n - 1)
                for k in range(DT):
                    g = k % 4
                    last = nc.tensor.matmul(core.ps[4 + n % 2][32 * g:32 * g + 32, 0:2 * P], cpad[:, k, :],
                                            w[:, k * 2 * P:(k + 1) * 2 * P], start=(k < 4), stop=(k >= 4),
                                            tile_position=(0, 32 * g))
                last.then_inc(used.sem, 1)
                if n >= 1:
                    turn(n - 1)
            turn(nch - 1)

        @block.scalar
        def _(act):
            for n in range(nch):
                act.wait_ge(used.sem, used.base + n + 1)
                if n >= 2:
                    act.wait_ge(turned.sem, turned.base + n - 1)
                nc.scalar.copy(partial[:, n % 2, :], core.ps[4 + n % 2][:, 0:2 * P]).then_inc(parts_ready.sem, 1)

        @block.vector
        def _(dve):
            dve.wait_ge(turned.sem, turned.base + nch)
            nc.vector.tensor_tensor(mod[:, :, :], core.ps[7][:, 0:4 * nch].rearrange("p (m i) -> p m i", i=2),
                                    bias.unsqueeze(2).broadcast_to([P, 2 * nch, 2]),
                                    ALU.add).then_inc(finished.sem, 1)

    used.advance(nch), parts_ready.advance(nch), turned.advance(nch), finished.advance(1)
    core.taken += nch


def layer_norm(core, x, gate, g, b, y_modulation, h, diff, sq, rstd):
    nc = core.nc
    mixed, mean_done, diff_done = core.counter("ln_mixed"), core.counter("ln_mean_done"), core.counter("ln_diff_done")
    sq_done, var_done, rstd_done = core.counter("ln_sq_done"), core.counter("ln_var_done"), core.counter("ln_rstd_done")
    unit_done, x_done, h_done = core.counter("ln_unit_done"), core.counter("ln_x_done"), core.counter("ln_h_done")
    mean, var = core.ps[4][:, 0:T], core.ps[5][:, 0:T]

    with core.block() as block:
        @block.tensor
        def _(pe):
            for j in range(DT):
                pe.wait_ge(mixed.sem, mixed.base + j + 1)
                last = nc.tensor.matmul(mean, core.ones_mean[:, :], x[:, j, :], start=(j == 0), stop=(j == DT - 1))
            last.then_inc(mean_done.sem, 1)
            for j in range(DT):
                pe.wait_ge(sq_done.sem, sq_done.base + j + 1)
                last = nc.tensor.matmul(var, core.ones_mean[:, :], sq[:, j, :], start=(j == 0), stop=(j == DT - 1))
            last.then_inc(var_done.sem, 1)

        def modulate(dve, j):
            scale, shift = y_modulation
            dve.wait_ge(x_done.sem, x_done.base + j + 1)
            nc.vector.tensor_scalar(h[:, j, :], x[:, j, :], scale[:, j:j + 1], shift[:, j:j + 1],
                                    ALU.mult, ALU.add).then_inc(h_done.sem, 1)

        @block.vector
        def _(dve):
            for j in range(DT):
                nc.vector.scalar_tensor_tensor(x[:, j, :], core.acc(j), gate[:, j:j + 1], x[:, j, :],
                                               ALU.mult, ALU.add).then_inc(mixed.sem, 1)
            dve.wait_ge(mean_done.sem, mean_done.base + 1)
            for j in range(DT):
                nc.vector.tensor_tensor(diff[:, j, :], x[:, j, :], mean, ALU.subtract).then_inc(diff_done.sem, 1)
            dve.wait_ge(rstd_done.sem, rstd_done.base + 1)
            nc.vector.reciprocal(rstd[:, :], rstd[:, :]).then_inc(rstd_done.sem, 1)
            dve.wait_ge(rstd_done.sem, rstd_done.base + 2)
            for j in range(DT):
                nc.vector.tensor_tensor(diff[:, j, :], diff[:, j, :], rstd[:, :], ALU.mult).then_inc(unit_done.sem, 1)
                if y_modulation is not None and j >= 2:
                    modulate(dve, j - 2)
            if y_modulation is not None:
                modulate(dve, DT - 2), modulate(dve, DT - 1)

        @block.scalar
        def _(act):
            for j in range(DT):
                act.wait_ge(diff_done.sem, diff_done.base + j + 1)
                nc.scalar.activation(sq[:, j, :], diff[:, j, :], ACT.Square).then_inc(sq_done.sem, 1)
            act.wait_ge(var_done.sem, var_done.base + 1)
            nc.scalar.activation(rstd[:, :], var, ACT.Sqrt, bias=core.ln_eps).then_inc(rstd_done.sem, 1)
            for j in range(DT):
                act.wait_ge(unit_done.sem, unit_done.base + j + 1)
                nc.scalar.activation(x[:, j, :], diff[:, j, :], ACT.Identity, scale=g[:, j:j + 1],
                                     bias=b[:, j:j + 1]).then_inc(x_done.sem, 1)

    for s in (mixed, diff_done, sq_done, unit_done, x_done):
        s.advance(DT)
    mean_done.advance(1), var_done.advance(1), rstd_done.advance(2)
    h_done.advance(DT if y_modulation is not None else 0)


def rms_norm(core, x, gate, scale, shift, h, sq, rstd):
    nc = core.nc
    mixed, sq_done, var_done = core.counter("rms_mixed"), core.counter("rms_sq_done"), core.counter("rms_mean_done")
    rstd_done, unit_done, h_done = core.counter("rms_rstd_done"), core.counter("rms_unit_done"), core.counter("rms_h_done")
    ms = core.ps[4][:, 0:T]

    with core.block() as block:
        @block.tensor
        def _(pe):
            for j in range(DT):
                pe.wait_ge(sq_done.sem, sq_done.base + j + 1)
                last = nc.tensor.matmul(ms, core.ones_mean[:, :], sq[:, j, :], start=(j == 0), stop=(j == DT - 1))
            last.then_inc(var_done.sem, 1)

        @block.vector
        def _(dve):
            if gate is not None:
                for j in range(DT):
                    nc.vector.scalar_tensor_tensor(x[:, j, :], core.acc(j), gate[:, j:j + 1], x[:, j, :],
                                                   ALU.mult, ALU.add).then_inc(mixed.sem, 1)
            dve.wait_ge(rstd_done.sem, rstd_done.base + 1)
            nc.vector.reciprocal(rstd[:, :], rstd[:, :]).then_inc(rstd_done.sem, 1)
            dve.wait_ge(rstd_done.sem, rstd_done.base + 2)
            for j in range(DT):
                nc.vector.tensor_tensor(sq[:, j, :], x[:, j, :], rstd[:, :], ALU.mult).then_inc(unit_done.sem, 1)

        @block.scalar
        def _(act):
            for j in range(DT):
                if gate is not None:
                    act.wait_ge(mixed.sem, mixed.base + j + 1)
                nc.scalar.activation(sq[:, j, :], x[:, j, :], ACT.Square).then_inc(sq_done.sem, 1)
            act.wait_ge(var_done.sem, var_done.base + 1)
            nc.scalar.activation(rstd[:, :], ms, ACT.Sqrt, bias=core.rms_eps).then_inc(rstd_done.sem, 1)
            for j in range(DT):
                act.wait_ge(unit_done.sem, unit_done.base + j + 1)
                nc.scalar.activation(h[:, j, :], sq[:, j, :], ACT.Identity, scale=scale[:, j:j + 1],
                                     bias=0.0 if shift is None else shift[:, j:j + 1]).then_inc(h_done.sem, 1)

    for s in (sq_done, unit_done, h_done):
        s.advance(DT)
    var_done.advance(1), rstd_done.advance(2)
    mixed.advance(DT if gate is not None else 0)


def attention(core, h, hc, out, a):
    nc, used = core.nc, core.used
    q, kk, v, tmp = a["q"], a["k"], a["v"], a["tmp"]
    bq, bk = core.col("bq"), core.col("bk")
    projected, biased = core.counter("attn_projected"), core.counter("attn_biased")
    turned, roped = core.counter("attn_rotated"), core.counter("attn_roped")

    with core.block() as block:
        @block.sync
        def _(sp):
            core.load_ahead(sp, 6)

        @block.tensor
        def _(pe):
            for c in range(4):
                w = core.chunk(pe, c)
                linear_tiles(core, pe, w, h, [core.acc(2 * c), core.acc(2 * c + 1)]).then_inc(used.sem, 1)
            w = core.chunk(pe, 4)
            for s, src in enumerate((h, hc)):
                last = linear_tiles(core, pe, w, src, [core.ps[4 + s][:, 0:T], core.ps[4 + s][:, T:2 * T]])
            last.then_inc(used.sem, 1)
            w = core.chunk(pe, 5)
            for s, src in enumerate((h, hc)):
                for t in range(TT):
                    for k in range(DT):
                        last = nc.tensor.matmul(core.ps[6 + s][:, t * T:t * T + T], src[:, k, t * P:t * P + P],
                                                w[:, k * T:k * T + T], start=(k == 0), stop=(k == DT - 1))
            last.then_inc(used.sem, 1)

        @block.vector
        def _(dve):
            for t in range(DT):
                if t % 2 == 0:
                    dve.wait_ge(used.sem, used.base + t // 2 + 1)
                nc.vector.tensor_scalar(q[:, t, :], core.acc(t), bq[:, t:t + 1], HD ** -0.5, ALU.add, ALU.mult)\
                    .then_inc(biased.sem, 1)
            dve.wait_ge(used.sem, used.base + 5)
            for s in range(2):
                for t in range(2):
                    nc.vector.tensor_scalar(kk[:, s, t, :], core.ps[4 + s][:, t * T:t * T + T], bk[:, t:t + 1],
                                            None, ALU.add).then_inc(biased.sem, 1)
            dve.wait_ge(used.sem, used.base + 6)
            for s in range(2):
                for t in range(TT):
                    nc.vector.tensor_tensor(v[:, s, t, :], core.ps[6 + s][:, t * T:t * T + T], a["bv"][:, :],
                                            ALU.add).then_inc(biased.sem, 1)

    used.advance(6)
    core.taken += 6
    biased.advance(DT + 8)

    with core.block() as block:
        pairs = [q[:, 2 * t:2 * t + 2, :] for t in range(DT // 2)] + [kk[:, 0, :, :]]
        flat = lambda x: x.rearrange("p a t -> p (a t)")

        @block.tensor
        def _(pe):
            for n, x in enumerate(pairs):
                nc.tensor.matmul(core.ps[n][:, :], a["swap"][:, :], flat(x), start=True, stop=True)\
                    .then_inc(turned.sem, 1)

        @block.vector
        def _(dve):
            step = Steps(dve, roped)
            both = lambda x: x.unsqueeze(1).broadcast_to([P, 2, T])
            for n, x in enumerate(pairs):
                dve.wait_ge(turned.sem, turned.base + n + 1)
                step(nc.vector.tensor_tensor(tmp[:, :, :], core.ps[n][:, :].rearrange("p (a t) -> p a t", a=2),
                                             both(a["sin"]), ALU.mult))
                step(nc.vector.tensor_tensor(x, x, both(a["cos"]), ALU.mult))
                step(nc.vector.tensor_tensor(x, x, tmp[:, :, :], ALU.add))
            step.end()

    turned.advance(len(pairs))

    scores_ready, masked, max_ready = core.counter("attn_scores"), core.counter("attn_masked"), core.counter("attn_max")
    exp_done, p_ready, p_turned = core.counter("attn_exp"), core.counter("attn_p_ready"), core.counter("attn_p_turned")
    pt_ready, pv_done, o_copied = core.counter("attn_pt_ready"), core.counter("attn_pv_done"), core.counter("attn_o_copied")
    dsteps = core.counter("attn_dve_steps")
    sm, pt, st = a["sm"], a["pt"], a["stat"]
    units = [(t, e, b) for t in range(DT) for e in range(2) for b in range(TT)]
    N = len(units)

    with core.block() as block:
        @block.tensor
        def _(pe):
            def scores(u):
                t, e, b = units[u]
                lo = 64 * e
                if u >= 2:
                    pe.wait_ge(masked.sem, masked.base + u - 1)
                for s in range(2):
                    last = nc.tensor.matmul(core.ps[u % 2][:, s * T:s * T + T], q[lo:lo + 64, t, b * P:b * P + P],
                                            kk[lo:lo + 64, s, t // 4, :], start=True, stop=True)
                last.then_inc(scores_ready.sem, 1)

            scores(0), scores(1)
            for u in range(N):
                t, e, b = units[u]
                head = 2 * (t // 4) + e
                pe.wait_ge(p_ready.sem, p_ready.base + u + 1)
                if u >= 2:
                    pe.wait_ge(pt_ready.sem, pt_ready.base + u - 1)
                for c in range(4):
                    last = nc.tensor.transpose(core.ps[2 + u % 2][:, c * P:c * P + P], sm[:, u % 2, c * P:c * P + P],
                                               core.ident[:, :])
                last.then_inc(p_turned.sem, 1)
                if u + 2 < N:
                    scores(u + 2)
                pe.wait_ge(pt_ready.sem, pt_ready.base + u + 1)
                if u % 4 == 0 and t >= 2:
                    pe.wait_ge(o_copied.sem, o_copied.base + t - 1)
                for c in range(4):
                    last = nc.tensor.matmul(core.ps[4 + t % 2][64 * e:64 * e + 64, b * P:b * P + P],
                                            v[:, c // 2, c % 2, head * HD:head * HD + HD],
                                            pt[:, u % 2, c * P:c * P + P], start=(c == 0), stop=(c == 3))
                last.then_inc(pv_done.sem, 1)

        @block.vector
        def _(dve):
            step = Steps(dve, dsteps)

            def top(u):
                t, e, b = units[u]
                head = 8 * (t // 4) + 4 * e + t % 4
                dve.wait_ge(scores_ready.sem, scores_ready.base + u + 1)
                if u >= 2:
                    dve.wait_ge(p_turned.sem, p_turned.base + u - 1)
                nc.vector.tensor_tensor(sm[:, u % 2, :], core.ps[u % 2][:, :], a["mask"][:, b, :], ALU.add)\
                    .then_inc(masked.sem, 1)
                dve.wait_ge(masked.sem, masked.base + u + 1)
                step(nc.vector.tensor_reduce(st[:, u % 2, 0:1], sm[:, u % 2, :], AX.X, ALU.max))
                nc.vector.tensor_scalar(st[:, u % 2, 1:2], st[:, u % 2, 0:1], a["sink"][:, head:head + 1], -1.0,
                                        ALU.max, ALU.mult).then_inc(max_ready.sem, 1)

            def normalize(u):
                dve.wait_ge(exp_done.sem, exp_done.base + u + 1)
                step(nc.vector.tensor_tensor(st[:, u % 2, 4:5], st[:, u % 2, 2:3], st[:, u % 2, 3:4], ALU.add))
                step(nc.vector.reciprocal(st[:, u % 2, 5:6], st[:, u % 2, 4:5]))
                nc.vector.tensor_scalar(sm[:, u % 2, :], sm[:, u % 2, :], st[:, u % 2, 5:6], None, ALU.mult)\
                    .then_inc(p_ready.sem, 1)

            top(0)
            for u in range(N):
                if u + 1 < N:
                    top(u + 1)
                normalize(u)
            step.end()

        @block.scalar
        def _(act):
            def copy_out(t):
                act.wait_ge(pv_done.sem, pv_done.base + 4 * t + 4)
                nc.scalar.copy(out[:, t, :], core.ps[4 + t % 2][:, 0:T]).then_inc(o_copied.sem, 1)

            def turn_back(u):
                act.wait_ge(p_turned.sem, p_turned.base + u + 1)
                if u >= 2:
                    act.wait_ge(pv_done.sem, pv_done.base + u - 1)
                nc.scalar.copy(pt[:, u % 2, :], core.ps[2 + u % 2][:, :]).then_inc(pt_ready.sem, 1)

            for u in range(N):
                t, e, b = units[u]
                head = 8 * (t // 4) + 4 * e + t % 4
                act.wait_ge(max_ready.sem, max_ready.base + u + 1)
                nc.scalar.activation(sm[:, u % 2, :], sm[:, u % 2, :], ACT.Exp, bias=st[:, u % 2, 1:2],
                                     accum_out=st[:, u % 2, 2:3])
                nc.scalar.activation(st[:, u % 2, 3:4], a["sink"][:, head:head + 1], ACT.Exp,
                                     bias=st[:, u % 2, 1:2]).then_inc(exp_done.sem, 1)
                if u >= 1:
                    turn_back(u - 1)
                    if (u - 1) % 4 == 3 and u >= 8:
                        copy_out((u - 1) // 4 - 1)
            turn_back(N - 1)
            copy_out(DT - 2), copy_out(DT - 1)

    for s in (scores_ready, masked, max_ready, exp_done, p_ready, p_turned, pt_ready, pv_done):
        s.advance(N)
    o_copied.advance(DT)


def fourier(core, h, out, cs, uv):
    nc = core.nc
    uv_ready, uv_copied = core.counter("fourier_uv_ready"), core.counter("fourier_uv_copied")
    f_ready, f_copied = core.counter("fourier_out_ready"), core.counter("fourier_out_copied")
    G = D // 256
    with core.block() as block:
        @block.tensor
        def _(pe):
            def features(g):
                for t in range(TT):
                    if g >= 2:
                        pe.wait_ge(uv_copied.sem, uv_copied.base + 2 * (g - 2) + t + 1)
                    for k in range(2):
                        last = nc.tensor.matmul(core.ps[2 * (g % 2) + t][:, :], h[:, 2 * g + k, t * P:t * P + P],
                                                cs[:, k, 0:2, :].rearrange("p a n -> p (a n)"),
                                                start=(k == 0), stop=(k == 1))
                    last.then_inc(uv_ready.sem, 1)

            def tokens(g):
                pe.wait_ge(uv_copied.sem, uv_copied.base + 2 * g + 2)
                if g >= 2:
                    pe.wait_ge(f_copied.sem, f_copied.base + g - 1)
                for m in range(2):
                    n = 0
                    for part in (0, 1):
                        for t in range(TT):
                            last = nc.tensor.matmul(core.ps[4 + g % 2][:, m * T:m * T + T],
                                                    uv[:, g % 2, t, part, m * P:m * P + P],
                                                    cs[:, t, 2 * part, :], start=(n == 0), stop=(n == 3))
                            n += 1
                last.then_inc(f_ready.sem, 1)

            features(0)
            for g in range(G):
                if g + 1 < G:
                    features(g + 1)
                tokens(g)

        @block.scalar
        def _(act):
            for n in range(2 * G):
                g, t = n // 2, n % 2
                act.wait_ge(uv_ready.sem, uv_ready.base + n + 1)
                if g >= 2:
                    act.wait_ge(f_ready.sem, f_ready.base + g - 1)
                nc.scalar.copy(uv[:, g % 2, t, :, :].rearrange("p a n -> p (a n)"), core.ps[2 * (g % 2) + t][:, :])\
                    .then_inc(uv_copied.sem, 1)

        @block.vector
        def _(dve):
            for g in range(G):
                dve.wait_ge(f_ready.sem, f_ready.base + g + 1)
                nc.vector.tensor_copy(out[:, 2 * g:2 * g + 2, :].rearrange("p m t -> p (m t)"),
                                      core.ps[4 + g % 2][:, :]).then_inc(f_copied.sem, 1)

    uv_ready.advance(2 * G), uv_copied.advance(2 * G), f_ready.advance(G), f_copied.advance(G)


NG = 4
TK = 2 * TT


def ab_project(core, h, hc, b):
    nc, used = core.nc, core.used
    raw, qkv = b["raw"], b["qkv"]
    copied, conv, small, convd = (core.counter(n) for n in ("ab_copied", "ab_conv_steps", "ab_small_ready", "ab_conv_done"))
    padded, smalls = core.counter("ab_padded"), core.counter("ab_small_copied")
    with core.block() as block:
        @block.sync
        def _(sp):
            core.load_ahead(sp, 14)

        @block.tensor
        def _(pe):
            def free(n):
                if n >= 8:
                    pe.wait_ge(copied.sem, copied.base + n - 7)

            n = 0
            for c in range(14):
                w = core.chunk(pe, c)
                if c in (10, 11):
                    for src in (hc, h):
                        free(n)
                        for t in range(TT):
                            for k in range(DT):
                                last = nc.tensor.matmul(core.ps[n % 8][:, t * T:t * T + T], src[:, k, t * P:t * P + P],
                                                        w[:, k * T:k * T + T], start=(k == 0), stop=(k == DT - 1))
                        last.then_inc(used.sem if src is h else small.sem, 1)
                        n += 1
                else:
                    for src in ((hc, h) if c in (0, 1, 2, 3, 9) else (h,)):
                        free(n)
                        last = linear_tiles(core, pe, w, src, [core.ps[n % 8][:, 0:T], core.ps[n % 8][:, T:2 * T]])
                        last.then_inc(used.sem if src is h else small.sem, 1)
                        n += 1

        order, nctx = [], 0
        for c in range(14):
            for src in ((0, 1) if c in (0, 1, 2, 3, 9, 10, 11) else (1,)):
                nctx += src == 0
                order.append((c, src, nctx))

        def destination(c, src):
            if c < 4:
                tile = 2 * c + (12 if src else 0)
                return raw[:, tile:tile + 2, 1:T + 1]
            if c < 6:
                return raw[:, 8 + 2 * (c - 4):10 + 2 * (c - 4), 1:T + 1]
            if c < 8:
                return b["gz"][:, 2 * (c - 6):2 * (c - 6) + 2, :]
            if c == 8:
                return b["lq"][:, :, :]
            if c == 9:
                return b["lk"][:, :, src * T:src * T + T]
            if c < 12:
                return b["lv"][:, 2 * src:2 * src + 2, (c - 10) * T:(c - 10) * T + T]
            return b["lg"][:, 2 * (c - 12):2 * (c - 12) + 2, :]

        @block.scalar
        def _(act):
            for n, (c, src, nctx) in enumerate(order):
                if src:
                    act.wait_ge(used.sem, used.base + c + 1)
                else:
                    act.wait_ge(small.sem, small.base + nctx)
                if n == 0:
                    act.wait_ge(padded.sem, padded.base + 1)
                nc.scalar.copy(destination(c, src), core.ps[n % 8][:, :].rearrange("p (a t) -> p a t", a=2))\
                    .then_inc(copied.sem, 1)
            for i in range(20):
                act.wait_ge(convd.sem, convd.base + i + 1)
                nc.scalar.activation(qkv[:, i, :], qkv[:, i, :], ACT.Silu).then_inc(smalls.sem, 1)

        @block.vector
        def _(dve):
            nc.vector.memset(raw[:, :, 0:1], 0.0)
            nc.vector.memset(raw[:, :, T + 1:T + 2], 0.0).then_inc(padded.sem, 1)
            dve.wait_ge(padded.sem, padded.base + 1)
            step = Steps(dve, conv)
            w = core.col("ab_conv")
            n_of = {(c, src): n for n, (c, src, _) in enumerate(order)}
            for i in range(20):
                c, src = (i // 2, 0) if i < 8 else ((4 + (i - 8) // 2, 1) if i < 12 else ((i - 12) // 2, 1))
                tile = i + 4 if i < 8 else i - 8
                dve.wait_ge(copied.sem, copied.base + n_of[(c, src)] + 1)
                y = qkv[:, i, :]
                step(nc.vector.tensor_scalar(y, raw[:, i, 0:T], w[:, tile:tile + 1], None, ALU.mult))
                step(nc.vector.scalar_tensor_tensor(y, raw[:, i, 1:T + 1], w[:, 12 + tile:13 + tile], y, ALU.mult, ALU.add))
                nc.vector.scalar_tensor_tensor(y, raw[:, i, 2:T + 2], w[:, 24 + tile:25 + tile], y, ALU.mult, ALU.add)\
                    .then_inc(convd.sem, 1)
            step.end()

    nout = len(order)
    used.advance(14)
    core.taken += 14
    copied.advance(nout), small.advance(nout - 14), padded.advance(1), convd.advance(20), smalls.advance(20)


def ab_gates(core, h, hc, b):
    nc = core.nc
    g, beta, gc, la = b["g"], b["beta"], b["gc"], b["la"]
    pe_s, dve_s, act_s = core.counter("gates_products"), core.counter("gates_dve_steps"), core.counter("gates_act_steps")
    wsm = b["w_small"]
    with core.block() as block:
        @block.tensor
        def _(pe):
            for s, src in enumerate((hc, h)):
                for t in range(TT):
                    n = 2 * s + t
                    for k in range(DT):
                        nc.tensor.matmul(core.ps[0][:, n * 16:n * 16 + 16], src[:, k, t * P:t * P + P],
                                         wsm[:, k, 0:16], start=(k == 0), stop=(k == DT - 1))
                for k in range(DT):
                    last = nc.tensor.matmul(core.ps[1][0:32, s * T:s * T + T], wsm[:, k, 16:48], src[:, k, :],
                                            start=(k == 0), stop=(k == DT - 1))
            last.then_inc(pe_s.sem, 1)
            pe.wait_ge(act_s.sem, act_s.base + 1)
            for d in range(2):
                for t in range(2):
                    last = nc.tensor.matmul(core.ps[2 + 2 * d + t][:, :], b["w_gate"][0:32, d, t * P:t * P + P],
                                            b["llr"][0:32, :], start=True, stop=True)
            last.then_inc(pe_s.sem, 1)
            pe.wait_ge(dve_s.sem, dve_s.base + b["g_steps"])
            for n in range(TK):
                for d in range(2):
                    nc.tensor.matmul(core.ps[6][:, n * 8 + 4 * d:n * 8 + 4 * d + 4], b["tri"][:, d, :],
                                     g[:, n, 4 * d:4 * d + 4], start=True, stop=True)
                last = nc.tensor.matmul(core.ps[6][:, 32 + n * 8:32 + n * 8 + 8], b["tri"][:, 2, :], g[:, n, :],
                                        start=True, stop=True)
            last.then_inc(pe_s.sem, 1)

        @block.scalar
        def _(act):
            step = Steps(act, act_s)
            act.wait_ge(pe_s.sem, pe_s.base + 1)
            step(nc.scalar.copy(b["llr"][0:32, :], core.ps[1][0:32, :]))
            act.wait_ge(dve_s.sem, dve_s.base + 2)
            step(nc.scalar.activation(b["t1"][:, :, :], b["t1"][:, :, :], ACT.Exp))
            step(nc.scalar.activation(b["t1"][:, :, :], b["t1"][:, :, :], ACT.Ln, bias=core.one[:, 0:1]))
            step(nc.scalar.activation(b["ea"][:, :], b["a_log"][:, :], ACT.Exp))
            act.wait_ge(dve_s.sem, dve_s.base + b["la_steps"])
            for i in range(4):
                step(nc.scalar.activation(b["lt"][:, i, :], b["lt"][:, i, :], ACT.Exp))
                step(nc.scalar.activation(b["lt"][:, i, :], b["lt"][:, i, :], ACT.Ln, bias=core.one[:, 0:1]))
            step(nc.scalar.activation(beta[:, :, :], core.ps[0][:, 0:64].rearrange("p (n i) -> p n i", i=16)[:, :, 8:16],
                                      ACT.Sigmoid))
            assert step.n == 13
            step.end()

        @block.vector
        def _(dve):
            step = Steps(dve, dve_s)
            ga = core.ps[0][:, 0:64].rearrange("p (n i) -> p n i", i=16)[:, :, 0:8]
            dve.wait_ge(pe_s.sem, pe_s.base + 1)
            step(nc.vector.tensor_tensor(b["t2"][:, :, :], ga, b["dt_bias"].unsqueeze(1).broadcast_to([P, TK, 8]), ALU.add))
            step(nc.vector.scalar_tensor_tensor(b["t1"][:, :, :], b["t2"][:, :, :], -1.0, b["t2"][:, :, :], ALU.mult, ALU.min))
            step(nc.vector.tensor_scalar(b["t2"][:, :, :], b["t2"][:, :, :], 0.0, None, ALU.max))
            dve.wait_ge(act_s.sem, act_s.base + 4)
            step(nc.vector.tensor_tensor(b["t2"][:, :, :], b["t2"][:, :, :], b["t1"][:, :, :], ALU.add))
            step(nc.vector.tensor_tensor(b["t2"][:, :, :], b["t2"][:, :, :],
                                         b["ea"].unsqueeze(1).broadcast_to([P, TK, 8]), ALU.mult))
            step(nc.vector.tensor_scalar(g[:, :, :], b["t2"][:, :, :], -1.0, None, ALU.mult))
            assert step.n == b["g_steps"]
            gb = core.col("gla_gate_b")
            dve.wait_ge(pe_s.sem, pe_s.base + 2)
            for i in range(4):
                step(nc.vector.tensor_scalar(b["la"][:, i, :], core.ps[2 + i][:, :], gb[:, i:i + 1], None, ALU.add))
                step(nc.vector.scalar_tensor_tensor(b["lt"][:, i, :], b["la"][:, i, :], -1.0, b["la"][:, i, :], ALU.mult, ALU.min))
                step(nc.vector.tensor_scalar(b["la"][:, i, :], b["la"][:, i, :], 0.0, None, ALU.min))
            assert step.n == b["la_steps"]
            dve.wait_ge(act_s.sem, act_s.base + 12)
            for i in range(4):
                step(nc.vector.tensor_tensor(b["la"][:, i, :], b["la"][:, i, :], b["lt"][:, i, :], ALU.subtract))
                step(nc.vector.tensor_scalar(b["la"][:, i, :], b["la"][:, i, :], 1.0 / 16.0, None, ALU.mult))
            dve.wait_ge(pe_s.sem, pe_s.base + 3)
            step(nc.vector.tensor_copy(gc[:, :, :, :].rearrange("p a n i -> p (a n i)"), core.ps[6][:, 0:64]))
            step.end()

    pe_s.advance(3)


def l2_norm(core, b):
    nc = core.nc
    qkv = b["qkv"]
    tiles = [0, 1, 2, 3, 8, 9, 10, 11, 12, 13, 14, 15]
    sq_d, sum_d, scaled = core.counter("l2_squares"), core.counter("l2_sums"), core.counter("l2_dve_steps")
    norm_d = core.counter("l2_norms")
    with core.block() as block:
        @block.scalar
        def _(act):
            for n, i in enumerate(tiles):
                nc.scalar.activation(b["sq12"][:, n, :], qkv[:, i, :], ACT.Square).then_inc(sq_d.sem, 1)
            for n, i in enumerate(tiles):
                act.wait_ge(sum_d.sem, sum_d.base + n // 2 + 1)
                query = 8 <= i < 12
                nc.scalar.activation(b["sq12"][:, n, :], core.ps[n // 2][:, (n % 2) * T:(n % 2) * T + T], ACT.Sqrt,
                                     scale=float(P) if query else 1.0, bias=core.q_eps if query else core.rms_eps)\
                    .then_inc(norm_d.sem, 1)

        @block.tensor
        def _(pe):
            for n in range(12):
                pe.wait_ge(sq_d.sem, sq_d.base + n + 1)
                last = nc.tensor.matmul(core.ps[n // 2][:, (n % 2) * T:(n % 2) * T + T], core.ones[:, :],
                                        b["sq12"][:, n, :], start=True, stop=True)
                if n % 2:
                    last.then_inc(sum_d.sem, 1)

        @block.vector
        def _(dve):
            step = Steps(dve, scaled)
            for n, i in enumerate(tiles):
                dve.wait_ge(norm_d.sem, norm_d.base + n + 1)
                step(nc.vector.reciprocal(b["sq12"][:, n, :], b["sq12"][:, n, :]))
                step(nc.vector.tensor_tensor(qkv[:, i, :], qkv[:, i, :], b["sq12"][:, n, :], ALU.mult))
            step.end()

    sq_d.advance(12), sum_d.advance(6), norm_d.advance(12)


def turn_tiles(core, pairs):
    nc = core.nc
    ready, copied = core.counter("tiles_turned"), core.counter("tiles_copied")
    with core.block() as block:
        @block.tensor
        def _(pe):
            for n, (ins, out) in enumerate(pairs):
                if n >= 4:
                    pe.wait_ge(copied.sem, copied.base + n - 3)
                for c, x in enumerate(ins):
                    last = nc.tensor.transpose(core.ps[n % 4][:, c * P:c * P + P], x, core.ident[:, :])
                last.then_inc(ready.sem, 1)

        @block.scalar
        def _(act):
            for n, (ins, out) in enumerate(pairs):
                act.wait_ge(ready.sem, ready.base + n + 1)
                nc.scalar.copy(out, core.ps[n % 4][:, :]).then_inc(copied.sem, 1)

    ready.advance(len(pairs)), copied.advance(len(pairs))


def chunk_tile(c):
    return c // 2, c % 2


def gdn_factors(core, b):
    nc = core.nc
    gc = b["gc"]
    d_s, a_s = core.counter("gdn_dve_steps"), core.counter("gdn_act_steps")
    with core.block() as block:
        @block.scalar
        def _(act):
            step = Steps(act, a_s)
            step(nc.scalar.activation(b["bg"][:, :, :], gc[:, 0, :, :], ACT.Exp))
            act.wait_ge(d_s.sem, d_s.base + 2)
            step(nc.scalar.activation(b["ed"][:, :, :], b["ed"][:, :, :], ACT.Exp))
            step.end()

        @block.vector
        def _(dve):
            step = Steps(dve, d_s)
            step(nc.vector.tensor_scalar(b["ngc"][:, :, :], gc[:, 0, :, :], -1.0, None, ALU.mult))
            step(nc.vector.tensor_tensor(b["ed"][:, :, :], gc[:, 1, :, :], gc[:, 0, :, :], ALU.subtract))
            dve.wait_ge(a_s.sem, a_s.base + 1)
            step(nc.vector.tensor_tensor(b["bg"][:, :, :], b["bg"][:, :, :], b["beta"][:, :, :], ALU.mult))
            step.end()


def gdn_tile(core, b, n):
    nc = core.nc
    g, beta, gc, rows, qkv = b["g"], b["beta"], b["gc"], b["rows"], b["qkv"]
    row_s, copy_s = core.counter("gdn_rows_ready"), core.counter("gdn_rows_copied")
    kk_s, ex_s, dd_s = core.counter("gdn_kk_ready"), core.counter("gdn_exponent_ready"), core.counter("gdn_decay_ready")
    l_s, r_s, q_s = core.counter("gdn_l_ready"), core.counter("gdn_rhs_ready"), core.counter("gdn_qd_exponential")
    latent = n >= TT
    m0 = n - TT
    k_of = lambda h: qkv[:, 12 + h, m0 * P:m0 * P + P] if latent else qkv[:, h, n * P:n * P + P]
    q_of = lambda h: qkv[:, 8 + h, m0 * P:m0 * P + P]
    jobs = [("l", d) for d in range(2)] + ([("a", d) for d in range(2)] if latent else [])

    with core.block() as block:
        @block.tensor
        def _(pe):
            for d in range(2):
                for h in range(NG):
                    last = nc.tensor.matmul(core.ps[d][:, h * P:h * P + P],
                                            g[:, n, 4 * d + h:4 * d + h + 1].broadcast_to([P, P]), b["tri"][:, d, :],
                                            start=True, stop=True)
                last.then_inc(row_s.sem, 1)
            for m in range(2 if latent else 1):
                for h in range(NG):
                    last = nc.tensor.matmul(core.ps[2 + m][:, h * P:h * P + P], k_of(h), q_of(h) if m else k_of(h),
                                            start=True, stop=True)
                last.then_inc(kk_s.sem, 1)

        @block.scalar
        def _(act):
            for d in range(2):
                act.wait_ge(row_s.sem, row_s.base + d + 1)
                nc.scalar.copy(rows[:, 4 * d:4 * d + 4, :].rearrange("p h t -> p (h t)"), core.ps[d][:, :])\
                    .then_inc(copy_s.sem, 1)
            for d in range(2):
                act.wait_ge(copy_s.sem, copy_s.base + d + 1)
                row = rows[:, 4 * d:4 * d + 4, :]
                at = row.rearrange("p h (c t) -> p h c t", t=CK)[:, :, :, CK - 1 if d == 0 else 0]
                last = nc.scalar.activation(b["gl"][:, 4 * d:4 * d + 4, 2 * n:2 * n + 2], at, ACT.Exp)
                if latent:
                    last = nc.scalar.activation(b["qd"][:, 4 * d:4 * d + 4, m0 * P:m0 * P + P], row, ACT.Exp)
                last.then_inc(q_s.sem, 1)
            for m, (kind, d) in enumerate(jobs):
                act.wait_ge(ex_s.sem, ex_s.base + m + 1)
                src = gc[:, 0, :, :] if kind == "l" else b["ngc"][:, :, :]
                for h in range(NG):
                    last = nc.scalar.activation(b["dd"][:, m % 2, h, :], b["dd"][:, m % 2, h, :], ACT.Exp,
                                                bias=src[:, n, 4 * d + h:4 * d + h + 1])
                last.then_inc(dd_s.sem, 1)

        @block.vector
        def _(dve):
            def exponent(m):
                kind, d = jobs[m]
                if m >= 2:
                    dve.wait_ge(l_s.sem, l_s.base + m - 1)
                else:
                    dve.wait_ge(copy_s.sem, copy_s.base + d + 1)
                mask = b["masks"][:, d, 0 if kind == "l" else 1, :].unsqueeze(1).broadcast_to([P, NG, P])
                nc.vector.tensor_tensor(b["dd"][:, m % 2, :, :], mask, rows[:, 4 * d:4 * d + 4, :],
                                        ALU.subtract if kind == "l" else ALU.add).then_inc(ex_s.sem, 1)

            exponent(0), exponent(1)
            for d in range(2):
                for out, x, f in (("kbe", "ktm", "bg"), ("vb", "vtm", "beta")):
                    nc.vector.tensor_tensor(b[out][:, 4 * d:4 * d + 4, :], b[x][:, n, :, :],
                                            b[f][:, n, 4 * d:4 * d + 4].unsqueeze(2).broadcast_to([P, NG, P]),
                                            ALU.mult).then_inc(r_s.sem, 1)
                if latent:
                    dve.wait_ge(q_s.sem, q_s.base + d + 1)
                    at = b["qd"][:, 4 * d:4 * d + 4, m0 * P:m0 * P + P]
                    nc.vector.tensor_tensor(at, at, qkv[:, 8:12, m0 * P:m0 * P + P], ALU.mult).then_inc(r_s.sem, 1)
            for m, (kind, d) in enumerate(jobs):
                dve.wait_ge(dd_s.sem, dd_s.base + m + 1)
                if kind == "l":
                    dve.wait_ge(kk_s.sem, kk_s.base + 1)
                    for h in range(NG):
                        last = nc.vector.scalar_tensor_tensor(b["l"][:, d, h * P:h * P + P],
                                                              core.ps[2][:, h * P:h * P + P],
                                                              beta[:, n, 4 * d + h:4 * d + h + 1],
                                                              b["dd"][:, m % 2, h, :], ALU.mult, ALU.mult)
                else:
                    dve.wait_ge(kk_s.sem, kk_s.base + 2)
                    last = nc.vector.tensor_tensor(b["att"][m0][:, 4 * d:4 * d + 4, :].rearrange("p h t -> p (h t)"),
                                                   core.ps[3][:, :],
                                                   b["dd"][:, m % 2, :, :].rearrange("p h t -> p (h t)"), ALU.mult)
                last.then_inc(l_s.sem, 1)
                if m + 2 < len(jobs):
                    exponent(m + 2)

    row_s.advance(2), copy_s.advance(2), q_s.advance(2), r_s.advance(6 if latent else 4)
    kk_s.advance(2 if latent else 1), ex_s.advance(len(jobs)), dd_s.advance(len(jobs)), l_s.advance(len(jobs))


def gdn_solve(core, b, tile):
    nc = core.nc
    LEVELS = 6
    x, w, o, pm, l = b["x"], b["w"], b["o"], b["pm"], b["l"]
    names = ("gdn_masked", "gdn_p_ready", "gdn_p_copied", "gdn_wp_ready", "gdn_updated", "gdn_w_copied", "gdn_out_copied")
    sg = [{k: core.counter(f"{k}_{d}") for k in names} for d in range(2)]
    own = [core.counter(f"gdn_solve_dve_{d}") for d in range(2)]
    hs = [slice(i * P, i * P + P) for i in range(NG)]

    with core.block() as block:
        @block.tensor
        def _(pe):
            for n in range(1):
                for d in range(2):
                    s = sg[d]
                    pe.wait_ge(s["gdn_masked"].sem, s["gdn_masked"].base + LEVELS * n + 1)
                    if n >= 1:
                        pe.wait_ge(s["gdn_out_copied"].sem, s["gdn_out_copied"].base + 2 * n)
                    for h in hs:
                        last = nc.tensor.transpose(core.ps[d][:, h], x[:, d, h], core.ident[:, :])
                    last.then_inc(s["gdn_p_ready"].sem, 1)
                for lv in range(1, LEVELS):
                    for d in range(2):
                        s = sg[d]
                        pe.wait_ge(s["gdn_masked"].sem, s["gdn_masked"].base + LEVELS * n + lv + 1)
                        if lv == 1:
                            pe.wait_ge(s["gdn_w_copied"].sem, s["gdn_w_copied"].base + n + 1)
                        else:
                            pe.wait_ge(s["gdn_updated"].sem, s["gdn_updated"].base + (LEVELS - 1) * n + lv - 1)
                        for h in hs:
                            last = nc.tensor.matmul(core.ps[d][:, h], o[:, d, h], w[:, d, h], start=True, stop=True)
                        last.then_inc(s["gdn_p_ready"].sem, 1)
                    for d in range(2):
                        s = sg[d]
                        pe.wait_ge(s["gdn_p_copied"].sem, s["gdn_p_copied"].base + (LEVELS - 1) * n + lv)
                        for h in hs:
                            last = nc.tensor.matmul(core.ps[2 + d][:, h], x[:, d, h], pm[:, d, h], start=True, stop=True)
                        if lv < LEVELS - 1:
                            for h in hs:
                                last = nc.tensor.matmul(core.ps[4 + d][:, h], pm[:, d, h], x[:, d, h],
                                                        start=True, stop=True)
                        last.then_inc(s["gdn_wp_ready"].sem, 1)
                for d in range(2):
                    s = sg[d]
                    pe.wait_ge(s["gdn_updated"].sem, s["gdn_updated"].base + (LEVELS - 1) * (n + 1))
                    if n >= 1:
                        pe.wait_ge(s["gdn_out_copied"].sem, s["gdn_out_copied"].base + 2 * n - 1)
                    for i, h in enumerate(hs):
                        last = nc.tensor.matmul(core.ps[6 + d][:, h], w[:, d, h], b["vb"][:, 4 * d + i, :],
                                                start=True, stop=True)
                    last.then_inc(s["gdn_wp_ready"].sem, 1)
                    for i, h in enumerate(hs):
                        last = nc.tensor.matmul(core.ps[d][:, h], b["kbe"][:, 4 * d + i, :], w[:, d, h],
                                                start=True, stop=True)
                    last.then_inc(s["gdn_p_ready"].sem, 1)

        @block.scalar
        def _(act):
            for n in range(1):
                for d in range(2):
                    s = sg[d]
                    act.wait_ge(s["gdn_p_ready"].sem, s["gdn_p_ready"].base + (LEVELS + 1) * n + 1)
                    nc.scalar.copy(w[:, d, :], core.ps[d][:, :]).then_inc(s["gdn_w_copied"].sem, 1)
                for lv in range(1, LEVELS):
                    for d in range(2):
                        s = sg[d]
                        act.wait_ge(s["gdn_p_ready"].sem, s["gdn_p_ready"].base + (LEVELS + 1) * n + lv + 1)
                        nc.scalar.copy(pm[:, d, :], core.ps[d][:, :]).then_inc(s["gdn_p_copied"].sem, 1)
                for d in range(2):
                    s = sg[d]
                    act.wait_ge(s["gdn_wp_ready"].sem, s["gdn_wp_ready"].base + LEVELS * (n + 1))
                    nc.scalar.copy(b["u0"][:, tile, 4 * d:4 * d + 4, :].rearrange("p h t -> p (h t)"), core.ps[6 + d][:, :])\
                        .then_inc(s["gdn_out_copied"].sem, 1)
                    act.wait_ge(s["gdn_p_ready"].sem, s["gdn_p_ready"].base + (LEVELS + 1) * (n + 1))
                    nc.scalar.copy(b["kcdT"][:, tile, 4 * d:4 * d + 4, :].rearrange("p h t -> p (h t)"), core.ps[d][:, :])\
                        .then_inc(s["gdn_out_copied"].sem, 1)

        @block.vector
        def _(dve):
            steps = [Steps(dve, own[d]) for d in range(2)]

            def mask(n, lv, d, out):
                return nc.vector.tensor_tensor(out[:, d, :].rearrange("p (h t) -> p h t", h=NG),
                                               l[:, d, :].rearrange("p (h t) -> p h t", h=NG),
                                               b["levels"][:, d, lv, :].unsqueeze(1).broadcast_to([P, NG, P]), ALU.mult)

            for n in range(1):
                for d in range(2):
                    s = sg[d]
                    if n >= 1:
                        dve.wait_ge(s["gdn_p_ready"].sem, s["gdn_p_ready"].base + (LEVELS + 1) * n)
                    steps[d](mask(n, 0, d, x))
                    nc.vector.tensor_tensor(x[:, d, :].rearrange("p (h t) -> p h t", h=NG),
                                            core.ident[:, :].unsqueeze(1).broadcast_to([P, NG, P]),
                                            x[:, d, :].rearrange("p (h t) -> p h t", h=NG), ALU.subtract)\
                        .then_inc(s["gdn_masked"].sem, 1)
                for lv in range(1, LEVELS):
                    for d in range(2):
                        s = sg[d]
                        if lv >= 2:
                            dve.wait_ge(s["gdn_p_ready"].sem, s["gdn_p_ready"].base + (LEVELS + 1) * n + lv)
                        mask(n, lv, d, o).then_inc(s["gdn_masked"].sem, 1)
                    for d in range(2):
                        s = sg[d]
                        dve.wait_ge(s["gdn_wp_ready"].sem, s["gdn_wp_ready"].base + LEVELS * n + lv)
                        last = nc.vector.tensor_tensor(w[:, d, :], w[:, d, :], core.ps[2 + d][:, :], ALU.subtract)
                        if lv < LEVELS - 1:
                            last = nc.vector.tensor_tensor(x[:, d, :], x[:, d, :], core.ps[4 + d][:, :], ALU.subtract)
                        last.then_inc(s["gdn_updated"].sem, 1)
            for s in steps:
                s.end()

    for s in sg:
        s["gdn_masked"].advance(LEVELS), s["gdn_p_ready"].advance(LEVELS + 1)
        s["gdn_p_copied"].advance(LEVELS - 1), s["gdn_wp_ready"].advance(LEVELS)
        s["gdn_updated"].advance(LEVELS - 1), s["gdn_w_copied"].advance(1)
        s["gdn_out_copied"].advance(2)


def gdn_scan(core, b):
    nc = core.nc
    s, u = b["s"], b["u"]
    ks_s = [core.counter(f"gdn_ks_ready_{d}") for d in range(2)]
    u_s = [core.counter(f"gdn_u_ready_{d}") for d in range(2)]
    du_s = [core.counter(f"gdn_delta_ready_{d}") for d in range(2)]
    st_s = [core.counter(f"gdn_state_ready_{d}") for d in range(2)]
    z_s = core.counter("gdn_state_cleared")
    order = [[0, 1, 2, 3, 4, 5, 6, 7], [3, 2, 1, 0, 7, 6, 5, 4]]
    opened = set()

    with core.block() as block:
        @block.tensor
        def _(pe):
            pe.wait_ge(z_s.sem, z_s.base + 1)
            for i in range(8):
                for d in range(2):
                    n, half = chunk_tile(order[d][i])
                    lo = CK * half
                    if i >= 1:
                        pe.wait_ge(st_s[d].sem, st_s[d].base + i)
                    for h in range(NG):
                        last = nc.tensor.matmul(core.ps[d][lo:lo + CK, h * P:h * P + P],
                                                b["kcdT"][:, n, 4 * d + h, lo:lo + CK], s[:, 4 * d + h, :],
                                                start=True, stop=True)
                    last.then_inc(ks_s[d].sem, 1)
                for d in range(2):
                    n, half = chunk_tile(order[d][i])
                    lo = CK * half
                    if n >= 2:
                        at = (n - 2) * P + lo
                        for h in range(NG):
                            bank = 6 + h // 2
                            nc.tensor.matmul(core.ps[bank][:, (h % 2) * T + at:(h % 2) * T + at + CK],
                                             s[:, 4 * d + h, :], b["qd"][:, 4 * d + h, at:at + CK],
                                             start=bank not in opened, stop=False, skip_group_check=True)
                            opened.add(bank)
                    pe.wait_ge(u_s[d].sem, u_s[d].base + 2 * i + 2)
                    for h in range(NG):
                        last = nc.tensor.matmul(core.ps[2 + d][:, h * P:h * P + P],
                                                b["ktm"][lo:lo + CK, n, h, :], b["ue"][lo:lo + CK, d, h * P:h * P + P],
                                                start=True, stop=True)
                    if n >= 2:
                        if d == 1:
                            pe.wait_ge(du_s[0].sem, du_s[0].base + i + 1)
                        elif i >= 1:
                            pe.wait_ge(du_s[1].sem, du_s[1].base + i)
                        for h in range(NG):
                            last = nc.tensor.matmul(core.ps[6 + h // 2][:, (h % 2) * T + at:(h % 2) * T + at + CK],
                                                    u[lo:lo + CK, d, h * P:h * P + P],
                                                    b["att"][n - 2][lo:lo + CK, 4 * d + h, lo:lo + CK],
                                                    start=False, stop=(i >= 6), skip_group_check=True)
                    last.then_inc(du_s[d].sem, 1)

        @block.vector
        def _(dve):
            nc.vector.memset(s[:, :, :], 0.0).then_inc(z_s.sem, 1)
            dve.wait_ge(z_s.sem, z_s.base + 1)
            for i in range(8):
                for d in range(2):
                    n, half = chunk_tile(order[d][i])
                    lo = CK * half
                    dve.wait_ge(ks_s[d].sem, ks_s[d].base + i + 1)
                    if i >= 1:
                        dve.wait_ge(du_s[d].sem, du_s[d].base + i)
                    nc.vector.tensor_tensor(u[lo:lo + CK, d, :],
                                            b["u0"][lo:lo + CK, n, 4 * d:4 * d + 4, :].rearrange("p h t -> p (h t)"),
                                            core.ps[d][lo:lo + CK, :], ALU.subtract).then_inc(u_s[d].sem, 1)
                    dve.wait_ge(u_s[d].sem, u_s[d].base + 2 * i + 1)
                    nc.vector.tensor_tensor(b["ue"][lo:lo + CK, d, :].rearrange("p (h t) -> p h t", h=NG),
                                            u[lo:lo + CK, d, :].rearrange("p (h t) -> p h t", h=NG),
                                            b["ed"][lo:lo + CK, n, 4 * d:4 * d + 4].unsqueeze(2).broadcast_to([CK, NG, P]),
                                            ALU.mult).then_inc(u_s[d].sem, 1)
                for d in range(2):
                    dve.wait_ge(du_s[d].sem, du_s[d].base + i + 1)
                    c = order[d][i]
                    for h in range(NG):
                        last = nc.vector.scalar_tensor_tensor(s[:, 4 * d + h, :], s[:, 4 * d + h, :],
                                                              b["gl"][:, 4 * d + h, c:c + 1],
                                                              core.ps[2 + d][:, h * P:h * P + P], ALU.mult, ALU.add)
                    last.then_inc(st_s[d].sem, 1)

    z_s.advance(1)
    for d in range(2):
        for x in (ks_s[d], du_s[d], st_s[d]):
            x.advance(8)
        u_s[d].advance(16)


def gla_prepare(core, b):
    nc = core.nc
    la, bc = b["la"], b["bc"]
    lq, lk = b["lq"], b["lk"]
    d_s, a_s, p_s = core.counter("gla_dve_steps"), core.counter("gla_act_steps"), core.counter("gla_attn_ready")
    chunks = lambda x: x.rearrange("p (c t) -> p c t", t=CK)

    with core.block() as block:
        @block.vector
        def _(dve):
            step = Steps(dve, d_s)
            for i in range(4):
                d = i // 2
                src, dst = la[:, i, :], bc[:, i, :]
                if d == 1:
                    src, dst = src[:, ::-1], dst[:, ::-1]
                step(nc.vector.tensor_tensor_scan(dst, b["carry"][:, :], src, 0.0, ALU.mult, ALU.add))
            for i in range(4):
                d, t = i // 2, i % 2
                end, mid = (CK - 1, CK // 2) if d == 0 else (0, CK // 2 - 1)
                c8 = chunks(bc[:, i, :])
                c4 = chunks(bc[:, i, T:2 * T])
                step(nc.vector.tensor_tensor(chunks(b["kdT"][:, i, :]), c8[:, :, end:end + 1].broadcast_to([P, 8, CK]),
                                             c8, ALU.subtract))
                step(nc.vector.tensor_tensor(chunks(b["qr"][:, i, :]), c4,
                                             c4[:, :, mid:mid + 1].broadcast_to([P, 4, CK]), ALU.subtract))
                step(nc.vector.tensor_tensor(chunks(b["kr"][:, i, :]), c4[:, :, mid:mid + 1].broadcast_to([P, 4, CK]),
                                             c4, ALU.subtract))
            for i in range(4):
                t = i % 2
                dve.wait_ge(a_s.sem, a_s.base + 5 * (i + 1))
                step(nc.vector.tensor_tensor(b["kdT"][:, i, :], b["kdT"][:, i, :], lk[:, t, :], ALU.mult))
                step(nc.vector.tensor_tensor(b["kr"][:, i, :], b["kr"][:, i, :], lk[:, t, T:2 * T], ALU.mult))
                step(nc.vector.scalar_tensor_tensor(b["qr"][:, i, :], b["qr"][:, i, :], CK ** -0.5, lq[:, t, :],
                                                    ALU.mult, ALU.mult))
                step(nc.vector.scalar_tensor_tensor(b["qe"][:, i, :], b["qe"][:, i, :], CK ** -0.5, lq[:, t, :],
                                                    ALU.mult, ALU.mult))
            step.end()

        @block.scalar
        def _(act):
            step = Steps(act, a_s)
            act.wait_ge(d_s.sem, d_s.base + 4)
            for i in range(4):
                end = CK - 1 if i // 2 == 0 else 0
                act.wait_ge(d_s.sem, d_s.base + 4 + 3 * (i + 1))
                step(nc.scalar.activation(b["kdT"][:, i, :], b["kdT"][:, i, :], ACT.Exp))
                step(nc.scalar.activation(b["qr"][:, i, :], b["qr"][:, i, :], ACT.Exp))
                step(nc.scalar.activation(b["kr"][:, i, :], b["kr"][:, i, :], ACT.Exp))
                step(nc.scalar.activation(b["qe"][:, i, :], bc[:, i, T:2 * T], ACT.Exp))
                step(nc.scalar.activation(b["lgl"][:, i, :], chunks(bc[:, i, :])[:, :, end], ACT.Exp))
            step.end()

    turn_tiles(core, [([b["kdT"][:, i, n * P:n * P + P] for n in range(TK)],
                       b["lkd"][:, i, :, :].rearrange("p n t -> p (n t)")) for i in range(4)])

    z_s, m_s = core.counter("gla_cleared"), core.counter("gla_attn_masked")
    with core.block() as block:
        @block.tensor
        def _(pe):
            for i in range(4):
                for n in range(2):
                    for e in range(2):
                        last = nc.tensor.matmul(core.ps[2 * i + e][:, n * P:n * P + P],
                                                b["kr"][64 * e:64 * e + 64, i, n * P:n * P + P],
                                                b["qr"][64 * e:64 * e + 64, i, n * P:n * P + P], start=True, stop=True)
                last.then_inc(p_s.sem, 1)

        @block.vector
        def _(dve):
            nc.vector.memset(b["latt"][:, :, :, :], 0.0).then_inc(z_s.sem, 1)
            dve.wait_ge(z_s.sem, z_s.base + 1)
            for i in range(4):
                dve.wait_ge(p_s.sem, p_s.base + i + 1)
                for m in range(4):
                    last = nc.vector.copy_predicated(b["latt"][:, i, m, :], b["gla_mask"][:, i // 2, :].bitcast(U32),
                                                     core.ps[2 * i + m % 2][:, (m // 2) * P:(m // 2) * P + P])
                last.then_inc(m_s.sem, 1)

    p_s.advance(4), z_s.advance(1), m_s.advance(4)


def gla_scan(core, b):
    nc = core.nc
    s, lv = b["ls"], b["lv"]
    kv_s = core.counter("gla_kv_ready")
    st_s = core.counter("gla_state_ready")
    z_s, done = core.counter("gla_state_cleared"), core.counter("gla_out_ready")
    order = [[0, 1, 2, 3, 4, 5, 6, 7], [3, 2, 1, 0, 7, 6, 5, 4]]
    opened = set()

    def place(h, at, size):
        return core.ps[4 + h % 2][:, (h // 2) * T + at:(h // 2) * T + at + size]

    with core.block() as block:
        @block.tensor
        def _(pe):
            for i in range(4):
                for n in range(2):
                    for e in range(2):
                        h = 2 * (i % 2) + e
                        bank = 4 + h % 2
                        nc.tensor.matmul(place(h, n * P, P), lv[:, 2 + n, h * P:h * P + P],
                                         b["latt"][:, i, 2 * n + e, :], start=bank not in opened, stop=False,
                                         skip_group_check=True)
                        opened.add(bank)
            pe.wait_ge(z_s.sem, z_s.base + 1)
            for i in range(8):
                for d in range(2):
                    n, half = chunk_tile(order[d][i])
                    lo = CK * half
                    if i >= 1:
                        pe.wait_ge(st_s.sem, st_s.base + 2 * (i - 1) + d + 1)
                    for h in range(NG):
                        t, e = h // 2, h % 2
                        if n >= 2:
                            at = (n - 2) * P + lo
                            nc.tensor.matmul(place(h, at, CK), s[64 * e:64 * e + 64, 2 * d + t, :],
                                             b["qe"][64 * e:64 * e + 64, 2 * d + t, at:at + CK], start=False,
                                             stop=(i >= 6), skip_group_check=True)
                        last = nc.tensor.matmul(core.ps[d][64 * e:64 * e + 64, t * P:t * P + P],
                                                b["lkd"][lo:lo + CK, 2 * d + t, n, 64 * e:64 * e + 64],
                                                lv[lo:lo + CK, n, h * P:h * P + P], start=True, stop=True)
                    last.then_inc(kv_s.sem, 1)

        @block.vector
        def _(dve):
            nc.vector.memset(s[:, :, :], 0.0).then_inc(z_s.sem, 1)
            dve.wait_ge(z_s.sem, z_s.base + 1)
            for i in range(8):
                for d in range(2):
                    c = order[d][i]
                    dve.wait_ge(kv_s.sem, kv_s.base + 2 * i + d + 1)
                    for t in range(2):
                        last = nc.vector.scalar_tensor_tensor(s[:, 2 * d + t, :], s[:, 2 * d + t, :],
                                                              b["lgl"][:, 2 * d + t, c:c + 1],
                                                              core.ps[d][:, t * P:t * P + P], ALU.mult, ALU.add)
                    last.then_inc(st_s.sem, 1)

    kv_s.advance(16), st_s.advance(16), z_s.advance(1)


def ab_merge(core, src, z, gain, sq):
    nc = core.nc
    squared, summed = core.counter("merge_squared"), core.counter("merge_sums")
    act_done, steps = core.counter("merge_act_done"), core.counter("merge_dve_steps")
    with core.block() as block:
        @block.scalar
        def _(act):
            for h in range(NG):
                nc.scalar.activation(sq[:, h, :], src(h), ACT.Square).then_inc(squared.sem, 1)
            for h in range(NG):
                nc.scalar.activation(z[:, h, :], z[:, h, :], ACT.Silu).then_inc(act_done.sem, 1)
            for h in range(NG):
                act.wait_ge(summed.sem, summed.base + h // 2 + 1)
                nc.scalar.activation(sq[:, h, :], core.ps[h // 2][:, (h % 2) * T:(h % 2) * T + T], ACT.Sqrt,
                                     scale=1.0 / P, bias=core.rms_eps).then_inc(act_done.sem, 1)

        @block.tensor
        def _(pe):
            for h in range(NG):
                pe.wait_ge(squared.sem, squared.base + h + 1)
                last = nc.tensor.matmul(core.ps[h // 2][:, (h % 2) * T:(h % 2) * T + T], core.ones[:, :], sq[:, h, :],
                                        start=True, stop=True)
                if h % 2:
                    last.then_inc(summed.sem, 1)

        @block.vector
        def _(dve):
            step = Steps(dve, steps)
            for h in range(NG):
                dve.wait_ge(act_done.sem, act_done.base + NG + h + 1)
                step(nc.vector.reciprocal(sq[:, h, :], sq[:, h, :]))
                step(nc.vector.tensor_tensor(sq[:, h, :], src(h), sq[:, h, :], ALU.mult))
                step(nc.vector.scalar_tensor_tensor(z[:, h, :], sq[:, h, :], gain[:, 0:1], z[:, h, :],
                                                    ALU.mult, ALU.mult))
            step.end()

    squared.advance(NG), summed.advance(NG // 2), act_done.advance(2 * NG)


def hyena_project(core, h, b):
    nc, used = core.nc, core.used
    raw, u = b["raw"], b["u"]
    copied, padded, steps = core.counter("hy_copied"), core.counter("hy_padded"), core.counter("hy_conv_steps")
    with core.block() as block:
        @block.sync
        def _(sp):
            core.load_ahead(sp, 12)

        @block.tensor
        def _(pe):
            for c in range(12):
                w = core.chunk(pe, c)
                if c >= 8:
                    pe.wait_ge(copied.sem, copied.base + c - 7)
                linear_tiles(core, pe, w, h, [core.ps[c % 8][:, 0:T], core.ps[c % 8][:, T:2 * T]])\
                    .then_inc(used.sem, 1)

        @block.scalar
        def _(act):
            act.wait_ge(padded.sem, padded.base + 1)
            for c in range(12):
                act.wait_ge(used.sem, used.base + c + 1)
                nc.scalar.copy(raw[:, 2 * c:2 * c + 2, 1:T + 1], core.ps[c % 8][:, :].rearrange("p (a t) -> p a t", a=2))\
                    .then_inc(copied.sem, 1)

        @block.vector
        def _(dve):
            nc.vector.memset(raw[:, :, 0:1], 0.0)
            nc.vector.memset(raw[:, :, T + 1:T + 2], 0.0).then_inc(padded.sem, 1)
            dve.wait_ge(padded.sem, padded.base + 1)
            step = Steps(dve, steps)
            w = core.col("hy_conv")
            for i in range(24):
                dve.wait_ge(copied.sem, copied.base + i // 2 + 1)
                y = u[:, i, :]
                step(nc.vector.tensor_scalar(y, raw[:, i, 0:T], w[:, i:i + 1], None, ALU.mult))
                step(nc.vector.scalar_tensor_tensor(y, raw[:, i, 1:T + 1], w[:, 24 + i:25 + i], y, ALU.mult, ALU.add))
                step(nc.vector.scalar_tensor_tensor(y, raw[:, i, 2:T + 2], w[:, 48 + i:49 + i], y, ALU.mult, ALU.add))
            step.end()

    used.advance(12)
    core.taken += 12
    copied.advance(12), padded.advance(1)


def hyena_hidden(core, b):
    nc = core.nc
    MAGIC, C1 = 1.5 * 2 ** 23, 6.28125
    C2 = 2 * math.pi - C1
    p_s, d_s, a_s = core.counter("hy_mlp_ready"), core.counter("hy_mlp_dve_steps"), core.counter("hy_mlp_sine_done")
    hid, t1, t2 = b["hidden"], b["t1"], b["t2"]
    Z = b["hy_z"]
    PISAFE = 3.1415925
    with core.block() as block:
        @block.tensor
        def _(pe):
            for i in range(3):
                lhs, rhs = ((b["hy_w1"], Z), (b["hy_w2"], hid), (b["hy_w3"], hid))[i]
                if i:
                    pe.wait_ge(a_s.sem, a_s.base + i)
                nc.tensor.matmul(core.ps[0][0:64, 0:T], lhs[:, :], rhs[:, :], start=True, stop=True).then_inc(p_s.sem, 1)

        @block.vector
        def _(dve):
            step = Steps(dve, d_s)
            par = core.col("hy_mlp")
            for i in range(3):
                dve.wait_ge(p_s.sem, p_s.base + i + 1)
                step(nc.vector.tensor_scalar(t1[:, :], core.ps[0][0:64, 0:T], par[0:64, i:i + 1], par[0:64, 3:4],
                                             ALU.add, ALU.mult))
                step(nc.vector.tensor_scalar(t2[:, :], t1[:, :], 1 / (2 * math.pi), MAGIC, ALU.mult, ALU.add))
                step(nc.vector.tensor_scalar(t2[:, :], t2[:, :], -MAGIC, None, ALU.add))
                step(nc.vector.scalar_tensor_tensor(t1[:, :], t2[:, :], -C1, t1[:, :], ALU.mult, ALU.add))
                step(nc.vector.scalar_tensor_tensor(t1[:, :], t2[:, :], -C2, t1[:, :], ALU.mult, ALU.add))
                step(nc.vector.tensor_scalar(t1[:, :], t1[:, :], PISAFE, -PISAFE, ALU.min, ALU.max))
            step.end()

        @block.scalar
        def _(act):
            for i in range(3):
                act.wait_ge(d_s.sem, d_s.base + 6 * (i + 1))
                nc.scalar.activation(hid[:, :], t1[:, :], ACT.Sin).then_inc(a_s.sem, 1)

    p_s.advance(3), a_s.advance(3)


def hyena_conv(core, b, n, z, gate, skip):
    nc = core.nc
    fwd, inv = b["hy_fwd"], b["hy_inv"]
    kp, km, ks = b["kp"], b["km"], b["kspec"]
    f_s, w_s, d_s = core.counter("hy_filter_ready"), core.counter("hy_windowed"), core.counter("hy_filter_steps")
    with core.block() as block:
        jobs = [(t, half) for t in range(TT) for half in range(2)]

        @block.tensor
        def _(pe):
            for m, (t, half) in enumerate(jobs):
                for dr in range(2):
                    at = (dr * 2 + n) * D + half * 512
                    last = nc.tensor.matmul(core.ps[2 * m + dr][:, :], b["hidden"][:, t * P:t * P + P],
                                            b["hy_filt"][:, at:at + 512], start=True, stop=True)
                last.then_inc(f_s.sem, 1)

        @block.vector
        def _(dve):
            step = Steps(dve, d_s)
            for m, (t, half) in enumerate(jobs):
                dve.wait_ge(f_s.sem, f_s.base + m + 1)
                sl = slice(half * 512, half * 512 + 512)
                step(nc.vector.tensor_tensor(kp[:, t, sl], core.ps[2 * m][:, :], b["hy_win"][:, t, sl], ALU.mult))
                step(nc.vector.tensor_tensor(b["bw"][:, :], core.ps[2 * m + 1][:, :], b["hy_win"][:, t, sl], ALU.mult))
                if t == 0:
                    step(nc.vector.memset(b["bw"][0:1, :], 0.0))
                step(nc.vector.tensor_tensor(km[:, t, sl], b["bw"][:, :], kp[:, t, sl], ALU.subtract))
                step(nc.vector.tensor_tensor(kp[:, t, sl], kp[:, t, sl], b["bw"][:, :], ALU.add))
            step.end()

    f_s.advance(4)

    turn_tiles(core, [([z[:, 4 * q + c, t * P:t * P + P] for c in range(4)], b["zt"][:, t, q * 512:q * 512 + 512])
                      for t in range(TT) for q in range(2)])

    kr_s, kc_s = core.counter("hy_kspec_ready"), core.counter("hy_kspec_copied")
    zr_s, pd_s, y_s, yg_s = (core.counter(x) for x in ("hy_zspec_ready", "hy_product_done", "hy_y_ready", "hy_gated"))
    st_s = core.counter("hy_product_steps")
    with core.block() as block:
        @block.tensor
        def _(pe):
            m = 0
            for half in range(2):
                sl = slice(half * 512, half * 512 + 512)
                for f in range(2):
                    for ri, src in enumerate((kp, km)):
                        if m >= 4:
                            pe.wait_ge(kc_s.sem, kc_s.base + m - 3)
                        for t in range(TT):
                            last = nc.tensor.matmul(core.ps[m % 4][:, :], fwd[:, t, ri, f * P:f * P + P], src[:, t, sl],
                                                    start=(t == 0), stop=(t == TT - 1))
                        last.then_inc(kr_s.sem, 1)
                        m += 1
            m = 0
            for half in range(2):
                sl = slice(half * 512, half * 512 + 512)
                for f in range(2):
                    if m >= 2:
                        pe.wait_ge(pd_s.sem, pd_s.base + m - 1)
                    for ri in range(2):
                        for t in range(TT):
                            last = nc.tensor.matmul(core.ps[4 + 2 * (m % 2) + ri][:, :], fwd[:, t, ri, f * P:f * P + P],
                                                    b["zt"][:, t, sl], start=(t == 0), stop=(t == TT - 1))
                    last.then_inc(zr_s.sem, 1)
                    m += 1
            pe.wait_ge(kc_s.sem, kc_s.base + 8)
            pe.wait_ge(pd_s.sem, pd_s.base + 4)
            for j in range(DT):
                i = 0
                for f in range(2):
                    for ri in range(2):
                        last = nc.tensor.matmul(core.acc(j), b["prod"][:, f, ri, j * P:j * P + P], inv[:, f, ri, :],
                                                start=(i == 0), stop=(i == 3))
                        i += 1
                if j % 2:
                    last.then_inc(y_s.sem, 1)

        @block.scalar
        def _(act):
            m = 0
            for half in range(2):
                sl = slice(half * 512, half * 512 + 512)
                for f in range(2):
                    for ri in range(2):
                        act.wait_ge(kr_s.sem, kr_s.base + m + 1)
                        nc.scalar.copy(ks[:, f, ri, sl], core.ps[m % 4][:, :]).then_inc(kc_s.sem, 1)
                        m += 1

        @block.vector
        def _(dve):
            step = Steps(dve, st_s)
            m = 0
            for half in range(2):
                sl = slice(half * 512, half * 512 + 512)
                for f in range(2):
                    dve.wait_ge(zr_s.sem, zr_s.base + m + 1)
                    dve.wait_ge(kc_s.sem, kc_s.base + 2 * (m + 1))
                    zc, zs = core.ps[4 + 2 * (m % 2)][:, :], core.ps[5 + 2 * (m % 2)][:, :]
                    kr, ki = ks[:, f, 0, sl], ks[:, f, 1, sl]
                    pr, pi = b["prod"][:, f, 0, sl], b["prod"][:, f, 1, sl]
                    step(nc.vector.tensor_tensor(pr, zc, kr, ALU.mult))
                    step(nc.vector.tensor_tensor(b["bw"][:, :], zs, ki, ALU.mult))
                    step(nc.vector.tensor_tensor(pr, pr, b["bw"][:, :], ALU.add))
                    step(nc.vector.tensor_tensor(pi, zc, ki, ALU.mult))
                    step(nc.vector.tensor_tensor(b["bw"][:, :], zs, kr, ALU.mult))
                    nc.vector.tensor_tensor(pi, pi, b["bw"][:, :], ALU.subtract).then_inc(pd_s.sem, 1)
                    dve.wait_ge(pd_s.sem, pd_s.base + m + 1)
                    m += 1
            for j in range(DT):
                dve.wait_ge(y_s.sem, y_s.base + j // 2 + 1)
                step(nc.vector.scalar_tensor_tensor(z[:, j, :], z[:, j, :], skip[:, j:j + 1], core.acc(j),
                                                    ALU.mult, ALU.add))
                nc.vector.tensor_tensor(z[:, j, :], z[:, j, :], gate[:, j, :], ALU.mult).then_inc(yg_s.sem, 1)
            step.end()

    kr_s.advance(8), kc_s.advance(8), zr_s.advance(4), pd_s.advance(4), y_s.advance(DT // 2), yg_s.advance(DT)


COLS = [("c", DT), ("c_ctx", DT), ("c_2", DT), ("c_ctx_2", DT), ("mod_b0", 72), ("mod_b1", 72), ("mod_b2", 48),
        ("mod_b3", 48), ("ln_g", 48), ("ln_b", 48), ("norm1", 16), ("norm2", 16), ("final", 8), ("bq", 8), ("bk", 2),
        ("ab_conv", 36), ("gdn_norm_w", 1), ("gla_norm_w", 1), ("gla_gate_b", 4), ("hy_conv", 72), ("hy_skip", 16),
        ("hy_mlp", 4)]
COL_AT, NCOL = {}, 0
for _n, _w in COLS:
    COL_AT[_n] = (NCOL, _w)
    NCOL += _w


def load(core, pairs):
    done = core.counter("inputs_loaded")
    with core.block() as block:
        @block.sync
        def _(sp):
            for dst, src in pairs:
                sp.dma_start(dst, src).then_inc(done.sem, 16)
            sp.wait_ge(done.sem, done.base + 16 * len(pairs))
    done.advance(16 * len(pairs))


def program(nc, a, out):
    with ExitStack() as ctx:
        core = Core(nc, ctx, a["weights"])
        x = core.sb("x", [P, DT, T])
        cols = core.sb("cols", [P, NCOL])
        core.col = lambda name: cols[:, COL_AT[name][0]:COL_AT[name][0] + COL_AT[name][1]]
        mods = [core.sb(f"mod_{i}", [P, 72 if i < 2 else 48, 2]) for i in range(4)]
        der = core.sb("derived", [P, 160])
        consts = core.sb("consts", [P, 3, P])
        core.ident, core.ones_mean, core.ones = (consts[:, i, :] for i in range(3))
        selector = core.sb("selector", [P, 5])
        core.selector = selector[:, 0:2]
        core.ln_eps, core.rms_eps, core.q_eps = (selector[:, i:i + 1] for i in (2, 3, 4))
        core.one = consts[:, 2, 0:1]
        ARENA = 35900
        arena = core.sb("arena", [P, ARENA])
        top = [0]

        def carve(*shape, parts=P):
            n = int(np.prod(shape))
            v = arena[0:parts, top[0]:top[0] + n]
            top[0] += n
            assert top[0] <= ARENA, top[0]
            if len(shape) == 2:
                v = v.rearrange("p (a b) -> p a b", a=shape[0])
            elif len(shape) == 3:
                v = v.rearrange("p (a b c) -> p a b c", a=shape[0], b=shape[1])
            elif len(shape) == 4:
                v = v.rearrange("p (a b c d) -> p a b c d", a=shape[0], b=shape[1], c=shape[2])
            return v

        def emit(v):
            done = core.counter("output_stored")
            with core.block() as block:
                @block.sync
                def _(sp):
                    sp.dma_start(out, v[:, :, :]).then_inc(done.sem, 16)
                    sp.wait_ge(done.sem, 16)

        load(core, [(cols[:, :], a["cols"]), (consts[:, :, :], a["consts"]), (selector[:, :], a["selector"]),
                    (x[:, :, :], a["x"])])

        ready = core.counter("cpad_ready")
        dsteps = core.counter("derived_steps")

        def prepare(i0, cpad):
            with core.block() as block:
                @block.vector
                def _(dve):
                    nc.vector.memset(cpad[:, :, :], 0.0).then_inc(ready.sem, 1)

                @block.scalar
                def _(act):
                    act.wait_ge(ready.sem, ready.base + 1)
                    for i, name in enumerate((("c", "c_ctx"), ("c_2", "c_ctx_2"))[i0]):
                        nc.scalar.activation(cpad[:, :, i], core.col(name), ACT.Silu).then_inc(ready.sem, 1)
            ready.advance(3)

        def vec(i, j, s=0):
            return mods[i][:, j * DT:(j + 1) * DT, s]

        def derive(ops):
            with core.block() as block:
                @block.vector
                def _(dve):
                    step = Steps(dve, dsteps)
                    for o, i, op, other in ops:
                        if isinstance(other, float):
                            step(nc.vector.tensor_scalar(o, i, other, None, op))
                        else:
                            step(nc.vector.tensor_tensor(o, i, other, op))
                    step.end()

        D8 = lambda k: der[:, k * DT:(k + 1) * DT]

        def modulate(src, dst, scale, shift):
            m = core.counter("modulated")
            with core.block() as block:
                @block.vector
                def _(dve):
                    for j in range(DT):
                        nc.vector.tensor_scalar(dst[:, j, :], src[:, j, :], scale[:, j:j + 1], shift[:, j:j + 1],
                                                ALU.mult, ALU.add).then_inc(m.sem, 1)
            m.advance(DT)

        h = carve(DT, T)
        hc = carve(DT, T)
        base = top[0]
        cpad, partial = carve(DT, 32), carve(2, 2 * P)
        prepare(0, cpad)
        for i in range(2):
            modulation(core, cpad, core.col(f"mod_b{i}"), mods[i], 9, partial)
        prepare(1, cpad)
        for i in range(2, 4):
            modulation(core, cpad, core.col(f"mod_b{i}"), mods[i], 6, partial)
        ln = lambda i, j: (core.col("ln_g")[:, (3 * i + j) * DT:(3 * i + j + 1) * DT],
                           core.col("ln_b")[:, (3 * i + j) * DT:(3 * i + j + 1) * DT])

        def scales(i, s):
            return [(D8(0), vec(i, 1, s), ALU.add, 1.0), (D8(1), vec(i, 4, s), ALU.add, 1.0),
                    (D8(2), vec(i, 7, s), ALU.add, 1.0), (D8(3), vec(i, 2, s), ALU.mult, 0.5 / ALPHA),
                    (D8(4), vec(i, 5, s), ALU.mult, 1.0 / ALPHA), (D8(5), vec(i, 8, s), ALU.mult, 0.5 / ALPHA)]

        def work():
            top[0] = base
            return dict(hid=carve(2, 2, T), sg=carve(2, 2, T)), (carve(DT, T), carve(DT, T), carve(T))

        f, (diff, sq, rstd) = work()
        cx = carve(DT, T)
        load(core, [(cx[:, :, :], a["ctx"])])
        derive(scales(0, 1))
        modulate(cx, h, D8(0), vec(0, 0, 1))
        ffn(core, h, f["hid"], f["sg"])
        layer_norm(core, cx, D8(3), *ln(0, 0), (D8(1), vec(0, 3, 1)), hc, diff, sq, rstd)
        derive(scales(0, 0))
        modulate(x, h, D8(0), vec(0, 0))
        ffn(core, h, f["hid"], f["sg"])
        layer_norm(core, x, D8(3), *ln(0, 0), (D8(1), vec(0, 3)), h, diff, sq, rstd)
        top[0] = base
        at = dict(q=carve(DT, T), k=carve(2, 2, T), v=carve(2, TT, T), tmp=carve(2, T), sm=carve(2, 2 * T), pt=carve(2, 2 * T),
                  stat=carve(2, 8), mask=carve(TT, 2 * T), cos=carve(T), sin=carve(T), swap=carve(P), bv=carve(T),
                  sink=carve(NH))
        o = carve(DT, T)
        load(core, [(at["mask"], a["mask"]), (at["cos"], a["rope"][:, 0, :]), (at["sin"], a["rope"][:, 1, :]),
                    (at["swap"], a["swap"]), (at["bv"], a["bv"]), (at["sink"], a["sink"])])
        attention(core, h, hc, o, at)
        linear(core, o)
        f, (diff, sq, rstd) = work()
        layer_norm(core, x, D8(4), *ln(0, 1), (D8(2), vec(0, 6)), h, diff, sq, rstd)
        ffn(core, h, f["hid"], f["sg"])
        derive([(D8(6), vec(1, 1), ALU.add, 1.0)])
        layer_norm(core, x, D8(5), *ln(0, 2), (D8(6), vec(1, 0)), h, diff, sq, rstd)
        derive(scales(1, 0))
        ffn(core, h, f["hid"], f["sg"])
        layer_norm(core, x, D8(3), *ln(1, 0), (D8(1), vec(1, 3)), h, diff, sq, rstd)
        top[0] = base
        cs, uv, fo = carve(2, 3, T), carve(2, TT, 2, T), carve(DT, T)
        load(core, [(cs, a["dft"])])
        fourier(core, h, fo, cs, uv)
        linear(core, fo)
        f, (diff, sq, rstd) = work()
        layer_norm(core, x, D8(4), *ln(1, 1), (D8(2), vec(1, 6)), h, diff, sq, rstd)
        ffn(core, h, f["hid"], f["sg"])
        layer_norm(core, x, D8(5), *ln(1, 2), None, h, diff, sq, rstd)

        def gains(i, s):
            ops = []
            for m, (scale, norm) in enumerate(((1, "norm1"), (4, "norm2"))):
                n = core.col(norm)[:, (i - 2) * DT:(i - 1) * DT]
                ops += [(D8(m), vec(i, scale, s), ALU.add, 1.0), (D8(m), D8(m), ALU.mult, n)]
            return ops

        cx = carve(DT, T)
        load(core, [(cx, a["ctx_2"])])
        derive(gains(2, 1))
        rms_norm(core, cx, None, D8(0), vec(2, 0, 1), hc, sq, rstd)
        derive(gains(2, 0))
        rms_norm(core, x, None, D8(0), vec(2, 0), h, sq, rstd)

        top[0] = base
        y = carve(DT, T)
        b = dict(qkv=carve(20, T), gz=y[:, 0:NG, :], lg=y[:, NG:2 * NG, :], g=carve(TK, 8), beta=carve(TK, 8), gc=carve(2, TK, 8),
                 tri=carve(3, P), levels=carve(2, 6, P), masks=carve(2, 2, P), gla_mask=carve(2, P))
        mid = top[0]
        b |= dict(lq=carve(2, T), lk=carve(2, 2 * T), lv=carve(TK, 512), la=carve(4, 2 * T), carry=carve(2 * T))
        late = top[0]
        b |= dict(raw=carve(20, T + 2))
        load(core, [(b["tri"], a["tri"]), (b["levels"], a["levels"]), (b["masks"], a["masks"]),
                    (b["gla_mask"], a["gla_mask"]), (b["carry"], a["carry"])])
        ab_project(core, h, hc, b)
        top[0] = late
        b |= dict(t1=carve(TK, 8), t2=carve(TK, 8), lt=carve(4, 2 * T), ea=carve(8), a_log=carve(8), dt_bias=carve(8),
                  w_small=carve(DT, 48), llr=carve(2 * T, parts=32), w_gate=carve(2, T, parts=32), g_steps=6, la_steps=18)
        cleared = core.counter("gate_weights_cleared")
        with core.block() as block:
            @block.vector
            def _(dve):
                nc.vector.memset(b["w_gate"], 0.0).then_inc(cleared.sem, 1)
        cleared.advance(1)
        load(core, [(b["a_log"], a["a_log"]), (b["dt_bias"], a["dt_bias"]), (b["w_small"], a["w_small"]),
                    (b["w_gate"][0:16, 0, :], a["w_gate"][0]), (b["w_gate"][16:32, 1, :], a["w_gate"][1])])
        ab_gates(core, h, hc, b)
        top[0] = 0
        b |= dict(lkd=carve(4, TK, P), lgl=carve(4, 8), ls=carve(4, P))
        assert top[0] <= base
        top[0] = late
        b |= dict(bc=carve(4, 2 * T), kdT=carve(4, 2 * T), qr=carve(4, T), kr=carve(4, T), qe=carve(4, T),
                  latt=carve(4, 4, P))
        gla_prepare(core, b)
        gla_scan(core, b)
        msq = b["qr"]
        ab_merge(core, lambda h: core.ps[4 + h % 2][:, (h // 2) * T:(h // 2) * T + T], b["lg"], core.col("gla_norm_w"), msq)
        top[0] = mid
        b |= dict(sq12=carve(12, T))
        l2_norm(core, b)
        top[0] = 0
        b |= dict(rows=carve(8, P), dd=carve(2, NG, P))
        b |= dict(s=carve(8, P), bg=carve(TK, 8), ed=carve(TK, 8), ngc=carve(TK, 8), gl=carve(8, 8))
        assert top[0] <= base
        top[0] = mid
        b |= dict(ktm=carve(TK, NG, P), vtm=carve(TK, NG, P), qd=carve(8, T), kbe=carve(8, P), vb=carve(8, P),
                  l=carve(2, 512), u0=carve(TK, 8, P), kcdT=carve(TK, 8, P), x=carve(2, 512), w=carve(2, 512),
                  o=carve(2, 512), pm=carve(2, 512))
        b["u"], b["ue"] = b["x"], b["w"]
        qkv = b["qkv"]
        b["att"] = [qkv[:, i:i + 4, :].rearrange("p a (b t) -> p (a b) t", t=P) for i in (4, 16)]
        place = lambda i, n: qkv[:, (0 if n < TT else 12) + i, (n % TT) * P:(n % TT) * P + P]
        turn_tiles(core, [([place(h_ + 4 * m, n) for h_ in range(NG)],
                           b["vtm" if m else "ktm"][:, n, :, :].rearrange("p h t -> p (h t)"))
                          for n in range(TK) for m in range(2)])
        gdn_factors(core, b)
        for n in range(TK):
            gdn_tile(core, b, n)
            gdn_solve(core, b, n)
        gdn_scan(core, b)
        top[0] = mid
        msq = carve(NG, T)
        ab_merge(core, lambda h: core.ps[6 + h // 2][:, (h % 2) * T:(h % 2) * T + T], b["gz"], core.col("gdn_norm_w"), msq)
        linear(core, y)
        top[0] = 0
        h = carve(DT, T)
        top[0] = base
        f, (diff, sq, rstd) = work()
        rms_norm(core, x, vec(2, 2), D8(1), vec(2, 3), h, sq, rstd)
        ffn(core, h, f["hid"], f["sg"])
        derive(gains(3, 0))
        rms_norm(core, x, vec(2, 5), D8(0), vec(3, 0), h, sq, rstd)
        top[0] = DT * T
        b = dict(u=carve(24, T))
        mid = top[0]
        b |= dict(raw=carve(24, T + 2))
        hyena_project(core, h, b)
        top[0] = 0
        b |= dict(zt=carve(TT, D))
        top[0] = mid
        b |= dict(hy_filt=carve(2 * 2 * D, parts=64), hidden=carve(T, parts=64), t1=carve(T, parts=64), t2=carve(T, parts=64),
                  hy_z=carve(T, parts=33), hy_w1=carve(64, parts=33), hy_w2=carve(64, parts=64), hy_w3=carve(64, parts=64),
                  hy_fwd=carve(TT, 2, T), hy_inv=carve(2, 2, T), hy_win=carve(TT, D), kp=carve(TT, D), km=carve(TT, D),
                  kspec=carve(2, 2, D), prod=carve(2, 2, D), bw=carve(512))
        load(core, [(b[n], a[n]) for n in ("hy_filt", "hy_z", "hy_w1", "hy_w2", "hy_w3", "hy_fwd", "hy_inv", "hy_win")])
        hyena_hidden(core, b)
        z = b["u"][:, 0:DT, :]
        for n in range(2):
            hyena_conv(core, b, n, z, b["u"][:, (n + 1) * DT:(n + 2) * DT, :],
                       core.col("hy_skip")[:, n * DT:(n + 1) * DT])
        linear(core, z)
        top[0] = 0
        h = carve(DT, T)
        f, (diff, sq, rstd) = work()
        rms_norm(core, x, vec(3, 2), D8(1), vec(3, 3), h, sq, rstd)
        ffn(core, h, f["hid"], f["sg"])
        rms_norm(core, x, vec(3, 5), core.col("final"), None, h, sq, rstd)
        emit(h)


def _features(v):
    v = np.asarray(v)
    return np.ascontiguousarray(v.reshape(-1, P).T)


def _tiles(m):
    return np.ascontiguousarray(m.reshape(-1, P, m.shape[1]).transpose(1, 0, 2))


def _chunks(m):
    return m.reshape(DT, P, -1, 256).transpose(2, 1, 0, 3).reshape(-1, P, CH)


def _ffn_chunks(wa, wg, wo):
    ag = np.stack([wa.reshape(DT, P, FFT, P), wg.reshape(DT, P, FFT, P)], 3).transpose(2, 1, 0, 3, 4).reshape(FFT, P, CH)
    down = wo.reshape(PAIRS, 2, P, D).transpose(0, 2, 1, 3).reshape(PAIRS, P, CH)
    order = [ag[0], ag[1], ag[2], ag[3], down[0]]
    for p in range(2, PAIRS):
        order += [ag[2 * p], ag[2 * p + 1], down[p - 1]]
    return np.stack(order + [down[PAIRS - 1]])


def layout(i):
    f32 = np.float32
    heads = [8 * (t // 4) + 4 * e + t % 4 for t in range(DT) for e in range(2)]
    perm = np.concatenate([np.arange(h * HD, h * HD + HD) for h in heads])
    wqkv, bqkv = i["attn_wqkv"][0], i["attn_bqkv"][0]
    ab = i["ab_w_in_2"][0]
    sizes = [512, 512, 512, 512, 8, 8, 256, 256, 512, 512, 32]
    at = np.concatenate([[0], np.cumsum(sizes)])
    part = {n: ab[:, at[k]:at[k + 1]] for k, n in
            enumerate(("gq", "gk", "gv", "gz", "ga", "gb", "lq", "lk", "lv", "lg", "llr"))}
    ff = lambda l, j: _ffn_chunks(i["ffn_wi"][l, j][:, :FF], i["ffn_wi"][l, j][:, FF:], i["ffn_wo"][l, j])
    ff2 = lambda l: _ffn_chunks(i["ffn_w3_2"][l], i["ffn_w1_2"][l], i["ffn_w2_2"][l])
    f00 = ff(0, 0)
    stream = [_chunks(i["mod_w"][0]), _chunks(i["mod_w"][1]), _chunks(i["mod_w_2"][0]), _chunks(i["mod_w_2"][1]),
              f00, f00, _chunks(wqkv[:, :1024][:, perm]), _chunks(wqkv[:, 1024:]), _chunks(i["attn_wo"][0][perm]), ff(0, 1),
              ff(1, 0), _chunks(i["fourier_wo"][0]), ff(1, 1)]
    stream += [_chunks(part[n]) for n in ("gk", "gv", "gq", "gz", "lq", "lk", "lv", "lg")]
    stream += [_chunks(i["ab_w_out_2"][0]), ff2(0), _chunks(i["hy_w_in_2"][0]), _chunks(i["hy_w_out_2"][0]), ff2(1)]
    a = {"weights": np.concatenate(stream)}

    mlp = np.zeros((P, 4), f32)
    for k, n in enumerate(("hy_pos_b1_2", "hy_pos_b2_2", "hy_pos_b3_2", "hy_freq_2")):
        mlp[:64, k] = i[n][0]
    cols = {"c": i["c"], "c_ctx": i["c_ctx"], "c_2": i["c_2"], "c_ctx_2": i["c_ctx_2"], "mod_b0": i["mod_b"][0],
            "mod_b1": i["mod_b"][1], "mod_b2": i["mod_b_2"][0], "mod_b3": i["mod_b_2"][1], "ln_g": i["ln_g"],
            "ln_b": i["ln_b"], "norm1": i["norm1_w_2"], "norm2": i["norm2_w_2"], "final": i["final_norm_w_2"],
            "bq": bqkv[:1024][perm], "bk": bqkv[1024:1280], "ab_conv": i["ab_conv_w_2"][0],
            "gdn_norm_w": i["gdn_norm_w_2"], "gla_norm_w": i["gla_norm_w_2"], "gla_gate_b": i["gla_gate_b_2"][0],
            "hy_conv": i["hy_conv_w_2"][0], "hy_skip": i["hy_skip_2"][0]}
    a["cols"] = np.concatenate([mlp if n == "hy_mlp" else _features(cols[n]) for n, _ in COLS], 1)
    assert a["cols"].shape == (P, NCOL)
    for n, src in (("x", i["x"][0]), ("ctx", i["ctx"][0]), ("ctx_2", i["ctx_2"][0])):
        a[n] = _tiles(src.T)
    a["consts"] = np.ascontiguousarray(np.stack([np.eye(P), np.full((P, P), 1 / D), np.ones((P, P))], 1).astype(f32))
    sel = np.zeros((P, 5), f32)
    sel[:, 2:] = LN_EPS / ALPHA ** 2, RMS_EPS, P * RMS_EPS
    for g in range(4):
        sel[32 * g, 0] = sel[32 * g + 1, 1] = 1
    a["selector"] = sel

    qpos, kpos = np.arange(T)[:, None], np.arange(T)[None, :]
    mask = np.zeros((T, 2 * T), f32)
    mask[:, :T] = np.where(np.abs(qpos - kpos) <= 128, 0, NEG)
    a["mask"] = _tiles(mask)
    inv = 10000.0 ** (-np.arange(0, 32, 2) / 32)
    pos = np.arange(T)
    ang = np.concatenate([(pos // 64)[:, None] * inv, (pos % 64)[:, None] * inv], -1)
    rope = np.zeros((P, 2, T), f32)
    swap = np.zeros((P, P), f32)
    for p in range(P):
        d = p % HD
        axis, second, j = d // 32, (d % 32) // 16, d % 16
        rope[p, 0] = np.cos(ang[:, axis * 16 + j])
        rope[p, 1] = np.sin(ang[:, axis * 16 + j])
        swap[p + (-16 if second else 16), p] = 1 if second else -1
    a["rope"], a["swap"] = rope, swap
    a["bv"] = np.ascontiguousarray(np.broadcast_to(bqkv[1280:], (P, 256)))
    a["sink"] = np.ascontiguousarray(np.broadcast_to(i["attn_sink"][0], (P, NH)))

    ph = 2 * np.pi * np.outer(np.arange(256), np.arange(256)) / 256
    a["dft"] = np.ascontiguousarray((np.stack([np.cos(ph), np.sin(ph), -np.sin(ph)], 1) / 16).astype(f32)
                                    .reshape(2, P, 3, 256).transpose(1, 0, 2, 3))

    r, c = np.arange(P)[:, None], np.arange(P)[None, :]
    same = r // CK == c // CK
    a["tri"] = np.ascontiguousarray(np.stack([same & (r <= c), same & (r >= c), same], 1).astype(f32))
    a["masks"] = np.ascontiguousarray(np.stack([
        np.stack([np.where(same & (c < r), 0, NEG), np.where(same & (r <= c), 0, NEG)], 1),
        np.stack([np.where(same & (c > r), 0, NEG), np.where(same & (r >= c), 0, NEG)], 1)], 1).astype(f32))
    a["gla_mask"] = np.ascontiguousarray(np.stack([same & (r <= c), same & (r >= c)], 1).astype(f32))
    lv = np.zeros((P, 2, 6, P), f32)
    for l in range(6):
        s = 2 ** l
        block = (r // (2 * s) == c // (2 * s)) & (r // s != c // s)
        lv[:, 0, l], lv[:, 1, l] = block & (c < r), block & (c > r)
    a["levels"] = lv
    a["carry"] = np.ascontiguousarray(np.broadcast_to((np.arange(2 * T) % CK != 0).astype(f32), (P, 2 * T)))
    a["a_log"] = np.ascontiguousarray(np.broadcast_to(i["gdn_a_log_2"].reshape(-1), (P, 8)))
    a["dt_bias"] = np.ascontiguousarray(np.broadcast_to(i["gdn_dt_bias_2"].reshape(-1), (P, 8)))
    a["w_small"] = _tiles(np.concatenate([part["ga"], part["gb"], part["llr"]], 1))
    a["w_gate"] = i["gla_gate_w_2"][0]

    t = np.linspace(0, 1, T, dtype=f32)[:, None]
    w = (f32(2 * math.pi / T) * np.arange(T, dtype=f32))[:, None]
    fr = np.linspace(1e-4, 15, 16, dtype=f32)[None, :]
    a["hy_z"] = np.ascontiguousarray(np.concatenate([t, np.cos(fr * w), -np.sin(fr * w)], -1).T.astype(f32))
    deltas = np.abs(np.linspace(math.log(1e-2) / 1.5, math.log(1e-2) / 0.3, D, dtype=f32))
    a["hy_win"] = _tiles((np.exp(-t * deltas) + f32(0.05)).astype(f32))
    th = (2 * np.arange(256) + 1)[None, :] * np.arange(T)[:, None] * (np.pi / 512)
    a["hy_fwd"] = np.ascontiguousarray(np.stack([np.cos(th), np.sin(th)], 1).astype(f32).reshape(2, P, 2, 256)
                                       .transpose(1, 0, 2, 3))
    a["hy_inv"] = np.ascontiguousarray((np.stack([np.cos(th.T), -np.sin(th.T)], 1) / 256).astype(f32)
                                       .reshape(2, P, 2, T).transpose(1, 0, 2, 3))
    a["hy_filt"] = i["hy_filt_out_2"][0]
    for k in range(1, 4):
        a[f"hy_w{k}"] = i[f"hy_pos_w{k}_2"][0]
    return {n: np.ascontiguousarray(v) for n, v in a.items()}


def kernel(**inputs):
    import concourse.bacc as bacc
    from concourse.bass_utils import run_bass_kernel_spmd

    arrays = layout({n: np.asarray(v) for n, v in inputs.items()})
    nc = bacc.Bacc("TRN2", target_bir_lowering=False, num_devices=1)
    views = {n: nc.dram_tensor(f"in_{n}", v.shape, mybir.dt.from_np(v.dtype), kind="ExternalInput").ap()
             for n, v in arrays.items()}
    out = nc.dram_tensor("out", (P, DT, T), F32, kind="ExternalOutput").ap()
    program(nc, views, out)
    r = run_bass_kernel_spmd(nc, [{f"in_{n}": v for n, v in arrays.items()}], core_ids=[0])
    y = r.results[0]["out"]
    return np.ascontiguousarray(y.transpose(2, 1, 0).reshape(1, T, D))
```

```python
import math

import numpy as np

import concourse.bass as bass
from concourse import mybir
from contextlib import ExitStack, contextmanager

F32 = mybir.dt.float32
F32R = mybir.dt.float32r
U32 = mybir.dt.uint32
ALU = mybir.AluOpType
ACT = mybir.ActivationFunctionType
AX = mybir.AxisListType

P = 128
D = 1024
DT = D // P
T = 256
TT = T // P
FF = 2816
FFT = FF // P
PAIRS = FFT // 2
CH = 2048
NSLOT = 6
NH, NKV, HD = 16, 4, 64
LN_EPS, RMS_EPS = 1e-5, 1e-6
ALPHA = 4.0 ** 0.25
NEG = -1e30
CK = 64


class Counter:

    def __init__(self, sem):
        self.sem, self.base, self.pending = sem, 0, 0

    def advance(self, n):
        self.base += n


class Steps:

    def __init__(self, eng, counter):
        self.eng, self.counter, self.n = eng, counter, 0

    def __call__(self, instruction):
        self.n += 1
        instruction.then_inc(self.counter.sem, 1)
        self.eng.wait_ge(self.counter.sem, self.counter.base + self.n)

    def end(self):
        self.counter.pending += self.n


class Core:

    def __init__(self, nc, ctx, weights, plan):
        self.nc, self.ctx, self.weights = nc, ctx, weights
        self.counters = {}
        self.plan = plan
        self.at = 0
        self.taken = 0
        self.last_in = [None] * NSLOT
        self.loads = [0] * NSLOT
        self.first_load = [0] * NSLOT
        self.wbuf = self.sb("weight_ring", [P, NSLOT, CH])
        self.loaded = [self.counter(f"weights_loaded_{s}") for s in range(NSLOT)]
        self.used = self.counter("weights_used")
        self.ps = [ctx.enter_context(nc.psum_tensor(f"bank{b}", [P, 512], F32)) for b in range(8)]

    def sb(self, name, shape, dt=F32):
        return self.ctx.enter_context(self.nc.sbuf_tensor(name, shape, dt))

    def counter(self, name):
        if name not in self.counters:
            self.counters[name] = Counter(self.ctx.enter_context(self.nc.semaphore(name)))
        return self.counters[name]

    @contextmanager
    def block(self):
        with self.nc.Block() as block:
            yield block
        for s in self.counters.values():
            s.base, s.pending = s.base + s.pending, 0

    def acc(self, j):
        return self.ps[j // 2][:, (j % 2) * T:(j % 2) * T + T]

    def load(self, sp, i, slot):
        if self.last_in[slot] is not None:
            sp.wait_ge(self.used.sem, self.last_in[slot] + 1)
        sp.dma_start(self.wbuf[:, slot, :], self.weights[i, :, :]).then_inc(self.loaded[slot].sem, 16)
        self.last_in[slot] = i
        self.loads[slot] += 1

    def load_first(self, sp, stage, first):
        n, ring = self.plan[stage]
        for l in range(min(n, ring)):
            self.load(sp, first + l, l)

    def load_ahead(self, sp):
        n, ring = self.plan[self.at]
        self.first_load = [self.loads[s] - (1 if s < min(n, ring) else 0) for s in range(NSLOT)]
        l = ring
        rounds = (n - ring) // ring
        if rounds >= 3:
            with sp.Fori(0, rounds) as r:
                for s in range(ring):
                    sp.wait_ge(self.used.sem, r * ring + (self.taken + s + 1))
                    sp.dma_start(self.wbuf[:, s, :], self.weights[r * ring + (self.taken + ring + s), :, :])\
                        .then_inc(self.loaded[s].sem, 16)
            for s in range(ring):
                self.last_in[s] = self.taken + rounds * ring + s
                self.loads[s] += rounds
            l += rounds * ring
        while l < n:
            self.load(sp, self.taken + l, l % ring)
            l += 1
        if self.at + 1 < len(self.plan):
            self.load_first(sp, self.at + 1, self.taken + n)

    def chunk(self, eng, l, r=0, rounds=0):
        ring = self.plan[self.at][1]
        s = l % ring
        eng.wait_ge(self.loaded[s].sem, r * (16 * rounds) + 16 * (self.first_load[s] + l // ring + 1))
        return self.wbuf[:, s, :]

    def stage_done(self):
        n = self.plan[self.at][0]
        self.used.advance(n)
        self.taken += n
        self.at += 1


def ffn(core, h, f, m=0):
    nc, used = core.nc, core.used
    wsplit, hs, hids, sg, tmp, side = f["wsplit"], f["hs"], f["hids"], f["sg"], f["tmp"], f["side"]
    split_hi, multiplied = core.counter("ffn_weights_hi"), core.counter("ffn_multiplied")
    h_hi, h_split = core.counter("ffn_h_hi"), core.counter("ffn_h_split")
    silu_ready, gated = core.counter("ffn_silu_ready"), core.counter("ffn_gated")
    hid_hi, hid_ready = core.counter("ffn_hidden_hi"), core.counter("ffn_hidden_ready")
    side_steps = core.counter("ffn_side_steps")
    rounds = (PAIRS - 3) // 2
    S = 3
    body = 6 + 2 * m
    rings = body // core.plan[core.at][1]
    mbase = multiplied.base
    place_pe = lambda q: 5 + q + (m if q < 3 else 2 * m)
    place_dve = lambda q: 8 + 2 * m + q + (m if q >= 3 else 0)

    with core.block() as block:
        @block.sync
        def _(sp):
            core.load_ahead(sp)

        @block.tensor
        def _(pe):
            def up(p, par, c, place, r=0, first=False):
                for t in range(2):
                    pe.wait_ge(used.sem, r * body + (used.base + place[t] + 1))
                    if not first:
                        pe.wait_ge(gated.sem, p * 2 + (gated.base + t - 3))
                    w, bank = wsplit[:, (c + t) % S, :, :], core.ps[4 + 2 * par + t]
                    for half in range(2):
                        for k in range(DT):
                            if first and p == 0 and t == 0 and half == 0:
                                pe.wait_ge(h_split.sem, h_split.base + k + 1)
                            at = slice(k * 2 * P + half * P, k * 2 * P + half * P + P)
                            for x, y in ((0, 0), (0, 1), (1, 0)):
                                last = nc.tensor.matmul(bank[:, half * T:half * T + T], w[:, x, at], hs[:, y, k, :],
                                                        start=(k == 0 and x + y == 0), stop=(k == DT - 1 and x == 1))
                    last.then_inc(multiplied.sem, 1)

            def down(p, par, c, place, r=0, first=False, final=False):
                pe.wait_ge(used.sem, r * body + (used.base + place + 1))
                w = wsplit[:, c % S, :, :]
                for t in range(2):
                    pe.wait_ge(hid_ready.sem, p * 2 + (hid_ready.base + t + 1))
                    for j in range(DT):
                        at = slice(t * D + j * P, t * D + j * P + P)
                        for x, y in ((0, 0), (0, 1), (1, 0)):
                            last = nc.tensor.matmul(core.acc(j), w[:, x, at], hids[:, par, t, y, :],
                                                    start=(first and t == 0 and j % 2 == 0 and x + y == 0),
                                                    stop=(final and t == 1 and x == 1), skip_group_check=True)
                last.then_inc(multiplied.sem, 1)

            at = place_pe
            up(0, 0, 0, (0, 1), first=True)
            up(1, 1, 2, (2, 3), first=True)
            down(0, 0, 4, 4, first=True)
            with pe.Fori(0, rounds) as r:
                up(r * 2 + 2, 0, 5, (at(0), at(1)), r)
                down(r * 2 + 1, 1, 7, at(2), r)
                up(r * 2 + 3, 1, 8, (at(3), at(4)), r)
                down(r * 2 + 2, 0, 10, at(5), r)
            R = rounds * body
            up(PAIRS - 1, 0, 29, (R + at(0), R + at(1)))
            down(PAIRS - 2, 1, 31, R + at(2))
            down(PAIRS - 1, 0, 32, R + at(3), final=True)

        @block.scalar
        def _(act):
            for k in range(DT):
                nc.scalar.copy(hs[:, 0, k, :], h[:, k, :]).then_inc(h_hi.sem, 1)

            def hi(c, place, r=0, first=False):
                raw = core.chunk(act, place, r, rings)
                if not first:
                    act.wait_ge(multiplied.sem, r * 6 + (mbase + c - 2))
                nc.scalar.copy(wsplit[:, c % S, 0, :], raw).then_inc(split_hi.sem, 1)

            def silu(p, at, par, t, first=False):
                act.wait_ge(multiplied.sem, at)
                if not first:
                    act.wait_ge(gated.sem, p * 2 + (gated.base + t - 3))
                nc.scalar.activation(sg[:, par, t, :], core.ps[4 + 2 * par + t][:, T:2 * T],
                                     ACT.Silu).then_inc(silu_ready.sem, 1)

            for c in range(3):
                hi(c, c, first=True)
            for c in range(4):
                silu(c // 2, mbase + c + 1, c // 2, c % 2, True)
                hi(c + 3, c + 3 + (m if c >= 2 else 0))
            hi(7, 7 + m)
            with act.Fori(0, rounds) as r:
                for q in range(6):
                    if q not in (2, 5):
                        silu(r * 2 + (2 + q // 3), r * 6 + (mbase + 6 + q), q // 3, q % 3)
                    hi(8 + q, place_dve(q), r)
            silu(PAIRS - 1, mbase + 30, 0, 0)
            hi(32, rounds * body + place_dve(0))
            silu(PAIRS - 1, mbase + 31, 0, 1)

        @block.vector
        def _(dve):
            for k in range(DT):
                dve.wait_ge(h_hi.sem, h_hi.base + k + 1)
                nc.vector.tensor_tensor(hs[:, 1, k, :], h[:, k, :], hs[:, 0, k, :].bitcast(F32), ALU.subtract)\
                    .then_inc(h_split.sem, 1)

            def lo(c, place, r=0):
                dve.wait_ge(split_hi.sem, r * 6 + (split_hi.base + c + 1))
                ring = core.plan[core.at][1]
                nc.vector.tensor_tensor(wsplit[:, c % S, 1, :], core.wbuf[:, place % ring, :],
                                        wsplit[:, c % S, 0, :].bitcast(F32), ALU.subtract).then_inc(used.sem, 1)

            def gate(p, par, t, freed=None):
                n = p * 2 + (t + 1)
                dve.wait_ge(silu_ready.sem, n + silu_ready.base)
                nc.vector.tensor_tensor(tmp[:, t, :], core.ps[4 + 2 * par + t][:, 0:T], sg[:, par, t, :], ALU.mult)\
                    .then_inc(gated.sem, 1)
                dve.wait_ge(gated.sem, n + gated.base)
                if freed is not None:
                    dve.wait_ge(multiplied.sem, freed)
                nc.vector.tensor_copy(hids[:, par, t, 0, :], tmp[:, t, :]).then_inc(hid_hi.sem, 1)
                dve.wait_ge(hid_hi.sem, n + hid_hi.base)
                nc.vector.tensor_tensor(hids[:, par, t, 1, :], tmp[:, t, :], hids[:, par, t, 0, :].bitcast(F32),
                                        ALU.subtract).then_inc(hid_ready.sem, 1)

            def modulation_products(n, place, r=0):
                raws = [core.chunk(dve, place + i, r, rings) for i in range(m)]
                for k in range(DT):
                    for i in range(m):
                        step = n * (DT - 1) + (side_steps.base + k * m + i + 1)
                        c = f["silu"][:, k:k + 1]
                        out, x = side[:, n + i, :], raws[i][:, k * 2 * P:(k + 1) * 2 * P]
                        if k == 0:
                            last = nc.vector.tensor_scalar(out, x, c, None, ALU.mult)
                        else:
                            dve.wait_ge(side_steps.sem, step - m)
                            last = nc.vector.scalar_tensor_tensor(out, x, c, out, ALU.mult, ALU.add)
                        last.then_inc(side_steps.sem if k < DT - 1 else used.sem, 1)

            for c in range(3):
                lo(c, c)
            for c in range(4):
                gate(c // 2, c // 2, c % 2)
                lo(c + 3, c + 3 + (m if c >= 2 else 0))
                if c == 1:
                    modulation_products(0, 5)
            lo(7, 7 + m)
            modulation_products(m, 8 + m)
            with dve.Fori(0, rounds) as r:
                for q in range(6):
                    if q not in (2, 5):
                        p = 2 + q // 3
                        gate(r * 2 + p, q // 3, q % 3, r * 6 + (mbase + 3 * p - 1))
                    lo(8 + q, place_dve(q), r)
                    if q in (2, 5):
                        modulation_products(r * (2 * m) + (2 * m + (m if q == 5 else 0)), place_dve(q) + 1, r)
            gate(PAIRS - 1, 0, 0, mbase + 3 * (PAIRS - 1) - 1)
            lo(32, rounds * body + place_dve(0))
            gate(PAIRS - 1, 0, 1, mbase + 3 * (PAIRS - 1) - 1)
            modulation_products(10 * m, rounds * body + place_dve(0) + 1)

    split_hi.advance(3 * PAIRS), multiplied.advance(3 * PAIRS)
    h_hi.advance(DT), h_split.advance(DT)
    for x in (silu_ready, gated, hid_hi, hid_ready):
        x.advance(2 * PAIRS)
    side_steps.advance(PAIRS * m * (DT - 1))
    core.stage_done()


def side_columns(core, side, jobs, rows):
    nc = core.nc
    summed, copied = core.counter("side_summed"), core.counter("side_rows_copied")
    turned, added = core.counter("side_turned"), core.counter("side_added")
    G = -(-len(jobs) // 4)
    with core.block() as block:
        @block.tensor
        def _(pe):
            for r in range(G):
                for g in range(4):
                    n = min(G * g + r, len(jobs) - 1)
                    last = nc.tensor.matmul(core.ps[7][32 * g:32 * g + 32, 0:2 * P], core.unit_row(r), side[:, n, :],
                                            start=(r == 0), stop=(r == G - 1), tile_position=(0, 32 * g))
            last.then_inc(summed.sem, 1)
            pe.wait_ge(copied.sem, copied.base + 1)
            for t in range(2):
                last = nc.tensor.transpose(core.ps[6][:, t * P:t * P + P], rows[:, t * P:t * P + P], core.ident[:, :])
            last.then_inc(turned.sem, 1)

        @block.scalar
        def _(act):
            act.wait_ge(summed.sem, summed.base + 1)
            nc.scalar.copy(rows, core.ps[7][:, 0:2 * P]).then_inc(copied.sem, 1)

        @block.vector
        def _(dve):
            dve.wait_ge(turned.sem, turned.base + 1)
            n = 0
            while n < len(jobs):
                mod, bias, tile = jobs[n]
                end = n
                while end < min(len(jobs), G * (n // G + 1)) and jobs[end][0] is mod and jobs[end][2] == tile + 2 * (end - n):
                    end += 1
                w, at = end - n, 32 * (n // G) + n % G
                pairs = lambda v: v[:, tile:tile + 2 * w].rearrange("p (n t) -> p n t", t=2)
                nc.vector.tensor_tensor(pairs(mod[:, :, 0]), core.ps[6][:, 0:2 * P].rearrange("p (t c) -> p c t", t=2)
                                        [:, at:at + w, :], pairs(bias), ALU.add).then_inc(added.sem, 1)
                added.pending += 1
                n = end

    summed.advance(1), copied.advance(1), turned.advance(1)


def linear_tiles(core, pe, w, h, outs):
    for j, out in enumerate(outs):
        for k in range(DT):
            last = core.nc.tensor.matmul(out, w[:, k * 2 * P + j * P:k * 2 * P + j * P + P], h[:, k, :],
                                         start=(k == 0), stop=(k == DT - 1))
    return last


def linear(core, h, name="linear"):
    nc, used = core.nc, core.used
    with core.block() as block:
        @block.sync
        def _(sp):
            core.load_ahead(sp)

        @block.tensor
        def _(pe):
            for c in range(4):
                w = core.chunk(pe, c)
                linear_tiles(core, pe, w, h, [core.acc(2 * c), core.acc(2 * c + 1)]).then_inc(used.sem, 1)

    core.stage_done()


def modulation(core, cpad, bias, mod, first, nch, partial):
    nc, used = core.nc, core.used
    parts_ready, turned = core.counter("mod_partial_copied"), core.counter("mod_turned")
    finished = core.counter("mod_finished")

    with core.block() as block:
        @block.sync
        def _(sp):
            core.load_ahead(sp)

        @block.tensor
        def _(pe):
            def turn(n):
                pe.wait_ge(parts_ready.sem, parts_ready.base + n + 1)
                for t in range(2):
                    m = 2 * n + t
                    last = nc.tensor.matmul(core.ps[7][:, 2 * m:2 * m + 2], partial[:, n % 2, t * P:t * P + P],
                                            core.selector[:, :], start=True, stop=True)
                last.then_inc(turned.sem, 1)

            for n in range(nch):
                w = core.chunk(pe, n)
                if n >= 2:
                    pe.wait_ge(parts_ready.sem, parts_ready.base + n - 1)
                for k in range(DT):
                    g = k % 4
                    last = nc.tensor.matmul(core.ps[4 + n % 2][32 * g:32 * g + 32, 0:2 * P], cpad[:, k, :],
                                            w[:, k * 2 * P:(k + 1) * 2 * P], start=(k < 4), stop=(k >= 4),
                                            tile_position=(0, 32 * g))
                last.then_inc(used.sem, 1)
                if n >= 1:
                    turn(n - 1)
            turn(nch - 1)

        @block.scalar
        def _(act):
            for n in range(nch):
                act.wait_ge(used.sem, used.base + n + 1)
                if n >= 2:
                    act.wait_ge(turned.sem, turned.base + n - 1)
                nc.scalar.copy(partial[:, n % 2, :], core.ps[4 + n % 2][:, 0:2 * P]).then_inc(parts_ready.sem, 1)

        @block.vector
        def _(dve):
            dve.wait_ge(turned.sem, turned.base + nch)
            at = slice(2 * first, 2 * (first + nch))
            nc.vector.tensor_tensor(mod[:, at, :], core.ps[7][:, 0:4 * nch].rearrange("p (m i) -> p m i", i=2),
                                    bias[:, at].unsqueeze(2).broadcast_to([P, 2 * nch, 2]),
                                    ALU.add).then_inc(finished.sem, 1)

    parts_ready.advance(nch), turned.advance(nch), finished.advance(1)
    core.stage_done()


def layer_norm(core, x, gate, g, b, y_modulation, h, diff, sq, rstd):
    nc = core.nc
    mixed, mean_done, diff_done = core.counter("ln_mixed"), core.counter("ln_mean_done"), core.counter("ln_diff_done")
    sq_done, var_done, rstd_done = core.counter("ln_sq_done"), core.counter("ln_var_done"), core.counter("ln_rstd_done")
    unit_done, x_done, h_done = core.counter("ln_unit_done"), core.counter("ln_x_done"), core.counter("ln_h_done")
    mean, var = core.ps[4][:, 0:T], core.ps[5][:, 0:T]

    with core.block() as block:
        @block.tensor
        def _(pe):
            for j in range(DT):
                pe.wait_ge(mixed.sem, mixed.base + j + 1)
                last = nc.tensor.matmul(mean, core.ones_mean[:, :], x[:, j, :], start=(j == 0), stop=(j == DT - 1))
            last.then_inc(mean_done.sem, 1)
            for j in range(DT):
                pe.wait_ge(sq_done.sem, sq_done.base + j + 1)
                last = nc.tensor.matmul(var, core.ones_mean[:, :], sq[:, j, :], start=(j == 0), stop=(j == DT - 1))
            last.then_inc(var_done.sem, 1)

        def modulate(dve, j):
            scale, shift = y_modulation
            dve.wait_ge(x_done.sem, x_done.base + j + 1)
            nc.vector.tensor_scalar(h[:, j, :], x[:, j, :], scale[:, j:j + 1], shift[:, j:j + 1],
                                    ALU.mult, ALU.add).then_inc(h_done.sem, 1)

        @block.vector
        def _(dve):
            for j in range(DT):
                nc.vector.scalar_tensor_tensor(x[:, j, :], core.acc(j), gate[:, j:j + 1], x[:, j, :],
                                               ALU.mult, ALU.add).then_inc(mixed.sem, 1)
            dve.wait_ge(mean_done.sem, mean_done.base + 1)
            for j in range(DT):
                nc.vector.tensor_tensor(diff[:, j, :], x[:, j, :], mean, ALU.subtract).then_inc(diff_done.sem, 1)
            dve.wait_ge(rstd_done.sem, rstd_done.base + 1)
            nc.vector.reciprocal(rstd[:, :], rstd[:, :]).then_inc(rstd_done.sem, 1)
            dve.wait_ge(rstd_done.sem, rstd_done.base + 2)
            for j in range(DT):
                nc.vector.tensor_tensor(diff[:, j, :], diff[:, j, :], rstd[:, :], ALU.mult).then_inc(unit_done.sem, 1)
                if y_modulation is not None and j >= 2:
                    modulate(dve, j - 2)
            if y_modulation is not None:
                modulate(dve, DT - 2), modulate(dve, DT - 1)

        @block.scalar
        def _(act):
            for j in range(DT):
                act.wait_ge(diff_done.sem, diff_done.base + j + 1)
                nc.scalar.activation(sq[:, j, :], diff[:, j, :], ACT.Square).then_inc(sq_done.sem, 1)
            act.wait_ge(var_done.sem, var_done.base + 1)
            nc.scalar.activation(rstd[:, :], var, ACT.Sqrt, bias=core.ln_eps).then_inc(rstd_done.sem, 1)
            for j in range(DT):
                act.wait_ge(unit_done.sem, unit_done.base + j + 1)
                nc.scalar.activation(x[:, j, :], diff[:, j, :], ACT.Identity, scale=g[:, j:j + 1],
                                     bias=b[:, j:j + 1]).then_inc(x_done.sem, 1)

    for s in (mixed, diff_done, sq_done, unit_done, x_done):
        s.advance(DT)
    mean_done.advance(1), var_done.advance(1), rstd_done.advance(2)
    h_done.advance(DT if y_modulation is not None else 0)


def rms_norm(core, x, gate, scale, shift, h, sq, rstd):
    nc = core.nc
    mixed, sq_done, var_done = core.counter("rms_mixed"), core.counter("rms_sq_done"), core.counter("rms_mean_done")
    rstd_done, unit_done, h_done = core.counter("rms_rstd_done"), core.counter("rms_unit_done"), core.counter("rms_h_done")
    ms = core.ps[4][:, 0:T]

    with core.block() as block:
        @block.tensor
        def _(pe):
            for j in range(DT):
                pe.wait_ge(sq_done.sem, sq_done.base + j + 1)
                last = nc.tensor.matmul(ms, core.ones_mean[:, :], sq[:, j, :], start=(j == 0), stop=(j == DT - 1))
            last.then_inc(var_done.sem, 1)

        @block.vector
        def _(dve):
            if gate is not None:
                for j in range(DT):
                    nc.vector.scalar_tensor_tensor(x[:, j, :], core.acc(j), gate[:, j:j + 1], x[:, j, :],
                                                   ALU.mult, ALU.add).then_inc(mixed.sem, 1)
            dve.wait_ge(rstd_done.sem, rstd_done.base + 1)
            nc.vector.reciprocal(rstd[:, :], rstd[:, :]).then_inc(rstd_done.sem, 1)
            dve.wait_ge(rstd_done.sem, rstd_done.base + 2)
            for j in range(DT):
                nc.vector.tensor_tensor(sq[:, j, :], x[:, j, :], rstd[:, :], ALU.mult).then_inc(unit_done.sem, 1)

        @block.scalar
        def _(act):
            for j in range(DT):
                if gate is not None:
                    act.wait_ge(mixed.sem, mixed.base + j + 1)
                nc.scalar.activation(sq[:, j, :], x[:, j, :], ACT.Square).then_inc(sq_done.sem, 1)
            act.wait_ge(var_done.sem, var_done.base + 1)
            nc.scalar.activation(rstd[:, :], ms, ACT.Sqrt, bias=core.rms_eps).then_inc(rstd_done.sem, 1)
            for j in range(DT):
                act.wait_ge(unit_done.sem, unit_done.base + j + 1)
                nc.scalar.activation(h[:, j, :], sq[:, j, :], ACT.Identity, scale=scale[:, j:j + 1],
                                     bias=0.0 if shift is None else shift[:, j:j + 1]).then_inc(h_done.sem, 1)

    for s in (sq_done, unit_done, h_done):
        s.advance(DT)
    var_done.advance(1), rstd_done.advance(2)
    mixed.advance(DT if gate is not None else 0)


def attention(core, h, hc, out, a):
    nc, used = core.nc, core.used
    q, kk, v = a["q"], a["k"], a["v"]
    tmp = a["sm"][:, 3, :].rearrange("p (a t) -> p a t", a=2)
    bq, bk = core.col("bq"), core.col("bk")
    projected, biased = core.counter("attn_projected"), core.counter("attn_biased")
    turned, roped = core.counter("attn_rotated"), core.counter("attn_roped")

    with core.block() as block:
        @block.sync
        def _(sp):
            core.load_ahead(sp)

        @block.tensor
        def _(pe):
            for c in range(4):
                w = core.chunk(pe, c)
                linear_tiles(core, pe, w, h, [core.acc(2 * c), core.acc(2 * c + 1)]).then_inc(used.sem, 1)
            w = core.chunk(pe, 4)
            for s, src in enumerate((h, hc)):
                last = linear_tiles(core, pe, w, src, [core.ps[4 + s][:, 0:T], core.ps[4 + s][:, T:2 * T]])
            last.then_inc(used.sem, 1)
            w = core.chunk(pe, 5)
            for s, src in enumerate((h, hc)):
                for t in range(TT):
                    for k in range(DT):
                        last = nc.tensor.matmul(core.ps[6 + s][:, t * T:t * T + T], src[:, k, t * P:t * P + P],
                                                w[:, k * T:k * T + T], start=(k == 0), stop=(k == DT - 1))
            last.then_inc(used.sem, 1)

        @block.vector
        def _(dve):
            for t in range(DT):
                if t % 2 == 0:
                    dve.wait_ge(used.sem, used.base + t // 2 + 1)
                nc.vector.tensor_scalar(q[:, t, :], core.acc(t), bq[:, t:t + 1], HD ** -0.5, ALU.add, ALU.mult)\
                    .then_inc(biased.sem, 1)
            dve.wait_ge(used.sem, used.base + 5)
            for s in range(2):
                for t in range(2):
                    nc.vector.tensor_scalar(kk[:, s, t, :], core.ps[4 + s][:, t * T:t * T + T], bk[:, t:t + 1],
                                            None, ALU.add).then_inc(biased.sem, 1)
            dve.wait_ge(used.sem, used.base + 6)
            for s in range(2):
                for t in range(TT):
                    nc.vector.tensor_tensor(v[:, s, t, :], core.ps[6 + s][:, t * T:t * T + T], a["bv"][:, :],
                                            ALU.add).then_inc(biased.sem, 1)

    core.stage_done()
    biased.advance(DT + 8)

    with core.block() as block:
        pairs = [q[:, 2 * t:2 * t + 2, :] for t in range(DT // 2)] + [kk[:, 0, :, :]]
        flat = lambda x: x.rearrange("p a t -> p (a t)")

        @block.tensor
        def _(pe):
            for n, x in enumerate(pairs):
                nc.tensor.matmul(core.ps[n][:, :], a["swap"][:, :], flat(x), start=True, stop=True)\
                    .then_inc(turned.sem, 1)

        @block.vector
        def _(dve):
            step = Steps(dve, roped)
            both = lambda x: x.unsqueeze(1).broadcast_to([P, 2, T])
            for n, x in enumerate(pairs):
                dve.wait_ge(turned.sem, turned.base + n + 1)
                step(nc.vector.tensor_tensor(tmp[:, :, :], core.ps[n][:, :].rearrange("p (a t) -> p a t", a=2),
                                             both(a["sin"]), ALU.mult))
                step(nc.vector.tensor_tensor(x, x, both(a["cos"]), ALU.mult))
                step(nc.vector.tensor_tensor(x, x, tmp[:, :, :], ALU.add))
            step.end()

    turned.advance(len(pairs))

    scores_ready, max_ready = core.counter("attn_scores"), core.counter("attn_max")
    exp_done, p_ready, p_turned = core.counter("attn_exp"), core.counter("attn_p_ready"), core.counter("attn_p_turned")
    pt_ready, pv_done, o_copied = core.counter("attn_pt_ready"), core.counter("attn_pv_done"), core.counter("attn_o_copied")
    dsteps = core.counter("attn_dve_steps")
    sm, pt, st = a["sm"], a["pt"], a["stat"]
    units = [(t, e, b) for t in range(DT) for e in range(2) for b in range(TT)]
    N = len(units)
    SCORES = (0, 1, 6, 7)

    with core.block() as block:
        @block.tensor
        def _(pe):
            def scores(u):
                t, e, b = units[u]
                lo = 64 * e
                if u >= 4:
                    pe.wait_ge(exp_done.sem, exp_done.base + u - 3)
                bank = core.ps[SCORES[u % 4]]
                for s in range(2):
                    nc.tensor.matmul(bank[:, s * T:s * T + T], q[lo:lo + 64, t, b * P:b * P + P],
                                     kk[lo:lo + 64, s, t // 4, :], start=(s == 0), stop=False, skip_group_check=True)
                far = (1 - b) * P
                last = nc.tensor.matmul(bank[:, far:far + P], core.ident[:, :], a["mask"][:, b, :],
                                        start=False, stop=True, skip_group_check=True)
                last.then_inc(scores_ready.sem, 1)

            def values(u):
                t, e, b = units[u]
                head = 2 * (t // 4) + e
                pe.wait_ge(pt_ready.sem, pt_ready.base + u + 1)
                if u % 4 == 0 and t >= 2:
                    pe.wait_ge(o_copied.sem, o_copied.base + t - 1)
                for c in range(4):
                    last = nc.tensor.matmul(core.ps[4 + t % 2][64 * e:64 * e + 64, b * P:b * P + P],
                                            v[:, c // 2, c % 2, head * HD:head * HD + HD],
                                            pt[:, u % 2, c * P:c * P + P], start=(c == 0), stop=(c == 3))
                last.then_inc(pv_done.sem, 1)

            scores(0), scores(1), scores(2)
            for u in range(N):
                if u + 3 < N:
                    scores(u + 3)
                pe.wait_ge(p_ready.sem, p_ready.base + u + 1)
                if u >= 2:
                    pe.wait_ge(pt_ready.sem, pt_ready.base + u - 1)
                for c in range(4):
                    last = nc.tensor.transpose(core.ps[2 + u % 2][:, c * P:c * P + P], sm[:, u % 4, c * P:c * P + P],
                                               core.ident[:, :])
                last.then_inc(p_turned.sem, 1)
                if u >= 1:
                    values(u - 1)
            values(N - 1)

        @block.vector
        def _(dve):
            step = Steps(dve, dsteps)

            def top(u):
                t, e, b = units[u]
                head = 8 * (t // 4) + 4 * e + t % 4
                dve.wait_ge(scores_ready.sem, scores_ready.base + u + 1)
                step(nc.vector.tensor_reduce(st[:, u % 4, 0:1], core.ps[SCORES[u % 4]][:, :], AX.X, ALU.max))
                nc.vector.tensor_scalar(st[:, u % 4, 1:2], st[:, u % 4, 0:1], a["sink"][:, head:head + 1], -1.0,
                                        ALU.max, ALU.mult).then_inc(max_ready.sem, 1)

            def normalize(u):
                dve.wait_ge(exp_done.sem, exp_done.base + u + 1)
                step(nc.vector.tensor_tensor(st[:, u % 4, 4:5], st[:, u % 4, 2:3], st[:, u % 4, 3:4], ALU.add))
                step(nc.vector.reciprocal(st[:, u % 4, 5:6], st[:, u % 4, 4:5]))
                nc.vector.tensor_scalar(sm[:, u % 4, :], sm[:, u % 4, :], st[:, u % 4, 5:6], None, ALU.mult)\
                    .then_inc(p_ready.sem, 1)

            top(0), top(1)
            for u in range(N):
                if u + 2 < N:
                    top(u + 2)
                normalize(u)
            step.end()

        @block.scalar
        def _(act):
            def copy_out(t):
                act.wait_ge(pv_done.sem, pv_done.base + 4 * t + 4)
                nc.scalar.copy(out[:, t, :], core.ps[4 + t % 2][:, 0:T]).then_inc(o_copied.sem, 1)

            def turn_back(u):
                act.wait_ge(p_turned.sem, p_turned.base + u + 1)
                if u >= 2:
                    act.wait_ge(pv_done.sem, pv_done.base + u - 1)
                nc.scalar.copy(pt[:, u % 2, :], core.ps[2 + u % 2][:, :]).then_inc(pt_ready.sem, 1)

            for u in range(N):
                t, e, b = units[u]
                head = 8 * (t // 4) + 4 * e + t % 4
                act.wait_ge(max_ready.sem, max_ready.base + u + 1)
                if u >= 4:
                    act.wait_ge(p_turned.sem, p_turned.base + u - 3)
                nc.scalar.activation(sm[:, u % 4, :], core.ps[SCORES[u % 4]][:, :], ACT.Exp, bias=st[:, u % 4, 1:2],
                                     accum_out=st[:, u % 4, 2:3])
                nc.scalar.activation(st[:, u % 4, 3:4], a["sink"][:, head:head + 1], ACT.Exp,
                                     bias=st[:, u % 4, 1:2]).then_inc(exp_done.sem, 1)
                if u >= 1:
                    turn_back(u - 1)
                    if (u - 1) % 4 == 3 and u >= 8:
                        copy_out((u - 1) // 4 - 1)
            turn_back(N - 1)
            copy_out(DT - 2), copy_out(DT - 1)

    for s in (scores_ready, max_ready, exp_done, p_ready, p_turned, pt_ready, pv_done):
        s.advance(N)
    o_copied.advance(DT)


def fourier(core, h, out, cs, uv):
    nc = core.nc
    uv_ready, uv_copied = core.counter("fourier_uv_ready"), core.counter("fourier_uv_copied")
    f_ready, f_copied = core.counter("fourier_out_ready"), core.counter("fourier_out_copied")
    G = D // 256
    with core.block() as block:
        @block.tensor
        def _(pe):
            def features(g):
                for t in range(TT):
                    if g >= 2:
                        pe.wait_ge(uv_copied.sem, uv_copied.base + 2 * (g - 2) + t + 1)
                    for k in range(2):
                        last = nc.tensor.matmul(core.ps[2 * (g % 2) + t][:, :], h[:, 2 * g + k, t * P:t * P + P],
                                                cs[:, k, 0:2, :].rearrange("p a n -> p (a n)"),
                                                start=(k == 0), stop=(k == 1))
                    last.then_inc(uv_ready.sem, 1)

            def tokens(g):
                pe.wait_ge(uv_copied.sem, uv_copied.base + 2 * g + 2)
                if g >= 2:
                    pe.wait_ge(f_copied.sem, f_copied.base + g - 1)
                for m in range(2):
                    n = 0
                    for part in (0, 1):
                        for t in range(TT):
                            last = nc.tensor.matmul(core.ps[4 + g % 2][:, m * T:m * T + T],
                                                    uv[:, g % 2, t, part, m * P:m * P + P],
                                                    cs[:, t, 2 * part, :], start=(n == 0), stop=(n == 3))
                            n += 1
                last.then_inc(f_ready.sem, 1)

            features(0)
            for g in range(G):
                if g + 1 < G:
                    features(g + 1)
                tokens(g)

        @block.scalar
        def _(act):
            for n in range(2 * G):
                g, t = n // 2, n % 2
                act.wait_ge(uv_ready.sem, uv_ready.base + n + 1)
                if g >= 2:
                    act.wait_ge(f_ready.sem, f_ready.base + g - 1)
                nc.scalar.copy(uv[:, g % 2, t, :, :].rearrange("p a n -> p (a n)"), core.ps[2 * (g % 2) + t][:, :])\
                    .then_inc(uv_copied.sem, 1)

        @block.vector
        def _(dve):
            for g in range(G):
                dve.wait_ge(f_ready.sem, f_ready.base + g + 1)
                nc.vector.tensor_copy(out[:, 2 * g:2 * g + 2, :].rearrange("p m t -> p (m t)"),
                                      core.ps[4 + g % 2][:, :]).then_inc(f_copied.sem, 1)

    uv_ready.advance(2 * G), uv_copied.advance(2 * G), f_ready.advance(G), f_copied.advance(G)


NG = 4
TK = 2 * TT


def ab_project(core, h, hc, b):
    nc, used = core.nc, core.used
    raw, qkv = b["raw"], b["qkv"]
    copied, conv, small, convd = (core.counter(n) for n in ("ab_copied", "ab_conv_steps", "ab_small_ready", "ab_conv_done"))
    padded, smalls = core.counter("ab_padded"), core.counter("ab_small_copied")
    with core.block() as block:
        @block.sync
        def _(sp):
            core.load_ahead(sp)

        @block.tensor
        def _(pe):
            def free(n):
                if n >= 8:
                    pe.wait_ge(copied.sem, copied.base + n - 7)

            n = 0
            for c in range(14):
                w = core.chunk(pe, c)
                if c in (10, 11):
                    for src in (hc, h):
                        free(n)
                        for t in range(TT):
                            for k in range(DT):
                                last = nc.tensor.matmul(core.ps[n % 8][:, t * T:t * T + T], src[:, k, t * P:t * P + P],
                                                        w[:, k * T:k * T + T], start=(k == 0), stop=(k == DT - 1))
                        last.then_inc(used.sem if src is h else small.sem, 1)
                        n += 1
                else:
                    for src in ((hc, h) if c in (0, 1, 2, 3, 9) else (h,)):
                        free(n)
                        last = linear_tiles(core, pe, w, src, [core.ps[n % 8][:, 0:T], core.ps[n % 8][:, T:2 * T]])
                        last.then_inc(used.sem if src is h else small.sem, 1)
                        n += 1

        order, nctx = [], 0
        for c in range(14):
            for src in ((0, 1) if c in (0, 1, 2, 3, 9, 10, 11) else (1,)):
                nctx += src == 0
                order.append((c, src, nctx))

        def destination(c, src):
            if c < 4:
                tile = 2 * c + (12 if src else 0)
                return raw[:, tile:tile + 2, 1:T + 1]
            if c < 6:
                return raw[:, 8 + 2 * (c - 4):10 + 2 * (c - 4), 1:T + 1]
            if c < 8:
                return b["gz"][:, 2 * (c - 6):2 * (c - 6) + 2, :]
            if c == 8:
                return b["lq"][:, :, :]
            if c == 9:
                return b["lk"][:, :, src * T:src * T + T]
            if c < 12:
                return b["lv"][:, 2 * src:2 * src + 2, (c - 10) * T:(c - 10) * T + T]
            return b["lg"][:, 2 * (c - 12):2 * (c - 12) + 2, :]

        @block.scalar
        def _(act):
            for n, (c, src, nctx) in enumerate(order):
                if src:
                    act.wait_ge(used.sem, used.base + c + 1)
                else:
                    act.wait_ge(small.sem, small.base + nctx)
                if n == 0:
                    act.wait_ge(padded.sem, padded.base + 1)
                nc.scalar.copy(destination(c, src), core.ps[n % 8][:, :].rearrange("p (a t) -> p a t", a=2))\
                    .then_inc(copied.sem, 1)
            for i in range(20):
                act.wait_ge(convd.sem, convd.base + i + 1)
                nc.scalar.activation(qkv[:, i, :], qkv[:, i, :], ACT.Silu).then_inc(smalls.sem, 1)

        @block.vector
        def _(dve):
            nc.vector.memset(raw[:, :, 0:1], 0.0)
            nc.vector.memset(raw[:, :, T + 1:T + 2], 0.0).then_inc(padded.sem, 1)
            dve.wait_ge(padded.sem, padded.base + 1)
            step = Steps(dve, conv)
            w = core.col("ab_conv")
            n_of = {(c, src): n for n, (c, src, _) in enumerate(order)}
            for i in range(20):
                c, src = (i // 2, 0) if i < 8 else ((4 + (i - 8) // 2, 1) if i < 12 else ((i - 12) // 2, 1))
                tile = i + 4 if i < 8 else i - 8
                dve.wait_ge(copied.sem, copied.base + n_of[(c, src)] + 1)
                y = qkv[:, i, :]
                step(nc.vector.tensor_scalar(y, raw[:, i, 0:T], w[:, tile:tile + 1], None, ALU.mult))
                step(nc.vector.scalar_tensor_tensor(y, raw[:, i, 1:T + 1], w[:, 12 + tile:13 + tile], y, ALU.mult, ALU.add))
                nc.vector.scalar_tensor_tensor(y, raw[:, i, 2:T + 2], w[:, 24 + tile:25 + tile], y, ALU.mult, ALU.add)\
                    .then_inc(convd.sem, 1)
            step.end()

    nout = len(order)
    core.stage_done()
    copied.advance(nout), small.advance(nout - 14), padded.advance(1), convd.advance(20), smalls.advance(20)


def ab_gates(core, h, hc, b):
    nc = core.nc
    g, beta, gc, la = b["g"], b["beta"], b["gc"], b["la"]
    pe_s, dve_s, act_s = core.counter("gates_products"), core.counter("gates_dve_steps"), core.counter("gates_act_steps")
    wsm = b["w_small"]
    with core.block() as block:
        @block.tensor
        def _(pe):
            for s, src in enumerate((hc, h)):
                for t in range(TT):
                    n = 2 * s + t
                    for k in range(DT):
                        nc.tensor.matmul(core.ps[0][:, n * 16:n * 16 + 16], src[:, k, t * P:t * P + P],
                                         wsm[:, k, 0:16], start=(k == 0), stop=(k == DT - 1))
                for k in range(DT):
                    last = nc.tensor.matmul(core.ps[1][0:32, s * T:s * T + T], wsm[:, k, 16:48], src[:, k, :],
                                            start=(k == 0), stop=(k == DT - 1))
            last.then_inc(pe_s.sem, 1)
            pe.wait_ge(act_s.sem, act_s.base + 1)
            for d in range(2):
                for t in range(2):
                    last = nc.tensor.matmul(core.ps[2 + 2 * d + t][:, :], b["w_gate"][0:32, d, t * P:t * P + P],
                                            b["llr"][0:32, :], start=True, stop=True)
            last.then_inc(pe_s.sem, 1)
            pe.wait_ge(dve_s.sem, dve_s.base + b["g_steps"])
            for n in range(TK):
                for d in range(2):
                    nc.tensor.matmul(core.ps[6][:, n * 8 + 4 * d:n * 8 + 4 * d + 4], b["tri"][:, d, :],
                                     g[:, n, 4 * d:4 * d + 4], start=True, stop=True)
                last = nc.tensor.matmul(core.ps[6][:, 32 + n * 8:32 + n * 8 + 8], b["tri"][:, 2, :], g[:, n, :],
                                        start=True, stop=True)
            last.then_inc(pe_s.sem, 1)

        @block.scalar
        def _(act):
            step = Steps(act, act_s)
            act.wait_ge(pe_s.sem, pe_s.base + 1)
            step(nc.scalar.copy(b["llr"][0:32, :], core.ps[1][0:32, :]))
            act.wait_ge(dve_s.sem, dve_s.base + 2)
            step(nc.scalar.activation(b["t1"][:, :, :], b["t1"][:, :, :], ACT.Exp))
            step(nc.scalar.activation(b["t1"][:, :, :], b["t1"][:, :, :], ACT.Ln, bias=core.one[:, 0:1]))
            step(nc.scalar.activation(b["ea"][:, :], b["a_log"][:, :], ACT.Exp))
            act.wait_ge(dve_s.sem, dve_s.base + b["la_steps"])
            for i in range(4):
                step(nc.scalar.activation(b["lt"][:, i, :], b["lt"][:, i, :], ACT.Exp))
                step(nc.scalar.activation(b["lt"][:, i, :], b["lt"][:, i, :], ACT.Ln, bias=core.one[:, 0:1]))
            step(nc.scalar.activation(beta[:, :, :], core.ps[0][:, 0:64].rearrange("p (n i) -> p n i", i=16)[:, :, 8:16],
                                      ACT.Sigmoid))
            assert step.n == 13
            step.end()

        @block.vector
        def _(dve):
            step = Steps(dve, dve_s)
            ga = core.ps[0][:, 0:64].rearrange("p (n i) -> p n i", i=16)[:, :, 0:8]
            dve.wait_ge(pe_s.sem, pe_s.base + 1)
            step(nc.vector.tensor_tensor(b["t2"][:, :, :], ga, b["dt_bias"].unsqueeze(1).broadcast_to([P, TK, 8]), ALU.add))
            step(nc.vector.scalar_tensor_tensor(b["t1"][:, :, :], b["t2"][:, :, :], -1.0, b["t2"][:, :, :], ALU.mult, ALU.min))
            step(nc.vector.tensor_scalar(b["t2"][:, :, :], b["t2"][:, :, :], 0.0, None, ALU.max))
            dve.wait_ge(act_s.sem, act_s.base + 4)
            step(nc.vector.tensor_tensor(b["t2"][:, :, :], b["t2"][:, :, :], b["t1"][:, :, :], ALU.add))
            step(nc.vector.tensor_tensor(b["t2"][:, :, :], b["t2"][:, :, :],
                                         b["ea"].unsqueeze(1).broadcast_to([P, TK, 8]), ALU.mult))
            step(nc.vector.tensor_scalar(g[:, :, :], b["t2"][:, :, :], -1.0, None, ALU.mult))
            assert step.n == b["g_steps"]
            gb = core.col("gla_gate_b")
            dve.wait_ge(pe_s.sem, pe_s.base + 2)
            for i in range(4):
                step(nc.vector.tensor_scalar(b["la"][:, i, :], core.ps[2 + i][:, :], gb[:, i:i + 1], None, ALU.add))
                step(nc.vector.scalar_tensor_tensor(b["lt"][:, i, :], b["la"][:, i, :], -1.0, b["la"][:, i, :], ALU.mult, ALU.min))
                step(nc.vector.tensor_scalar(b["la"][:, i, :], b["la"][:, i, :], 0.0, None, ALU.min))
            assert step.n == b["la_steps"]
            dve.wait_ge(act_s.sem, act_s.base + 12)
            for i in range(4):
                step(nc.vector.tensor_tensor(b["la"][:, i, :], b["la"][:, i, :], b["lt"][:, i, :], ALU.subtract))
                step(nc.vector.tensor_scalar(b["la"][:, i, :], b["la"][:, i, :], 1.0 / 16.0, None, ALU.mult))
            dve.wait_ge(pe_s.sem, pe_s.base + 3)
            step(nc.vector.tensor_copy(gc[:, :, :, :].rearrange("p a n i -> p (a n i)"), core.ps[6][:, 0:64]))
            step.end()

    pe_s.advance(3)


def l2_norm(core, b):
    nc = core.nc
    qkv = b["qkv"]
    tiles = [0, 1, 2, 3, 8, 9, 10, 11, 12, 13, 14, 15]
    sq_d, sum_d, scaled = core.counter("l2_squares"), core.counter("l2_sums"), core.counter("l2_dve_steps")
    norm_d = core.counter("l2_norms")
    with core.block() as block:
        @block.scalar
        def _(act):
            for n, i in enumerate(tiles):
                nc.scalar.activation(b["sq12"][:, n, :], qkv[:, i, :], ACT.Square).then_inc(sq_d.sem, 1)
            for n, i in enumerate(tiles):
                act.wait_ge(sum_d.sem, sum_d.base + n // 2 + 1)
                query = 8 <= i < 12
                nc.scalar.activation(b["sq12"][:, n, :], core.ps[n // 2][:, (n % 2) * T:(n % 2) * T + T], ACT.Sqrt,
                                     scale=float(P) if query else 1.0, bias=core.q_eps if query else core.rms_eps)\
                    .then_inc(norm_d.sem, 1)

        @block.tensor
        def _(pe):
            for n in range(12):
                pe.wait_ge(sq_d.sem, sq_d.base + n + 1)
                last = nc.tensor.matmul(core.ps[n // 2][:, (n % 2) * T:(n % 2) * T + T], core.ones[:, :],
                                        b["sq12"][:, n, :], start=True, stop=True)
                if n % 2:
                    last.then_inc(sum_d.sem, 1)

        @block.vector
        def _(dve):
            step = Steps(dve, scaled)
            for n, i in enumerate(tiles):
                dve.wait_ge(norm_d.sem, norm_d.base + n + 1)
                step(nc.vector.reciprocal(b["sq12"][:, n, :], b["sq12"][:, n, :]))
                step(nc.vector.tensor_tensor(qkv[:, i, :], qkv[:, i, :], b["sq12"][:, n, :], ALU.mult))
            step.end()

    sq_d.advance(12), sum_d.advance(6), norm_d.advance(12)


def turn_tiles(core, pairs):
    nc = core.nc
    ready, copied = core.counter("tiles_turned"), core.counter("tiles_copied")
    with core.block() as block:
        @block.tensor
        def _(pe):
            for n, (ins, out) in enumerate(pairs):
                if n >= 4:
                    pe.wait_ge(copied.sem, copied.base + n - 3)
                for c, x in enumerate(ins):
                    last = nc.tensor.transpose(core.ps[n % 4][:, c * P:c * P + P], x, core.ident[:, :])
                last.then_inc(ready.sem, 1)

        @block.scalar
        def _(act):
            for n, (ins, out) in enumerate(pairs):
                act.wait_ge(ready.sem, ready.base + n + 1)
                nc.scalar.copy(out, core.ps[n % 4][:, :]).then_inc(copied.sem, 1)

    ready.advance(len(pairs)), copied.advance(len(pairs))


HALVES = (0, CK)


def chunk_tile(c):
    return c // 2, c % 2


def gdn_factors(core, b):
    nc = core.nc
    gc = b["gc"]
    d_s, a_s = core.counter("gdn_dve_steps"), core.counter("gdn_act_steps")
    with core.block() as block:
        @block.scalar
        def _(act):
            step = Steps(act, a_s)
            step(nc.scalar.activation(b["bg"][:, :, :], gc[:, 0, :, :], ACT.Exp))
            act.wait_ge(d_s.sem, d_s.base + 2)
            step(nc.scalar.activation(b["ed"][:, :, :], b["ed"][:, :, :], ACT.Exp))
            step.end()

        @block.vector
        def _(dve):
            step = Steps(dve, d_s)
            step(nc.vector.tensor_scalar(b["ngc"][:, :, :], gc[:, 0, :, :], -1.0, None, ALU.mult))
            step(nc.vector.tensor_tensor(b["ed"][:, :, :], gc[:, 1, :, :], gc[:, 0, :, :], ALU.subtract))
            dve.wait_ge(a_s.sem, a_s.base + 1)
            step(nc.vector.tensor_tensor(b["bg"][:, :, :], b["bg"][:, :, :], b["beta"][:, :, :], ALU.mult))
            step.end()


def gdn_tile(core, b, n):
    nc = core.nc
    g, beta, gc, rows, qkv = b["g"], b["beta"], b["gc"], b["rows"], b["qkv"]
    row_s, copy_s = core.counter("gdn_rows_ready"), core.counter("gdn_rows_copied")
    kk_s, ex_s, dd_s = core.counter("gdn_kk_ready"), core.counter("gdn_exponent_ready"), core.counter("gdn_decay_ready")
    l_s, qd_s, q_s = core.counter("gdn_l_ready"), core.counter("gdn_qd_ready"), core.counter("gdn_qd_exponential")
    latent = n >= TT
    m0 = n - TT
    k_of = lambda h: qkv[:, 12 + h, m0 * P:m0 * P + P] if latent else qkv[:, h, n * P:n * P + P]
    q_of = lambda h: qkv[:, 8 + h, m0 * P:m0 * P + P]
    jobs = [("l", d) for d in range(2)] + ([("a", d) for d in range(2)] if latent else [])

    with core.block() as block:
        @block.tensor
        def _(pe):
            for d in range(2):
                for h in range(NG):
                    last = nc.tensor.matmul(core.ps[d][:, h * P:h * P + P],
                                            g[:, n, 4 * d + h:4 * d + h + 1].broadcast_to([P, P]), b["tri"][:, d, :],
                                            start=True, stop=True)
                last.then_inc(row_s.sem, 1)
            for m in range(2 if latent else 1):
                for h in range(NG):
                    for lo in HALVES:
                        last = nc.tensor.matmul(core.ps[2 + m][lo:lo + CK, h * CK:h * CK + CK],
                                                k_of(h)[:, lo:lo + CK],
                                                (q_of(h) if m else k_of(h))[:, lo:lo + CK], start=True, stop=True)
                last.then_inc(kk_s.sem, 1)

        @block.scalar
        def _(act):
            for d in range(2):
                act.wait_ge(row_s.sem, row_s.base + d + 1)
                nc.scalar.copy(rows[:, 4 * d:4 * d + 4, :].rearrange("p h t -> p (h t)"), core.ps[d][:, :])\
                    .then_inc(copy_s.sem, 1)
            for d in range(2):
                act.wait_ge(copy_s.sem, copy_s.base + d + 1)
                row = rows[:, 4 * d:4 * d + 4, :]
                at = row.rearrange("p h (c t) -> p h c t", t=CK)[:, :, :, CK - 1 if d == 0 else 0]
                last = nc.scalar.activation(b["gl"][:, 4 * d:4 * d + 4, 2 * n:2 * n + 2], at, ACT.Exp)
                if latent:
                    last = nc.scalar.activation(b["qd"][:, 4 * d:4 * d + 4, m0 * P:m0 * P + P], row, ACT.Exp)
                last.then_inc(q_s.sem, 1)
            for m, (kind, d) in enumerate(jobs):
                act.wait_ge(ex_s.sem, ex_s.base + m + 1)
                src = gc[:, 0, :, :] if kind == "l" else b["ngc"][:, :, :]
                for h in range(NG):
                    last = nc.scalar.activation(b["dd"][:, m % 2, h, :], b["dd"][:, m % 2, h, :], ACT.Exp,
                                                bias=src[:, n, 4 * d + h:4 * d + h + 1])
                last.then_inc(dd_s.sem, 1)

        @block.vector
        def _(dve):
            def exponent(m):
                kind, d = jobs[m]
                if m >= 2:
                    dve.wait_ge(l_s.sem, l_s.base + m - 1)
                else:
                    dve.wait_ge(copy_s.sem, copy_s.base + d + 1)
                for lo in HALVES:
                    at = slice(lo, lo + CK)
                    mask = b["masks"][at, d, 0 if kind == "l" else 1, :].unsqueeze(1).broadcast_to([CK, NG, CK])
                    last = nc.vector.tensor_tensor(b["dd"][at, m % 2, :, :], mask, rows[at, 4 * d:4 * d + 4, at],
                                                   ALU.subtract if kind == "l" else ALU.add)
                last.then_inc(ex_s.sem, 1)

            exponent(0), exponent(1)
            for d in range(2):
                if latent:
                    dve.wait_ge(q_s.sem, q_s.base + d + 1)
                    at = b["qd"][:, 4 * d:4 * d + 4, m0 * P:m0 * P + P]
                    nc.vector.tensor_tensor(at, at, qkv[:, 8:12, m0 * P:m0 * P + P], ALU.mult).then_inc(qd_s.sem, 1)
            for m, (kind, d) in enumerate(jobs):
                dve.wait_ge(dd_s.sem, dd_s.base + m + 1)
                if kind == "l":
                    dve.wait_ge(kk_s.sem, kk_s.base + 1)
                    for h in range(NG):
                        last = nc.vector.scalar_tensor_tensor(b["l"][:, n % 2, 4 * d + h, :],
                                                              core.ps[2][:, h * CK:h * CK + CK],
                                                              beta[:, n, 4 * d + h:4 * d + h + 1],
                                                              b["dd"][:, m % 2, h, :], ALU.mult, ALU.mult)
                else:
                    dve.wait_ge(kk_s.sem, kk_s.base + 2)
                    last = nc.vector.tensor_tensor(b["att"][m0][:, 4 * d:4 * d + 4, :],
                                                   core.ps[3][:, 0:NG * CK].rearrange("p (h t) -> p h t", h=NG),
                                                   b["dd"][:, m % 2, :, :], ALU.mult)
                last.then_inc(l_s.sem, 1)
                if m + 2 < len(jobs):
                    exponent(m + 2)

    row_s.advance(2), copy_s.advance(2), q_s.advance(2), qd_s.advance(2 if latent else 0)
    kk_s.advance(2 if latent else 1), ex_s.advance(len(jobs)), dd_s.advance(len(jobs)), l_s.advance(len(jobs))


def gdn_solve(core, b, tiles):
    nc = core.nc
    LEVELS, UNITS = 6, 4
    x, w, o, pm, l = b["x"], b["w"], b["o"], b["pm"], b["l"]
    names = ("gdn_masked", "gdn_p_ready", "gdn_p_copied", "gdn_wp_ready", "gdn_updated")
    sg = [{k: core.counter(f"{k}_{u}") for k in names} for u in range(UNITS)]
    cleared, out_copied = core.counter("gdn_cleared"), core.counter("gdn_out_copied")
    own = core.counter("gdn_solve_dve_steps")
    wait = lambda eng, s, name, n: eng.wait_ge(s[name].sem, s[name].base + n)
    hs = [slice(i * P, i * P + P) for i in range(NG)]

    with core.block() as block:
        @block.tensor
        def _(pe):
            for u, s in enumerate(sg):
                wait(pe, s, "gdn_masked", 1)
                for h in hs:
                    last = nc.tensor.transpose(core.ps[u][:, h], x[:, u, h], core.ident[:, :])
                last.then_inc(s["gdn_p_ready"].sem, 1)
            for lv in range(1, LEVELS):
                for u, s in enumerate(sg):
                    wait(pe, s, "gdn_masked", lv + 1)
                    if lv == 1:
                        wait(pe, s, "gdn_p_copied", 1)
                    else:
                        wait(pe, s, "gdn_updated", lv - 1)
                    for h in hs:
                        last = nc.tensor.matmul(core.ps[u][:, h], o[:, u, h], w[:, u, h], start=True, stop=True)
                    last.then_inc(s["gdn_p_ready"].sem, 1)
                for u, s in enumerate(sg):
                    wait(pe, s, "gdn_p_copied", lv + 1)
                    for h in hs:
                        last = nc.tensor.matmul(core.ps[u][:, h], x[:, u, h], pm[:, u, h], start=True, stop=True)
                    if lv < LEVELS - 1:
                        for h in hs:
                            last = nc.tensor.matmul(core.ps[4 + u][:, h], pm[:, u, h], x[:, u, h], start=True, stop=True)
                    last.then_inc(s["gdn_wp_ready"].sem, 1)
            for u, s in enumerate(sg):
                n = tiles[u // 2]
                wait(pe, s, "gdn_updated", LEVELS + 1)
                for i, h in enumerate(hs):
                    last = nc.tensor.matmul(core.ps[u][:, h], o[:, u, h], b["vtm"][:, n, i, :], start=True, stop=True)
                last.then_inc(s["gdn_wp_ready"].sem, 1)
                for i, h in enumerate(hs):
                    last = nc.tensor.matmul(core.ps[4 + u][:, h], b["ktm"][:, n, i, :], pm[:, u, h], start=True, stop=True)
                last.then_inc(s["gdn_wp_ready"].sem, 1)

        @block.scalar
        def _(act):
            for u, s in enumerate(sg):
                wait(act, s, "gdn_p_ready", 1)
                nc.scalar.copy(w[:, u, :], core.ps[u][:, :]).then_inc(s["gdn_p_copied"].sem, 1)
            for lv in range(1, LEVELS):
                for u, s in enumerate(sg):
                    wait(act, s, "gdn_p_ready", lv + 1)
                    if lv >= 2:
                        wait(act, s, "gdn_wp_ready", lv - 1)
                    nc.scalar.copy(pm[:, u, :], core.ps[u][:, :]).then_inc(s["gdn_p_copied"].sem, 1)
            for u, s in enumerate(sg):
                wait(act, s, "gdn_wp_ready", LEVELS + 1)
                d = u % 2
                nc.scalar.copy(b["kcdT"][:, tiles[u // 2], 4 * d:4 * d + 4, :].rearrange("p h t -> p (h t)"),
                               core.ps[4 + u][:, :]).then_inc(out_copied.sem, 1)

        @block.vector
        def _(dve):
            step = Steps(dve, own)
            heads = lambda v: v.rearrange("p (h t) -> p h t", h=NG)
            at = [slice(lo, lo + CK) for lo in HALVES]
            level = lambda u, lv, r: b["levels"][r, u % 2, lv, :].unsqueeze(1).broadcast_to([CK, NG, CK])
            part = lambda u, r: l[r, u // 2, 4 * (u % 2):4 * (u % 2) + 4, :]

            nc.vector.memset(x[:, :, :], 0.0)
            nc.vector.memset(o[:, :, :], 0.0).then_inc(cleared.sem, 1)
            dve.wait_ge(cleared.sem, cleared.base + 1)
            for u, s in enumerate(sg):
                for r in at:
                    last = nc.vector.tensor_tensor(heads(x[r, u, :])[:, :, r], part(u, r), level(u, 0, r), ALU.mult)
                step(last)
                for r in at:
                    last = nc.vector.tensor_tensor(heads(x[r, u, :])[:, :, r], level(u, LEVELS, r),
                                                   heads(x[r, u, :])[:, :, r], ALU.subtract)
                last.then_inc(s["gdn_masked"].sem, 1)
            for lv in range(1, LEVELS):
                for u, s in enumerate(sg):
                    if lv >= 2:
                        wait(dve, s, "gdn_p_ready", lv)
                    for r in at:
                        last = nc.vector.tensor_tensor(heads(o[r, u, :])[:, :, r], part(u, r), level(u, lv, r), ALU.mult)
                    last.then_inc(s["gdn_masked"].sem, 1)
                for u, s in enumerate(sg):
                    wait(dve, s, "gdn_wp_ready", lv)
                    last = nc.vector.tensor_tensor(w[:, u, :], w[:, u, :], core.ps[u][:, :], ALU.subtract)
                    if lv < LEVELS - 1:
                        last = nc.vector.tensor_tensor(x[:, u, :], x[:, u, :], core.ps[4 + u][:, :], ALU.subtract)
                    last.then_inc(s["gdn_updated"].sem, 1)
            for u, s in enumerate(sg):
                wait(dve, s, "gdn_updated", LEVELS - 1)
                for out, f in ((o, "beta"), (pm, "bg")):
                    factor = b[f][:, tiles[u // 2], 4 * (u % 2):4 * (u % 2) + 4].unsqueeze(2).broadcast_to([P, NG, P])
                    nc.vector.tensor_tensor(heads(out[:, u, :]), heads(w[:, u, :]), factor, ALU.mult)\
                        .then_inc(s["gdn_updated"].sem, 1)
            for u, s in enumerate(sg):
                wait(dve, s, "gdn_wp_ready", LEVELS)
                d = u % 2
                nc.vector.tensor_copy(b["u0"][:, tiles[u // 2], 4 * d:4 * d + 4, :].rearrange("p h t -> p (h t)"),
                                      core.ps[u][:, :]).then_inc(out_copied.sem, 1)
            step.end()

    for s in sg:
        for name, n in (("gdn_masked", LEVELS), ("gdn_p_ready", LEVELS), ("gdn_p_copied", LEVELS),
                        ("gdn_wp_ready", LEVELS + 1), ("gdn_updated", LEVELS + 1)):
            s[name].advance(n)
    cleared.advance(1), out_copied.advance(2 * UNITS)


def gdn_scan(core, b):
    nc = core.nc
    s, u = b["s"], b["u"]
    ks_s = [core.counter(f"gdn_ks_ready_{d}") for d in range(2)]
    u_s = [core.counter(f"gdn_u_ready_{d}") for d in range(2)]
    du_s = [core.counter(f"gdn_delta_ready_{d}") for d in range(2)]
    st_s = [core.counter(f"gdn_state_ready_{d}") for d in range(2)]
    z_s = core.counter("gdn_state_cleared")
    order = [[0, 1, 2, 3, 4, 5, 6, 7], [3, 2, 1, 0, 7, 6, 5, 4]]
    opened = set()

    with core.block() as block:
        @block.tensor
        def _(pe):
            pe.wait_ge(z_s.sem, z_s.base + 1)
            for i in range(8):
                for d in range(2):
                    n, half = chunk_tile(order[d][i])
                    lo = CK * half
                    if i >= 1:
                        pe.wait_ge(st_s[d].sem, st_s[d].base + i)
                    for h in range(NG):
                        last = nc.tensor.matmul(core.ps[d][lo:lo + CK, h * P:h * P + P],
                                                b["kcdT"][:, n, 4 * d + h, lo:lo + CK], s[:, 4 * d + h, :],
                                                start=True, stop=True)
                    last.then_inc(ks_s[d].sem, 1)
                for d in range(2):
                    n, half = chunk_tile(order[d][i])
                    lo = CK * half
                    if n >= 2:
                        at = (n - 2) * P + lo
                        for h in range(NG):
                            bank = 6 + h // 2
                            nc.tensor.matmul(core.ps[bank][:, (h % 2) * T + at:(h % 2) * T + at + CK],
                                             s[:, 4 * d + h, :], b["qd"][:, 4 * d + h, at:at + CK],
                                             start=bank not in opened, stop=False, skip_group_check=True)
                            opened.add(bank)
                    pe.wait_ge(u_s[d].sem, u_s[d].base + 2 * i + 2)
                    for h in range(NG):
                        last = nc.tensor.matmul(core.ps[2 + d][:, h * P:h * P + P],
                                                b["ktm"][lo:lo + CK, n, h, :], b["ue"][lo:lo + CK, d, h * P:h * P + P],
                                                start=True, stop=True)
                    if n >= 2:
                        if d == 1:
                            pe.wait_ge(du_s[0].sem, du_s[0].base + i + 1)
                        elif i >= 1:
                            pe.wait_ge(du_s[1].sem, du_s[1].base + i)
                        for h in range(NG):
                            last = nc.tensor.matmul(core.ps[6 + h // 2][:, (h % 2) * T + at:(h % 2) * T + at + CK],
                                                    u[lo:lo + CK, d, h * P:h * P + P],
                                                    b["att"][n - 2][lo:lo + CK, 4 * d + h, :],
                                                    start=False, stop=(i >= 6), skip_group_check=True)
                    last.then_inc(du_s[d].sem, 1)

        @block.vector
        def _(dve):
            nc.vector.memset(s[:, :, :], 0.0).then_inc(z_s.sem, 1)
            dve.wait_ge(z_s.sem, z_s.base + 1)
            for i in range(8):
                for d in range(2):
                    n, half = chunk_tile(order[d][i])
                    lo = CK * half
                    dve.wait_ge(ks_s[d].sem, ks_s[d].base + i + 1)
                    if i >= 1:
                        dve.wait_ge(du_s[d].sem, du_s[d].base + i)
                    nc.vector.tensor_tensor(u[lo:lo + CK, d, :],
                                            b["u0"][lo:lo + CK, n, 4 * d:4 * d + 4, :].rearrange("p h t -> p (h t)"),
                                            core.ps[d][lo:lo + CK, :], ALU.subtract).then_inc(u_s[d].sem, 1)
                    dve.wait_ge(u_s[d].sem, u_s[d].base + 2 * i + 1)
                    nc.vector.tensor_tensor(b["ue"][lo:lo + CK, d, :].rearrange("p (h t) -> p h t", h=NG),
                                            u[lo:lo + CK, d, :].rearrange("p (h t) -> p h t", h=NG),
                                            b["ed"][lo:lo + CK, n, 4 * d:4 * d + 4].unsqueeze(2).broadcast_to([CK, NG, P]),
                                            ALU.mult).then_inc(u_s[d].sem, 1)
                for d in range(2):
                    dve.wait_ge(du_s[d].sem, du_s[d].base + i + 1)
                    c = order[d][i]
                    for h in range(NG):
                        last = nc.vector.scalar_tensor_tensor(s[:, 4 * d + h, :], s[:, 4 * d + h, :],
                                                              b["gl"][:, 4 * d + h, c:c + 1],
                                                              core.ps[2 + d][:, h * P:h * P + P], ALU.mult, ALU.add)
                    last.then_inc(st_s[d].sem, 1)

    z_s.advance(1)
    for d in range(2):
        for x in (ks_s[d], du_s[d], st_s[d]):
            x.advance(8)
        u_s[d].advance(16)


def gla_prepare(core, b):
    nc = core.nc
    la, bc = b["la"], b["bc"]
    lq, lk = b["lq"], b["lk"]
    d_s, a_s, p_s = core.counter("gla_dve_steps"), core.counter("gla_act_steps"), core.counter("gla_attn_ready")
    chunks = lambda x: x.rearrange("p (c t) -> p c t", t=CK)

    with core.block() as block:
        @block.vector
        def _(dve):
            step = Steps(dve, d_s)
            for i in range(4):
                d = i // 2
                src, dst = la[:, i, :], bc[:, i, :]
                if d == 1:
                    src, dst = src[:, ::-1], dst[:, ::-1]
                step(nc.vector.tensor_tensor_scan(dst, b["carry"][:, :], src, 0.0, ALU.mult, ALU.add))
            for i in range(4):
                d, t = i // 2, i % 2
                end, mid = (CK - 1, CK // 2) if d == 0 else (0, CK // 2 - 1)
                c8 = chunks(bc[:, i, :])
                c4 = chunks(bc[:, i, T:2 * T])
                step(nc.vector.tensor_tensor(chunks(b["kdT"][:, i, :]), c8[:, :, end:end + 1].broadcast_to([P, 8, CK]),
                                             c8, ALU.subtract))
                step(nc.vector.tensor_tensor(chunks(b["qr"][:, i, :]), c4,
                                             c4[:, :, mid:mid + 1].broadcast_to([P, 4, CK]), ALU.subtract))
                step(nc.vector.tensor_tensor(chunks(b["kr"][:, i, :]), c4[:, :, mid:mid + 1].broadcast_to([P, 4, CK]),
                                             c4, ALU.subtract))
            for i in range(4):
                t = i % 2
                dve.wait_ge(a_s.sem, a_s.base + 5 * (i + 1))
                step(nc.vector.tensor_tensor(b["kdT"][:, i, :], b["kdT"][:, i, :], lk[:, t, :], ALU.mult))
                step(nc.vector.tensor_tensor(b["kr"][:, i, :], b["kr"][:, i, :], lk[:, t, T:2 * T], ALU.mult))
                step(nc.vector.scalar_tensor_tensor(b["qr"][:, i, :], b["qr"][:, i, :], CK ** -0.5, lq[:, t, :],
                                                    ALU.mult, ALU.mult))
                step(nc.vector.scalar_tensor_tensor(b["qe"][:, i, :], b["qe"][:, i, :], CK ** -0.5, lq[:, t, :],
                                                    ALU.mult, ALU.mult))
            step.end()

        @block.scalar
        def _(act):
            step = Steps(act, a_s)
            act.wait_ge(d_s.sem, d_s.base + 4)
            for i in range(4):
                end = CK - 1 if i // 2 == 0 else 0
                act.wait_ge(d_s.sem, d_s.base + 4 + 3 * (i + 1))
                step(nc.scalar.activation(b["kdT"][:, i, :], b["kdT"][:, i, :], ACT.Exp))
                step(nc.scalar.activation(b["qr"][:, i, :], b["qr"][:, i, :], ACT.Exp))
                step(nc.scalar.activation(b["kr"][:, i, :], b["kr"][:, i, :], ACT.Exp))
                step(nc.scalar.activation(b["qe"][:, i, :], bc[:, i, T:2 * T], ACT.Exp))
                step(nc.scalar.activation(b["lgl"][:, i, :], chunks(bc[:, i, :])[:, :, end], ACT.Exp))
            step.end()

    turn_tiles(core, [([b["kdT"][:, i, n * P:n * P + P] for n in range(TK)],
                       b["lkd"][:, i, :, :].rearrange("p n t -> p (n t)")) for i in range(4)])

    z_s, m_s = core.counter("gla_cleared"), core.counter("gla_attn_masked")
    with core.block() as block:
        @block.tensor
        def _(pe):
            for i in range(4):
                for n in range(2):
                    for e in range(2):
                        last = nc.tensor.matmul(core.ps[2 * i + e][:, n * P:n * P + P],
                                                b["kr"][64 * e:64 * e + 64, i, n * P:n * P + P],
                                                b["qr"][64 * e:64 * e + 64, i, n * P:n * P + P], start=True, stop=True)
                last.then_inc(p_s.sem, 1)

        @block.vector
        def _(dve):
            nc.vector.memset(b["latt"][:, :, :, :], 0.0).then_inc(z_s.sem, 1)
            dve.wait_ge(z_s.sem, z_s.base + 1)
            for i in range(4):
                dve.wait_ge(p_s.sem, p_s.base + i + 1)
                for m in range(4):
                    last = nc.vector.copy_predicated(b["latt"][:, i, m, :], b["gla_mask"][:, i // 2, :].bitcast(U32),
                                                     core.ps[2 * i + m % 2][:, (m // 2) * P:(m // 2) * P + P])
                last.then_inc(m_s.sem, 1)

    p_s.advance(4), z_s.advance(1), m_s.advance(4)


def gla_scan(core, b):
    nc = core.nc
    s, lv = b["ls"], b["lv"]
    kv_s = core.counter("gla_kv_ready")
    st_s = core.counter("gla_state_ready")
    z_s, done = core.counter("gla_state_cleared"), core.counter("gla_out_ready")
    order = [[0, 1, 2, 3, 4, 5, 6, 7], [3, 2, 1, 0, 7, 6, 5, 4]]
    opened = set()

    def place(h, at, size):
        return core.ps[4 + h % 2][:, (h // 2) * T + at:(h // 2) * T + at + size]

    with core.block() as block:
        @block.tensor
        def _(pe):
            for i in range(4):
                for n in range(2):
                    for e in range(2):
                        h = 2 * (i % 2) + e
                        bank = 4 + h % 2
                        nc.tensor.matmul(place(h, n * P, P), lv[:, 2 + n, h * P:h * P + P],
                                         b["latt"][:, i, 2 * n + e, :], start=bank not in opened, stop=False,
                                         skip_group_check=True)
                        opened.add(bank)
            pe.wait_ge(z_s.sem, z_s.base + 1)
            for i in range(8):
                for d in range(2):
                    n, half = chunk_tile(order[d][i])
                    lo = CK * half
                    if i >= 1:
                        pe.wait_ge(st_s.sem, st_s.base + 2 * (i - 1) + d + 1)
                    for h in range(NG):
                        t, e = h // 2, h % 2
                        if n >= 2:
                            at = (n - 2) * P + lo
                            nc.tensor.matmul(place(h, at, CK), s[64 * e:64 * e + 64, 2 * d + t, :],
                                             b["qe"][64 * e:64 * e + 64, 2 * d + t, at:at + CK], start=False,
                                             stop=(i >= 6), skip_group_check=True)
                        last = nc.tensor.matmul(core.ps[d][64 * e:64 * e + 64, t * P:t * P + P],
                                                b["lkd"][lo:lo + CK, 2 * d + t, n, 64 * e:64 * e + 64],
                                                lv[lo:lo + CK, n, h * P:h * P + P], start=True, stop=True)
                    last.then_inc(kv_s.sem, 1)

        @block.vector
        def _(dve):
            nc.vector.memset(s[:, :, :], 0.0).then_inc(z_s.sem, 1)
            dve.wait_ge(z_s.sem, z_s.base + 1)
            for i in range(8):
                for d in range(2):
                    c = order[d][i]
                    dve.wait_ge(kv_s.sem, kv_s.base + 2 * i + d + 1)
                    for t in range(2):
                        last = nc.vector.scalar_tensor_tensor(s[:, 2 * d + t, :], s[:, 2 * d + t, :],
                                                              b["lgl"][:, 2 * d + t, c:c + 1],
                                                              core.ps[d][:, t * P:t * P + P], ALU.mult, ALU.add)
                    last.then_inc(st_s.sem, 1)

    kv_s.advance(16), st_s.advance(16), z_s.advance(1)


def ab_merge(core, src, z, gain, sq):
    nc = core.nc
    squared, summed = core.counter("merge_squared"), core.counter("merge_sums")
    act_done, steps = core.counter("merge_act_done"), core.counter("merge_dve_steps")
    with core.block() as block:
        @block.scalar
        def _(act):
            for h in range(NG):
                nc.scalar.activation(sq[:, h, :], src(h), ACT.Square).then_inc(squared.sem, 1)
            for h in range(NG):
                nc.scalar.activation(z[:, h, :], z[:, h, :], ACT.Silu).then_inc(act_done.sem, 1)
            for h in range(NG):
                act.wait_ge(summed.sem, summed.base + h // 2 + 1)
                nc.scalar.activation(sq[:, h, :], core.ps[h // 2][:, (h % 2) * T:(h % 2) * T + T], ACT.Sqrt,
                                     scale=1.0 / P, bias=core.rms_eps).then_inc(act_done.sem, 1)

        @block.tensor
        def _(pe):
            for h in range(NG):
                pe.wait_ge(squared.sem, squared.base + h + 1)
                last = nc.tensor.matmul(core.ps[h // 2][:, (h % 2) * T:(h % 2) * T + T], core.ones[:, :], sq[:, h, :],
                                        start=True, stop=True)
                if h % 2:
                    last.then_inc(summed.sem, 1)

        @block.vector
        def _(dve):
            step = Steps(dve, steps)
            for h in range(NG):
                dve.wait_ge(act_done.sem, act_done.base + NG + h + 1)
                step(nc.vector.reciprocal(sq[:, h, :], sq[:, h, :]))
                step(nc.vector.tensor_tensor(sq[:, h, :], src(h), sq[:, h, :], ALU.mult))
                step(nc.vector.scalar_tensor_tensor(z[:, h, :], sq[:, h, :], gain[:, 0:1], z[:, h, :],
                                                    ALU.mult, ALU.mult))
            step.end()

    squared.advance(NG), summed.advance(NG // 2), act_done.advance(2 * NG)


def hyena_project(core, h, b):
    nc, used = core.nc, core.used
    raw, u = b["raw"], b["u"]
    copied, padded, steps = core.counter("hy_copied"), core.counter("hy_padded"), core.counter("hy_conv_steps")
    with core.block() as block:
        @block.sync
        def _(sp):
            core.load_ahead(sp)

        @block.tensor
        def _(pe):
            for c in range(12):
                w = core.chunk(pe, c)
                if c >= 8:
                    pe.wait_ge(copied.sem, copied.base + c - 7)
                linear_tiles(core, pe, w, h, [core.ps[c % 8][:, 0:T], core.ps[c % 8][:, T:2 * T]])\
                    .then_inc(used.sem, 1)

        @block.scalar
        def _(act):
            act.wait_ge(padded.sem, padded.base + 1)
            for c in range(12):
                act.wait_ge(used.sem, used.base + c + 1)
                nc.scalar.copy(raw[:, 2 * c:2 * c + 2, 1:T + 1], core.ps[c % 8][:, :].rearrange("p (a t) -> p a t", a=2))\
                    .then_inc(copied.sem, 1)

        @block.vector
        def _(dve):
            nc.vector.memset(raw[:, :, 0:1], 0.0)
            nc.vector.memset(raw[:, :, T + 1:T + 2], 0.0).then_inc(padded.sem, 1)
            dve.wait_ge(padded.sem, padded.base + 1)
            step = Steps(dve, steps)
            w = core.col("hy_conv")
            for i in range(24):
                dve.wait_ge(copied.sem, copied.base + i // 2 + 1)
                y = u[:, i, :]
                step(nc.vector.tensor_scalar(y, raw[:, i, 0:T], w[:, i:i + 1], None, ALU.mult))
                step(nc.vector.scalar_tensor_tensor(y, raw[:, i, 1:T + 1], w[:, 24 + i:25 + i], y, ALU.mult, ALU.add))
                step(nc.vector.scalar_tensor_tensor(y, raw[:, i, 2:T + 2], w[:, 48 + i:49 + i], y, ALU.mult, ALU.add))
            step.end()

    core.stage_done()
    copied.advance(12), padded.advance(1)


def hyena_hidden(core, b):
    nc = core.nc
    MAGIC, C1 = 1.5 * 2 ** 23, 6.28125
    C2 = 2 * math.pi - C1
    p_s, d_s, a_s = core.counter("hy_mlp_ready"), core.counter("hy_mlp_dve_steps"), core.counter("hy_mlp_sine_done")
    hid, t1, t2 = b["hidden"], b["t1"], b["t2"]
    Z = b["hy_z"]
    PISAFE = 3.1415925
    with core.block() as block:
        @block.tensor
        def _(pe):
            for i in range(3):
                lhs, rhs = ((b["hy_w1"], Z), (b["hy_w2"], hid), (b["hy_w3"], hid))[i]
                if i:
                    pe.wait_ge(a_s.sem, a_s.base + i)
                nc.tensor.matmul(core.ps[0][0:64, 0:T], lhs[:, :], rhs[:, :], start=True, stop=True).then_inc(p_s.sem, 1)

        @block.vector
        def _(dve):
            step = Steps(dve, d_s)
            par = core.col("hy_mlp")
            for i in range(3):
                dve.wait_ge(p_s.sem, p_s.base + i + 1)
                step(nc.vector.tensor_scalar(t1[:, :], core.ps[0][0:64, 0:T], par[0:64, i:i + 1], par[0:64, 3:4],
                                             ALU.add, ALU.mult))
                step(nc.vector.tensor_scalar(t2[:, :], t1[:, :], 1 / (2 * math.pi), MAGIC, ALU.mult, ALU.add))
                step(nc.vector.tensor_scalar(t2[:, :], t2[:, :], -MAGIC, None, ALU.add))
                step(nc.vector.scalar_tensor_tensor(t1[:, :], t2[:, :], -C1, t1[:, :], ALU.mult, ALU.add))
                step(nc.vector.scalar_tensor_tensor(t1[:, :], t2[:, :], -C2, t1[:, :], ALU.mult, ALU.add))
                step(nc.vector.tensor_scalar(t1[:, :], t1[:, :], PISAFE, -PISAFE, ALU.min, ALU.max))
            step.end()

        @block.scalar
        def _(act):
            for i in range(3):
                act.wait_ge(d_s.sem, d_s.base + 6 * (i + 1))
                nc.scalar.activation(hid[:, :], t1[:, :], ACT.Sin).then_inc(a_s.sem, 1)

    p_s.advance(3), a_s.advance(3)


def hyena_conv(core, b, n, z, gate, skip):
    nc = core.nc
    fwd, inv = b["hy_fwd"], b["hy_inv"]
    kp, km, ks = b["kp"], b["km"], b["kspec"]
    f_s, w_s, d_s = core.counter("hy_filter_ready"), core.counter("hy_windowed"), core.counter("hy_filter_steps")
    with core.block() as block:
        jobs = [(t, half) for t in range(TT) for half in range(2)]

        @block.tensor
        def _(pe):
            for m, (t, half) in enumerate(jobs):
                for dr in range(2):
                    at = (dr * 2 + n) * D + half * 512
                    last = nc.tensor.matmul(core.ps[2 * m + dr][:, :], b["hidden"][:, t * P:t * P + P],
                                            b["hy_filt"][:, at:at + 512], start=True, stop=True)
                last.then_inc(f_s.sem, 1)

        @block.vector
        def _(dve):
            step = Steps(dve, d_s)
            for m, (t, half) in enumerate(jobs):
                dve.wait_ge(f_s.sem, f_s.base + m + 1)
                sl = slice(half * 512, half * 512 + 512)
                step(nc.vector.tensor_tensor(kp[:, t, sl], core.ps[2 * m][:, :], b["hy_win"][:, t, sl], ALU.mult))
                step(nc.vector.tensor_tensor(b["bw"][:, :], core.ps[2 * m + 1][:, :], b["hy_win"][:, t, sl], ALU.mult))
                if t == 0:
                    step(nc.vector.memset(b["bw"][0:1, :], 0.0))
                step(nc.vector.tensor_tensor(km[:, t, sl], b["bw"][:, :], kp[:, t, sl], ALU.subtract))
                step(nc.vector.tensor_tensor(kp[:, t, sl], kp[:, t, sl], b["bw"][:, :], ALU.add))
            step.end()

    f_s.advance(4)

    turn_tiles(core, [([z[:, 4 * q + c, t * P:t * P + P] for c in range(4)], b["zt"][:, t, q * 512:q * 512 + 512])
                      for t in range(TT) for q in range(2)])

    kr_s, kc_s = core.counter("hy_kspec_ready"), core.counter("hy_kspec_copied")
    zr_s, pd_s, y_s, yg_s = (core.counter(x) for x in ("hy_zspec_ready", "hy_product_done", "hy_y_ready", "hy_gated"))
    st_s = core.counter("hy_product_steps")
    with core.block() as block:
        @block.tensor
        def _(pe):
            m = 0
            for half in range(2):
                sl = slice(half * 512, half * 512 + 512)
                for f in range(2):
                    for ri, src in enumerate((kp, km)):
                        if m >= 4:
                            pe.wait_ge(kc_s.sem, kc_s.base + m - 3)
                        for t in range(TT):
                            last = nc.tensor.matmul(core.ps[m % 4][:, :], fwd[:, t, ri, f * P:f * P + P], src[:, t, sl],
                                                    start=(t == 0), stop=(t == TT - 1))
                        last.then_inc(kr_s.sem, 1)
                        m += 1
            m = 0
            for half in range(2):
                sl = slice(half * 512, half * 512 + 512)
                for f in range(2):
                    if m >= 2:
                        pe.wait_ge(pd_s.sem, pd_s.base + m - 1)
                    for ri in range(2):
                        for t in range(TT):
                            last = nc.tensor.matmul(core.ps[4 + 2 * (m % 2) + ri][:, :], fwd[:, t, ri, f * P:f * P + P],
                                                    b["zt"][:, t, sl], start=(t == 0), stop=(t == TT - 1))
                    last.then_inc(zr_s.sem, 1)
                    m += 1
            pe.wait_ge(kc_s.sem, kc_s.base + 8)
            pe.wait_ge(pd_s.sem, pd_s.base + 4)
            for j in range(DT):
                i = 0
                for f in range(2):
                    for ri in range(2):
                        last = nc.tensor.matmul(core.acc(j), b["prod"][:, f, ri, j * P:j * P + P], inv[:, f, ri, :],
                                                start=(i == 0), stop=(i == 3))
                        i += 1
                if j % 2:
                    last.then_inc(y_s.sem, 1)

        @block.scalar
        def _(act):
            m = 0
            for half in range(2):
                sl = slice(half * 512, half * 512 + 512)
                for f in range(2):
                    for ri in range(2):
                        act.wait_ge(kr_s.sem, kr_s.base + m + 1)
                        nc.scalar.copy(ks[:, f, ri, sl], core.ps[m % 4][:, :]).then_inc(kc_s.sem, 1)
                        m += 1

        @block.vector
        def _(dve):
            step = Steps(dve, st_s)
            m = 0
            for half in range(2):
                sl = slice(half * 512, half * 512 + 512)
                for f in range(2):
                    dve.wait_ge(zr_s.sem, zr_s.base + m + 1)
                    dve.wait_ge(kc_s.sem, kc_s.base + 2 * (m + 1))
                    zc, zs = core.ps[4 + 2 * (m % 2)][:, :], core.ps[5 + 2 * (m % 2)][:, :]
                    kr, ki = ks[:, f, 0, sl], ks[:, f, 1, sl]
                    pr, pi = b["prod"][:, f, 0, sl], b["prod"][:, f, 1, sl]
                    step(nc.vector.tensor_tensor(pr, zc, kr, ALU.mult))
                    step(nc.vector.tensor_tensor(b["bw"][:, :], zs, ki, ALU.mult))
                    step(nc.vector.tensor_tensor(pr, pr, b["bw"][:, :], ALU.add))
                    step(nc.vector.tensor_tensor(pi, zc, ki, ALU.mult))
                    step(nc.vector.tensor_tensor(b["bw"][:, :], zs, kr, ALU.mult))
                    nc.vector.tensor_tensor(pi, pi, b["bw"][:, :], ALU.subtract).then_inc(pd_s.sem, 1)
                    dve.wait_ge(pd_s.sem, pd_s.base + m + 1)
                    m += 1
            for j in range(DT):
                dve.wait_ge(y_s.sem, y_s.base + j // 2 + 1)
                step(nc.vector.scalar_tensor_tensor(z[:, j, :], z[:, j, :], skip[:, j:j + 1], core.acc(j),
                                                    ALU.mult, ALU.add))
                nc.vector.tensor_tensor(z[:, j, :], z[:, j, :], gate[:, j, :], ALU.mult).then_inc(yg_s.sem, 1)
            step.end()

    kr_s.advance(8), kc_s.advance(8), zr_s.advance(4), pd_s.advance(4), y_s.advance(DT // 2), yg_s.advance(DT)


COLS = [("c", DT), ("c_ctx", DT), ("c_2", DT), ("c_ctx_2", DT), ("mod_b0", 72), ("mod_b1", 72), ("mod_b2", 48),
        ("mod_b3", 48), ("ln_g", 48), ("ln_b", 48), ("norm1", 16), ("norm2", 16), ("final", 8), ("bq", 8), ("bk", 2),
        ("ab_conv", 36), ("gdn_norm_w", 1), ("gla_norm_w", 1), ("gla_gate_b", 4), ("hy_conv", 72), ("hy_skip", 16),
        ("hy_mlp", 4)]
COL_AT, NCOL = {}, 0
for _n, _w in COLS:
    COL_AT[_n] = (NCOL, _w)
    NCOL += _w


def load(core, pairs, first=False):
    done = core.counter("inputs_loaded")
    with core.block() as block:
        @block.sync
        def _(sp):
            for dst, src in pairs:
                sp.dma_start(dst, src).then_inc(done.sem, 16)
            if first:
                core.load_first(sp, 0, 0)
            sp.wait_ge(done.sem, done.base + 16 * len(pairs))
    done.advance(16 * len(pairs))


SIDE = {0: (2, [(0, c) for c in range(20, 36)] + [(1, c) for c in range(6)]),
        1: (2, [(1, c) for c in range(6, 28)]),
        2: (2, [(2, c) for c in range(4, 24)] + [(3, c) for c in range(2)]),
        3: (2, [(3, c) for c in range(2, 24)])}
FFN_PLAIN, FFN_SIDE = (33, 6), (55, 5)
PLAN = [(20, 6), FFN_SIDE, FFN_SIDE, (6, 6), (8, 6), (4, 6), FFN_SIDE, FFN_SIDE, (8, 6), (4, 6), FFN_PLAIN,
        (14, 6), (4, 6), FFN_PLAIN, (12, 6), (4, 6), FFN_PLAIN]


def program(nc, a, out):
    with ExitStack() as ctx:
        core = Core(nc, ctx, a["weights"], PLAN)
        x = core.sb("x", [P, DT, T])
        cols = core.sb("cols", [P, NCOL])
        core.col = lambda name: cols[:, COL_AT[name][0]:COL_AT[name][0] + COL_AT[name][1]]
        mods = [core.sb(f"mod_{i}", [P, 72 if i < 2 else 48, 2]) for i in range(4)]
        der = core.sb("derived", [P, 160])
        consts = core.sb("consts", [P, 3, P])
        core.ident, core.ones_mean, core.ones = (consts[:, i, :] for i in range(3))
        selector = core.sb("selector", [P, 5 + 63])
        core.unit_row = lambda r: selector[:, 5 + 31 - r:5 + 63 - r]
        core.selector = selector[:, 0:2]
        core.ln_eps, core.rms_eps, core.q_eps = (selector[:, i:i + 1] for i in (2, 3, 4))
        core.one = consts[:, 2, 0:1]
        cpads = core.sb("silu_c", [P, 2, DT, 32])
        top = [0]
        space = {}

        @contextmanager
        def phase(name, size, splits):
            with ExitStack() as scope:
                get = lambda n, shape, dt: scope.enter_context(nc.sbuf_tensor(f"{name}_{n}", shape, dt))
                space["arena"], space["size"] = get("arena", [P, size], F32), size
                if splits:
                    space["splits"] = dict(wsplit=get("weights_split", [P, 3, 2, CH], F32R),
                                           hs=get("h_split", [P, 2, DT, T], F32R),
                                           hids=get("hidden_split", [P, 2, 2, 2, T], F32R))
                top[0] = 0
                yield

        def carve(*shape, parts=P):
            n = int(np.prod(shape))
            v = space["arena"][0:parts, top[0]:top[0] + n]
            top[0] += n
            assert top[0] <= space["size"], top[0]
            if len(shape) == 2:
                v = v.rearrange("p (a b) -> p a b", a=shape[0])
            elif len(shape) == 3:
                v = v.rearrange("p (a b c) -> p a b c", a=shape[0], b=shape[1])
            elif len(shape) == 4:
                v = v.rearrange("p (a b c d) -> p a b c d", a=shape[0], b=shape[1], c=shape[2])
            return v

        def emit(v):
            done = core.counter("output_stored")
            with core.block() as block:
                @block.sync
                def _(sp):
                    sp.dma_start(out, v[:, :, :]).then_inc(done.sem, 16)
                    sp.wait_ge(done.sem, 16)

        ready = core.counter("cpad_ready")
        dsteps = core.counter("derived_steps")

        def prepare():
            with core.block() as block:
                @block.vector
                def _(dve):
                    nc.vector.memset(cpads[:, :, :, :], 0.0).then_inc(ready.sem, 1)

                @block.scalar
                def _(act):
                    act.wait_ge(ready.sem, ready.base + 1)
                    for i, name in enumerate(("c", "c_ctx", "c_2", "c_ctx_2")):
                        nc.scalar.activation(cpads[:, i // 2, :, i % 2], core.col(name), ACT.Silu).then_inc(ready.sem, 1)
            ready.advance(5)

        def vec(i, j, s=0):
            return mods[i][:, j * DT:(j + 1) * DT, s]

        def derive(ops):
            with core.block() as block:
                @block.vector
                def _(dve):
                    step = Steps(dve, dsteps)
                    for o, i, op, other in ops:
                        if isinstance(other, float):
                            step(nc.vector.tensor_scalar(o, i, other, None, op))
                        else:
                            step(nc.vector.tensor_tensor(o, i, other, op))
                    step.end()

        D8 = lambda k: der[:, k * DT:(k + 1) * DT]

        def modulate(src, dst, scale, shift):
            m = core.counter("modulated")
            with core.block() as block:
                @block.vector
                def _(dve):
                    for j in range(DT):
                        nc.vector.tensor_scalar(dst[:, j, :], src[:, j, :], scale[:, j:j + 1], shift[:, j:j + 1],
                                                ALU.mult, ALU.add).then_inc(m.sem, 1)
            m.advance(DT)

        ln = lambda i, j: (core.col("ln_g")[:, (3 * i + j) * DT:(3 * i + j + 1) * DT],
                           core.col("ln_b")[:, (3 * i + j) * DT:(3 * i + j + 1) * DT])

        def modulation_of(i, first, n, base):
            top[0] = base
            partial = carve(2, 2 * P)
            modulation(core, cpads[:, i // 2, :, :], core.col(f"mod_b{i}"), mods[i], first, n, partial)

        def feed_forward(h, base, stage=None):
            top[0] = base
            f = dict(space["splits"], sg=carve(2, 2, T), tmp=carve(2, T), side=None)
            m, jobs = SIDE.get(stage, (0, []))
            if m:
                f["silu"] = cpads[:, jobs[0][0] // 2, :, 0]
                start = top[0]
                f["side"] = carve(PAIRS * m, 2 * P)
                top[0] = start
            ffn(core, h, f, m)
            if m:
                side_columns(core, f["side"], [(mods[i], core.col(f"mod_b{i}"), 2 * c) for i, c in jobs], f["sg"][:, 0, 0, :])
            return carve(DT, T), carve(DT, T), carve(T)

        def first_block():
            def scales(i, s, which):
                ops = {0: (D8(0), vec(i, 1, s), ALU.add, 1.0), 1: (D8(1), vec(i, 4, s), ALU.add, 1.0),
                       3: (D8(3), vec(i, 2, s), ALU.mult, 0.5 / ALPHA), 4: (D8(4), vec(i, 5, s), ALU.mult, 1.0 / ALPHA)}
                if 2 in which:
                    ops |= {2: (D8(2), vec(i, 7, s), ALU.add, 1.0), 5: (D8(5), vec(i, 8, s), ALU.mult, 0.5 / ALPHA)}
                return [ops[w] for w in which]

            h, hc = carve(DT, T), carve(DT, T)
            base = top[0]
            cx = space["arena"][:, space["size"] - DT * T:].rearrange("p (j t) -> p j t", j=DT)
            load(core, [(cols[:, :], a["cols"]), (selector[:, :], a["selector"]), (consts[:, :, :], a["consts"]),
                        (cx, a["ctx"]), (x[:, :, :], a["x"])], first=True)
            prepare()
            modulation_of(0, 0, 20, base)
            derive(scales(0, 1, (0, 1, 3)))
            modulate(cx, h, D8(0), vec(0, 0, 1))
            diff, sq, rstd = feed_forward(h, base, 0)
            layer_norm(core, cx, D8(3), *ln(0, 0), (D8(1), vec(0, 3, 1)), hc, diff, sq, rstd)
            derive(scales(0, 0, range(6)))
            modulate(x, h, D8(0), vec(0, 0))
            diff, sq, rstd = feed_forward(h, base, 1)
            layer_norm(core, x, D8(3), *ln(0, 0), (D8(1), vec(0, 3)), h, diff, sq, rstd)
            top[0] = base
            at = dict(q=carve(DT, T), k=carve(2, 2, T), v=carve(2, TT, T), sm=carve(4, 2 * T),
                      pt=carve(2, 2 * T), stat=carve(4, 8), mask=carve(TT, P), cos=carve(T), sin=carve(T),
                      swap=carve(P), bv=carve(T), sink=carve(NH))
            o = carve(DT, T)
            load(core, [(at["mask"], a["mask"]), (at["cos"], a["rope"][:, 0, :]), (at["sin"], a["rope"][:, 1, :]),
                        (at["swap"], a["swap"]), (at["bv"], a["bv"]), (at["sink"], a["sink"])])
            attention(core, h, hc, o, at)
            modulation_of(2, 0, 8, base)
            linear(core, o)
            top[0] = base
            layer_norm(core, x, D8(4), *ln(0, 1), (D8(2), vec(0, 6)), h, carve(DT, T), carve(DT, T), carve(T))
            diff, sq, rstd = feed_forward(h, base, 2)
            derive([(D8(6), vec(1, 1), ALU.add, 1.0)])
            layer_norm(core, x, D8(5), *ln(0, 2), (D8(6), vec(1, 0)), h, diff, sq, rstd)
            derive(scales(1, 0, (1, 3, 4)))
            diff, sq, rstd = feed_forward(h, base, 3)
            layer_norm(core, x, D8(3), *ln(1, 0), (D8(1), vec(1, 3)), h, diff, sq, rstd)
            top[0] = base
            cs, uv, fo = carve(2, 3, T), carve(2, TT, 2, T), carve(DT, T)
            load(core, [(cs, a["dft"])])
            fourier(core, h, fo, cs, uv)
            modulation_of(1, 28, 8, base)
            derive(scales(1, 0, (2, 5)))
            linear(core, fo)
            top[0] = base
            layer_norm(core, x, D8(4), *ln(1, 1), (D8(2), vec(1, 6)), h, carve(DT, T), carve(DT, T), carve(T))
            diff, sq, rstd = feed_forward(h, base)
            layer_norm(core, x, D8(5), *ln(1, 2), None, h, diff, sq, rstd)

        with phase("first", 15284, True):
            first_block()

        def gains(i, s):
            ops = []
            for m, scale, norm in ((0, 1, "norm1"), (1, 4, "norm2"))[:2 - s]:
                n = core.col(norm)[:, (i - 2) * DT:(i - 1) * DT]
                ops += [(D8(m), vec(i, scale, s), ALU.add, 1.0), (D8(m), D8(m), ALU.mult, n)]
            return ops

        def recurrent_mixer():
            h = carve(DT, T)
            hc = carve(DT, T)
            base = top[0]
            cx = carve(DT, T)
            load(core, [(cx, a["ctx_2"])])
            derive(gains(2, 1))
            sq, rstd = carve(DT, T), carve(T)
            rms_norm(core, cx, None, D8(0), vec(2, 0, 1), hc, sq, rstd)
            derive(gains(2, 0))
            rms_norm(core, x, None, D8(0), vec(2, 0), h, sq, rstd)

            top[0] = base
            y = carve(DT, T)
            b = dict(qkv=carve(20, T), gz=y[:, 0:NG, :], lg=y[:, NG:2 * NG, :], g=carve(TK, 8), beta=carve(TK, 8), gc=carve(2, TK, 8),
                     tri=carve(3, P), levels=carve(2, 7, CK), masks=carve(2, 2, CK), gla_mask=carve(2, P))
            mid = top[0]
            b |= dict(lq=carve(2, T), lk=carve(2, 2 * T), lv=carve(TK, 512), la=carve(4, 2 * T), carry=carve(2 * T))
            late = top[0]
            b |= dict(raw=carve(20, T + 2))
            load(core, [(b["tri"], a["tri"]), (b["levels"], a["levels"]), (b["masks"], a["masks"]),
                        (b["gla_mask"], a["gla_mask"]), (b["carry"], a["carry"])])
            ab_project(core, h, hc, b)
            top[0] = late
            b |= dict(t1=carve(TK, 8), t2=carve(TK, 8), lt=carve(4, 2 * T), ea=carve(8), a_log=carve(8), dt_bias=carve(8),
                      w_small=carve(DT, 48), llr=carve(2 * T, parts=32), w_gate=carve(2, T, parts=32), g_steps=6, la_steps=18)
            cleared = core.counter("gate_weights_cleared")
            with core.block() as block:
                @block.vector
                def _(dve):
                    nc.vector.memset(b["w_gate"], 0.0).then_inc(cleared.sem, 1)
            cleared.advance(1)
            load(core, [(b["a_log"], a["a_log"]), (b["dt_bias"], a["dt_bias"]), (b["w_small"], a["w_small"]),
                        (b["w_gate"][0:16, 0, :], a["w_gate"][0]), (b["w_gate"][16:32, 1, :], a["w_gate"][1])])
            ab_gates(core, h, hc, b)
            top[0] = 0
            b |= dict(lkd=carve(4, TK, P), lgl=carve(4, 8), ls=carve(4, P))
            assert top[0] <= base
            top[0] = late
            b |= dict(bc=carve(4, 2 * T), kdT=carve(4, 2 * T), qr=carve(4, T), kr=carve(4, T), qe=carve(4, T),
                      latt=carve(4, 4, P))
            gla_prepare(core, b)
            gla_scan(core, b)
            msq = b["qr"]
            ab_merge(core, lambda h: core.ps[4 + h % 2][:, (h // 2) * T:(h // 2) * T + T], b["lg"], core.col("gla_norm_w"), msq)
            top[0] = mid
            b |= dict(sq12=carve(12, T))
            l2_norm(core, b)
            top[0] = 0
            b |= dict(rows=carve(8, P), dd=carve(2, NG, CK), l=carve(2, 8, CK))
            b |= dict(s=carve(8, P), bg=carve(TK, 8), ed=carve(TK, 8), ngc=carve(TK, 8), gl=carve(8, 8))
            assert top[0] <= base
            top[0] = mid
            b |= dict(ktm=carve(TK, NG, P), vtm=carve(TK, NG, P), qd=carve(8, T),
                      u0=carve(TK, 8, P), kcdT=carve(TK, 8, P), x=carve(4, NG * P), w=carve(4, NG * P),
                      o=carve(4, NG * P), pm=carve(4, NG * P))
            b["u"], b["ue"] = b["x"][:, 0:2, :], b["w"][:, 0:2, :]
            qkv = b["qkv"]
            b["att"] = [qkv[:, i:i + 2, :].rearrange("p a (b t) -> p (a b) t", t=CK) for i in (4, 16)]
            place = lambda i, n: qkv[:, (0 if n < TT else 12) + i, (n % TT) * P:(n % TT) * P + P]
            turn_tiles(core, [([place(h_ + 4 * m, n) for h_ in range(NG)],
                               b["vtm" if m else "ktm"][:, n, :, :].rearrange("p h t -> p (h t)"))
                              for n in range(TK) for m in range(2)])
            gdn_factors(core, b)
            for n in range(0, TK, 2):
                gdn_tile(core, b, n)
                gdn_tile(core, b, n + 1)
                gdn_solve(core, b, (n, n + 1))
            gdn_scan(core, b)
            top[0] = mid
            msq = carve(NG, T)
            ab_merge(core, lambda h: core.ps[6 + h // 2][:, (h % 2) * T:(h % 2) * T + T], b["gz"], core.col("gdn_norm_w"), msq)
            linear(core, y)

        def hyena_mixer():
            h = carve(DT, T)
            rms_norm(core, x, vec(2, 5), D8(0), vec(3, 0), h, carve(DT, T), carve(T))
            top[0] = DT * T
            b = dict(u=carve(24, T))
            mid = top[0]
            b |= dict(raw=carve(24, T + 2))
            hyena_project(core, h, b)
            top[0] = 0
            b |= dict(zt=carve(TT, D))
            top[0] = mid
            b |= dict(hy_filt=carve(2 * 2 * D, parts=64), hidden=carve(T, parts=64), t1=carve(T, parts=64), t2=carve(T, parts=64),
                      hy_z=carve(T, parts=33), hy_w1=carve(64, parts=33), hy_w2=carve(64, parts=64), hy_w3=carve(64, parts=64),
                      hy_fwd=carve(TT, 2, T), hy_inv=carve(2, 2, T), hy_win=carve(TT, D), kp=carve(TT, D), km=carve(TT, D),
                      kspec=carve(2, 2, D), prod=carve(2, 2, D), bw=carve(512))
            load(core, [(b[n], a[n]) for n in ("hy_filt", "hy_z", "hy_w1", "hy_w2", "hy_w3", "hy_fwd", "hy_inv", "hy_win")])
            hyena_hidden(core, b)
            z = b["u"][:, 0:DT, :]
            for n in range(2):
                hyena_conv(core, b, n, z, b["u"][:, (n + 1) * DT:(n + 2) * DT, :],
                           core.col("hy_skip")[:, n * DT:(n + 1) * DT])
            linear(core, z)

        def ffn_half(h, i):
            top[0] = DT * T
            rms_norm(core, x, vec(i, 2), D8(1), vec(i, 3), h, carve(DT, T), carve(T))
            return feed_forward(h, DT * T)

        with phase("recurrent", 35712, False):
            recurrent_mixer()
        with phase("ffn_2", 9000, True):
            ffn_half(carve(DT, T), 2)
        derive(gains(3, 0))
        with phase("hyena", 35584, False):
            hyena_mixer()
        with phase("ffn_3", 9000, True):
            h = carve(DT, T)
            _, sq, rstd = ffn_half(h, 3)
            rms_norm(core, x, vec(3, 5), core.col("final"), None, h, sq, rstd)
            emit(h)


def _features(v):
    v = np.asarray(v)
    return np.ascontiguousarray(v.reshape(-1, P).T)


def _tiles(m):
    return np.ascontiguousarray(m.reshape(-1, P, m.shape[1]).transpose(1, 0, 2))


def _chunks(m):
    return m.reshape(DT, P, -1, 256).transpose(2, 1, 0, 3).reshape(-1, P, CH)


def _ffn_chunks(wa, wg, wo):
    ag = np.stack([wa.reshape(DT, P, FFT, P), wg.reshape(DT, P, FFT, P)], 3).transpose(2, 1, 0, 3, 4).reshape(FFT, P, CH)
    down = wo.reshape(PAIRS, 2, P, D).transpose(0, 2, 1, 3).reshape(PAIRS, P, CH)
    order = [ag[0], ag[1], ag[2], ag[3], down[0]]
    for p in range(2, PAIRS):
        order += [ag[2 * p], ag[2 * p + 1], down[p - 1]]
    return np.stack(order + [down[PAIRS - 1]])


def layout(i):
    f32 = np.float32
    heads = [8 * (t // 4) + 4 * e + t % 4 for t in range(DT) for e in range(2)]
    perm = np.concatenate([np.arange(h * HD, h * HD + HD) for h in heads])
    wqkv, bqkv = i["attn_wqkv"][0], i["attn_bqkv"][0]
    ab = i["ab_w_in_2"][0]
    sizes = [512, 512, 512, 512, 8, 8, 256, 256, 512, 512, 32]
    at = np.concatenate([[0], np.cumsum(sizes)])
    part = {n: ab[:, at[k]:at[k + 1]] for k, n in
            enumerate(("gq", "gk", "gv", "gz", "ga", "gb", "lq", "lk", "lv", "lg", "llr"))}
    ff = lambda l, j: _ffn_chunks(i["ffn_wi"][l, j][:, :FF], i["ffn_wi"][l, j][:, FF:], i["ffn_wo"][l, j])
    ff2 = lambda l: _ffn_chunks(i["ffn_w3_2"][l], i["ffn_w1_2"][l], i["ffn_w2_2"][l])
    f00 = ff(0, 0)
    mod = [_chunks(m) for m in (*i["mod_w"], *i["mod_w_2"])]

    def with_side(ffn, stage):
        m, jobs = SIDE[stage]
        out, n = [], 0
        for c in range(len(ffn)):
            out.append(ffn[c])
            if c in (4, 32) or (c > 4 and c % 3 == 1):
                out += [mod[q][k] for q, k in jobs[n:n + m]]
                n += m
        assert n == len(jobs)
        return np.stack(out)

    stream = [mod[0][:20], with_side(f00, 0), with_side(f00, 1), _chunks(wqkv[:, :1024][:, perm]),
              _chunks(wqkv[:, 1024:]), mod[2][:8], _chunks(i["attn_wo"][0][perm]), with_side(ff(0, 1), 2),
              with_side(ff(1, 0), 3), mod[1][28:], _chunks(i["fourier_wo"][0]), ff(1, 1)]
    stream += [_chunks(part[n]) for n in ("gk", "gv", "gq", "gz", "lq", "lk", "lv", "lg")]
    stream += [_chunks(i["ab_w_out_2"][0]), ff2(0), _chunks(i["hy_w_in_2"][0]), _chunks(i["hy_w_out_2"][0]), ff2(1)]
    a = {"weights": np.concatenate(stream)}
    assert len(a["weights"]) == sum(n for n, _ in PLAN)

    mlp = np.zeros((P, 4), f32)
    for k, n in enumerate(("hy_pos_b1_2", "hy_pos_b2_2", "hy_pos_b3_2", "hy_freq_2")):
        mlp[:64, k] = i[n][0]
    cols = {"c": i["c"], "c_ctx": i["c_ctx"], "c_2": i["c_2"], "c_ctx_2": i["c_ctx_2"], "mod_b0": i["mod_b"][0],
            "mod_b1": i["mod_b"][1], "mod_b2": i["mod_b_2"][0], "mod_b3": i["mod_b_2"][1], "ln_g": i["ln_g"],
            "ln_b": i["ln_b"], "norm1": i["norm1_w_2"], "norm2": i["norm2_w_2"], "final": i["final_norm_w_2"],
            "bq": bqkv[:1024][perm], "bk": bqkv[1024:1280], "ab_conv": i["ab_conv_w_2"][0],
            "gdn_norm_w": i["gdn_norm_w_2"], "gla_norm_w": i["gla_norm_w_2"], "gla_gate_b": i["gla_gate_b_2"][0],
            "hy_conv": i["hy_conv_w_2"][0], "hy_skip": i["hy_skip_2"][0]}
    a["cols"] = np.concatenate([mlp if n == "hy_mlp" else _features(cols[n]) for n, _ in COLS], 1)
    assert a["cols"].shape == (P, NCOL)
    for n, src in (("x", i["x"][0]), ("ctx", i["ctx"][0]), ("ctx_2", i["ctx_2"][0])):
        a[n] = _tiles(src.T)
    a["consts"] = np.ascontiguousarray(np.stack([np.eye(P), np.full((P, P), 1 / D), np.ones((P, P))], 1).astype(f32))
    sel = np.zeros((P, 5 + 63), f32)
    sel[:, 5 + 31] = 1
    sel[:, 2:5] = LN_EPS / ALPHA ** 2, RMS_EPS, P * RMS_EPS
    for g in range(4):
        sel[32 * g, 0] = sel[32 * g + 1, 1] = 1
    a["selector"] = sel

    qpos, kpos = np.arange(T)[:, None], np.arange(T)[None, :]
    mask = np.where(np.abs(qpos - kpos) <= 128, 0, NEG).astype(f32)
    a["mask"] = np.ascontiguousarray(np.stack([mask[:P, P:], mask[P:, :P]], 1))
    inv = 10000.0 ** (-np.arange(0, 32, 2) / 32)
    pos = np.arange(T)
    ang = np.concatenate([(pos // 64)[:, None] * inv, (pos % 64)[:, None] * inv], -1)
    rope = np.zeros((P, 2, T), f32)
    swap = np.zeros((P, P), f32)
    for p in range(P):
        d = p % HD
        axis, second, j = d // 32, (d % 32) // 16, d % 16
        rope[p, 0] = np.cos(ang[:, axis * 16 + j])
        rope[p, 1] = np.sin(ang[:, axis * 16 + j])
        swap[p + (-16 if second else 16), p] = 1 if second else -1
    a["rope"], a["swap"] = rope, swap
    a["bv"] = np.ascontiguousarray(np.broadcast_to(bqkv[1280:], (P, 256)))
    a["sink"] = np.ascontiguousarray(np.broadcast_to(i["attn_sink"][0], (P, NH)))

    ph = 2 * np.pi * np.outer(np.arange(256), np.arange(256)) / 256
    a["dft"] = np.ascontiguousarray((np.stack([np.cos(ph), np.sin(ph), -np.sin(ph)], 1) / 16).astype(f32)
                                    .reshape(2, P, 3, 256).transpose(1, 0, 2, 3))

    r, c = np.arange(P)[:, None], np.arange(P)[None, :]
    same = r // CK == c // CK
    a["tri"] = np.ascontiguousarray(np.stack([same & (r <= c), same & (r >= c), same], 1).astype(f32))
    own = np.arange(P)[:, None], r // CK * CK + np.arange(CK)[None, :]
    a["masks"] = np.ascontiguousarray(np.stack([
        np.stack([np.where(same & (c < r), 0, NEG), np.where(same & (r <= c), 0, NEG)], 1),
        np.stack([np.where(same & (c > r), 0, NEG), np.where(same & (r >= c), 0, NEG)], 1)], 1).astype(f32)
        [own[0], :, :, own[1]].transpose(0, 2, 3, 1))
    a["gla_mask"] = np.ascontiguousarray(np.stack([same & (r <= c), same & (r >= c)], 1).astype(f32))
    lv = np.zeros((P, 2, 7, P), f32)
    for l in range(6):
        s = 2 ** l
        block = (r // (2 * s) == c // (2 * s)) & (r // s != c // s)
        lv[:, 0, l], lv[:, 1, l] = block & (c < r), block & (c > r)
    lv[:, :, 6] = np.eye(P)[:, None]
    a["levels"] = np.ascontiguousarray(lv[own[0], :, :, own[1]].transpose(0, 2, 3, 1))
    a["carry"] = np.ascontiguousarray(np.broadcast_to((np.arange(2 * T) % CK != 0).astype(f32), (P, 2 * T)))
    a["a_log"] = np.ascontiguousarray(np.broadcast_to(i["gdn_a_log_2"].reshape(-1), (P, 8)))
    a["dt_bias"] = np.ascontiguousarray(np.broadcast_to(i["gdn_dt_bias_2"].reshape(-1), (P, 8)))
    a["w_small"] = _tiles(np.concatenate([part["ga"], part["gb"], part["llr"]], 1))
    a["w_gate"] = i["gla_gate_w_2"][0]

    t = np.linspace(0, 1, T, dtype=f32)[:, None]
    w = (f32(2 * math.pi / T) * np.arange(T, dtype=f32))[:, None]
    fr = np.linspace(1e-4, 15, 16, dtype=f32)[None, :]
    a["hy_z"] = np.ascontiguousarray(np.concatenate([t, np.cos(fr * w), -np.sin(fr * w)], -1).T.astype(f32))
    deltas = np.abs(np.linspace(math.log(1e-2) / 1.5, math.log(1e-2) / 0.3, D, dtype=f32))
    a["hy_win"] = _tiles((np.exp(-t * deltas) + f32(0.05)).astype(f32))
    th = (2 * np.arange(256) + 1)[None, :] * np.arange(T)[:, None] * (np.pi / 512)
    a["hy_fwd"] = np.ascontiguousarray(np.stack([np.cos(th), np.sin(th)], 1).astype(f32).reshape(2, P, 2, 256)
                                       .transpose(1, 0, 2, 3))
    a["hy_inv"] = np.ascontiguousarray((np.stack([np.cos(th.T), -np.sin(th.T)], 1) / 256).astype(f32)
                                       .reshape(2, P, 2, T).transpose(1, 0, 2, 3))
    a["hy_filt"] = i["hy_filt_out_2"][0]
    for k in range(1, 4):
        a[f"hy_w{k}"] = i[f"hy_pos_w{k}_2"][0]
    return {n: np.ascontiguousarray(v) for n, v in a.items()}


def kernel(**inputs):
    import concourse.bacc as bacc
    from concourse.bass_utils import run_bass_kernel_spmd

    arrays = layout({n: np.asarray(v) for n, v in inputs.items()})
    nc = bacc.Bacc("TRN2", target_bir_lowering=False, num_devices=1)
    views = {n: nc.dram_tensor(f"in_{n}", v.shape, mybir.dt.from_np(v.dtype), kind="ExternalInput").ap()
             for n, v in arrays.items()}
    out = nc.dram_tensor("out", (P, DT, T), F32, kind="ExternalOutput").ap()
    program(nc, views, out)
    r = run_bass_kernel_spmd(nc, [{f"in_{n}": v for n, v in arrays.items()}], core_ids=[0])
    y = r.results[0]["out"]
    return np.ascontiguousarray(y.transpose(2, 1, 0).reshape(1, T, D))
```
